# Optimizing a Trainium2 kernel written in Bass

```python
import jax, jax.numpy as jnp
from jax import lax
import numpy as np
import math

D_MODEL = 1024
BATCH = 1
SEQ = 256
DEPTH = 2

GRID_W = 64
CTX_LEN = 256
N_MIXERS = 2
N_POOL_GROUPS = 4
POOL_WINDOWS = (2, 4, 8, 16)
POOL_GROUP_DIM = D_MODEL // N_POOL_GROUPS
HEAD_DIM = 128
N_Q_HEADS = D_MODEL // HEAD_DIM
N_KV_HEADS = 2
Q_PER_KV = N_Q_HEADS // N_KV_HEADS
QKV_DIM = (N_Q_HEADS + 2 * N_KV_HEADS) * HEAD_DIM
ROPE_THETA = 10000.0
Q_BLOCK = 128
D_FF = 4 * D_MODEL
N_MOD = 6
EPS = 1e-6
N_POOL_LAYERS = (DEPTH + 1) // 2
N_ATTN_LAYERS = DEPTH // 2


def rms_norm(x, g):
    xf = x.astype(jnp.float32)
    y = xf * lax.rsqrt(jnp.mean(xf * xf, axis=-1, keepdims=True) + EPS)
    return (y * g.astype(jnp.float32)).astype(x.dtype)

def ada_mods(cond, w, b):
    m = (jax.nn.silu(cond) @ w + b)[..., None, :]
    return jnp.split(m, N_MOD, axis=-1)

def modulate(h, shift, scale):
    return h * (1.0 + scale) + shift

def pool_mixer(h, w_pool, pool_scale):
    B, L, D = h.shape
    t = jnp.arange(L)
    hf = h.astype(jnp.float32)
    cs = jnp.concatenate([jnp.zeros((B, 1, D), jnp.float32), jnp.cumsum(hf, axis=1)], axis=1)
    outs = []
    for g, w in enumerate(POOL_WINDOWS):
        sl = slice(g * POOL_GROUP_DIM, (g + 1) * POOL_GROUP_DIM)
        lo = jnp.clip(t - w // 2, 0, L)
        hi = jnp.clip(t + w - w // 2, 0, L)
        csg = cs[..., sl]
        cnt = (hi - lo).astype(jnp.float32)[:, None]
        mean = (jnp.take(csg, hi, axis=1) - jnp.take(csg, lo, axis=1)) / cnt
        diff = (mean - hf[..., sl]).astype(h.dtype)
        outs.append(diff @ w_pool[g])
    return jnp.concatenate(outs, axis=-1) * pool_scale

def axial_rope_tables(L):
    rows = L // GRID_W
    row = jnp.broadcast_to(jnp.arange(rows)[:, None], (rows, GRID_W)).reshape(L).astype(jnp.float32)
    col = jnp.broadcast_to(jnp.arange(GRID_W)[None, :], (rows, GRID_W)).reshape(L).astype(jnp.float32)
    half = HEAD_DIM // 2
    inv_freq = jnp.power(jnp.float32(ROPE_THETA), -jnp.arange(0, half, 2, dtype=jnp.float32) / half)
    ang_r = row[:, None] * inv_freq
    ang_c = col[:, None] * inv_freq
    return (jnp.cos(ang_r)[:, None, :], jnp.sin(ang_r)[:, None, :],
            jnp.cos(ang_c)[:, None, :], jnp.sin(ang_c)[:, None, :])

def _rotate(x, cos, sin):
    x1, x2 = jnp.split(x, 2, axis=-1)
    return jnp.concatenate([x1 * cos - x2 * sin, x2 * cos + x1 * sin], axis=-1)

def apply_axial_rope(x, tables):
    cr, sr, cc, sc = tables
    xf = x.astype(jnp.float32)
    half = HEAD_DIM // 2
    out = jnp.concatenate([_rotate(xf[..., :half], cr, sr), _rotate(xf[..., half:], cc, sc)], axis=-1)
    return out.astype(x.dtype)

def qkv_project(h, w_qkv, g_q, g_k):
    B, L, _ = h.shape
    qkv = h @ w_qkv
    q = qkv[..., :N_Q_HEADS * HEAD_DIM].reshape(B, L, N_Q_HEADS, HEAD_DIM)
    k = qkv[..., N_Q_HEADS * HEAD_DIM:(N_Q_HEADS + N_KV_HEADS) * HEAD_DIM].reshape(B, L, N_KV_HEADS, HEAD_DIM)
    v = qkv[..., (N_Q_HEADS + N_KV_HEADS) * HEAD_DIM:].reshape(B, L, N_KV_HEADS, HEAD_DIM)
    return rms_norm(q, g_q), rms_norm(k, g_k), v

def attend(q, k, v):
    s = jnp.einsum('bqhgd,bkhd->bhgqk', q, k).astype(jnp.float32) * (HEAD_DIM ** -0.5)
    p = jax.nn.softmax(s, axis=-1).astype(v.dtype)
    return jnp.einsum('bhgqk,bkhd->bqhgd', p, v)

def attention_mixer(h_lat, h_ctx, w_qkv, g_q, g_k, w_o, need_ctx_out):
    B, L, D = h_lat.shape
    C = h_ctx.shape[1]
    tables = axial_rope_tables(L)
    q_l, k_l, v_l = qkv_project(h_lat, w_qkv, g_q, g_k)
    q_l = apply_axial_rope(q_l, tables)
    k_l = apply_axial_rope(k_l, tables)
    q_c, k_c, v_c = qkv_project(h_ctx, w_qkv, g_q, g_k)
    k_all = jnp.concatenate([k_c, k_l], axis=1)
    v_all = jnp.concatenate([v_c, v_l], axis=1)
    nb = L // Q_BLOCK
    qb = q_l.reshape(B, nb, Q_BLOCK, N_KV_HEADS, Q_PER_KV, HEAD_DIM).transpose(1, 0, 2, 3, 4, 5)
    o_blocks = lax.map(lambda qblk: attend(qblk, k_all, v_all), qb)
    o_lat = o_blocks.transpose(1, 0, 2, 3, 4, 5).reshape(B, L, D) @ w_o
    o_ctx = None
    if need_ctx_out:
        qc = q_c.reshape(B, C, N_KV_HEADS, Q_PER_KV, HEAD_DIM)
        o_ctx = attend(qc, k_c, v_c).reshape(B, C, D) @ w_o
    return o_lat, o_ctx

def sq_relu_mlp(h, w_in, w_out):
    return jnp.square(jax.nn.relu(h @ w_in)) @ w_out

def first_inputs(seed: int = 0) -> dict:
    key = jax.random.key(seed)
    ks = jax.random.split(key, 20)
    f32 = jnp.float32
    nrm = lambda k, shape: jax.random.normal(k, shape, f32)
    gain = lambda k, shape: 1.0 + 0.05 * nrm(k, shape)
    return {
        'x': nrm(ks[0], (BATCH, SEQ, D_MODEL)),
        'c': nrm(ks[1], (BATCH, D_MODEL)),
        'ctx': nrm(ks[2], (BATCH, CTX_LEN, D_MODEL)),
        'c_ctx': nrm(ks[3], (D_MODEL,)),
        'w_ada': nrm(ks[4], (DEPTH, D_MODEL, N_MOD * D_MODEL)) * (0.5 * D_MODEL ** -0.5),
        'b_ada': 0.01 * nrm(ks[5], (DEPTH, N_MOD * D_MODEL)),
        'g_mix_pre': gain(ks[6], (DEPTH, D_MODEL)),
        'g_mix_post': gain(ks[7], (DEPTH, D_MODEL)),
        'g_mlp_pre': gain(ks[8], (DEPTH, D_MODEL)),
        'g_mlp_post': gain(ks[9], (DEPTH, D_MODEL)),
        'w_pool': nrm(ks[10], (N_POOL_LAYERS, N_POOL_GROUPS, POOL_GROUP_DIM, POOL_GROUP_DIM)) * POOL_GROUP_DIM ** -0.5,
        'pool_scale': 1.0 + 0.1 * nrm(ks[11], (N_POOL_LAYERS, D_MODEL)),
        'w_qkv': nrm(ks[12], (N_ATTN_LAYERS, D_MODEL, QKV_DIM)) * D_MODEL ** -0.5,
        'g_q': gain(ks[13], (N_ATTN_LAYERS, HEAD_DIM)),
        'g_k': gain(ks[14], (N_ATTN_LAYERS, HEAD_DIM)),
        'w_o': nrm(ks[15], (N_ATTN_LAYERS, D_MODEL, D_MODEL)) * D_MODEL ** -0.5,
        'w_mlp_in': nrm(ks[16], (DEPTH, D_MODEL, D_FF)) * D_MODEL ** -0.5,
        'w_mlp_out': nrm(ks[17], (DEPTH, D_FF, D_MODEL)) * D_FF ** -0.5,
    }

def first_block(x, c, ctx, c_ctx, w_ada, b_ada, g_mix_pre, g_mix_post, g_mlp_pre, g_mlp_post,
              w_pool, pool_scale, w_qkv, g_q, g_k, w_o, w_mlp_in, w_mlp_out):
    for i in range(DEPTH):
        last = i == DEPTH - 1
        j = i // N_MIXERS
        sh1, sc1, gt1, sh2, sc2, gt2 = ada_mods(c, w_ada[i], b_ada[i])
        csh1, csc1, cgt1, csh2, csc2, cgt2 = ada_mods(c_ctx, w_ada[i], b_ada[i])
        h_lat = modulate(rms_norm(x, g_mix_pre[i]), sh1, sc1)
        h_ctx = modulate(rms_norm(ctx, g_mix_pre[i]), csh1, csc1)
        if i % N_MIXERS == 0:
            y_lat = pool_mixer(h_lat, w_pool[j], pool_scale[j])
            y_ctx = None if last else pool_mixer(h_ctx, w_pool[j], pool_scale[j])
        else:
            y_lat, y_ctx = attention_mixer(h_lat, h_ctx, w_qkv[j], g_q[j], g_k[j], w_o[j], not last)
        x = x + gt1 * rms_norm(y_lat, g_mix_post[i])
        m_lat = sq_relu_mlp(modulate(rms_norm(x, g_mlp_pre[i]), sh2, sc2), w_mlp_in[i], w_mlp_out[i])
        x = x + gt2 * rms_norm(m_lat, g_mlp_post[i])
        if not last:
            ctx = ctx + cgt1 * rms_norm(y_ctx, g_mix_post[i])
            m_ctx = sq_relu_mlp(modulate(rms_norm(ctx, g_mlp_pre[i]), csh2, csc2), w_mlp_in[i], w_mlp_out[i])
            ctx = ctx + cgt2 * rms_norm(m_ctx, g_mlp_post[i])
    return x


DEPTH_2 = 4

N_MIXERS_2 = 3
HEAD_DIM_2 = 64
PLE_DIM = 256
D_FF_2 = 4 * D_MODEL
NORM_EPS = 1e-6
NEG_INF = -1e30

REL_BUCKETS = 32
REL_MAX_DIST = 128
REL_HEADS = D_MODEL // HEAD_DIM_2

DA_HEADS = D_MODEL // (2 * HEAD_DIM_2)
DA_IN = 3 * D_MODEL

NSA_HEADS = D_MODEL // HEAD_DIM_2
NSA_KV_GROUPS = 4
NSA_GROUP_SIZE = NSA_HEADS // NSA_KV_GROUPS
NSA_CMP_LEN = 32
NSA_CMP_STRIDE = 16
NSA_CMP_HIDDEN = 256
NSA_SEL_LEN = 64
NSA_TOP_N = 16
NSA_WINDOW = 512
NSA_Q_CHUNK = 64
NSA_FORCE_SCORE = 1e4
NSA_KV_DIM = NSA_KV_GROUPS * HEAD_DIM_2
NSA_IN = NSA_HEADS * HEAD_DIM_2 + 6 * NSA_KV_DIM + 3 * NSA_HEADS

FOX_HEADS = D_MODEL // HEAD_DIM_2
FOX_IN = 3 * D_MODEL + FOX_HEADS

N_DA = (DEPTH_2 + 2) // 3
N_NSA = (DEPTH_2 + 1) // 3
N_FOX = DEPTH_2 // 3


def rmsnorm(x, g):
    xf = x.astype(jnp.float32)
    y = xf * lax.rsqrt(jnp.mean(xf * xf, axis=-1, keepdims=True) + NORM_EPS)
    return (y * g.astype(jnp.float32)).astype(x.dtype)

def t5_bucket(dist):
    n = jnp.maximum(dist, 0)
    max_exact = REL_BUCKETS // 2
    nf = jnp.maximum(n, 1).astype(jnp.float32)
    large = max_exact + (jnp.log(nf / max_exact) / math.log(REL_MAX_DIST / max_exact)
                         * (REL_BUCKETS - max_exact)).astype(jnp.int32)
    large = jnp.minimum(large, REL_BUCKETS - 1)
    return jnp.where(n < max_exact, n, large)

def masked_softmax(s, mask):
    s = jnp.where(mask, s.astype(jnp.float32), NEG_INF)
    return jnp.where(mask, jax.nn.softmax(s, axis=-1), 0.0)

def query_blocks(a, blk):
    B, S = a.shape[:2]
    return jnp.moveaxis(a.reshape(B, S // blk, blk, *a.shape[2:]), 1, 0)

def merge_blocks(o):
    o = jnp.moveaxis(o, 0, 1)
    return o.reshape(o.shape[0], -1, *o.shape[3:])

def diff_attention(h, w_in, lam, subln_g, w_out, rel_bias, lam_init):
    B, S, _ = h.shape
    q, k, v = jnp.split(h @ w_in, 3, axis=-1)
    q = q.reshape(B, S, DA_HEADS, 2, HEAD_DIM_2)
    k = k.reshape(B, S, DA_HEADS, 2, HEAD_DIM_2)
    v = v.reshape(B, S, DA_HEADS, 2 * HEAD_DIM_2)
    lf = lam.astype(jnp.float32)
    lam_full = jnp.exp(jnp.sum(lf[0] * lf[1])) - jnp.exp(jnp.sum(lf[2] * lf[3])) + lam_init
    scale = HEAD_DIM_2 ** -0.5
    key_pos = jnp.arange(S)

    def block(args):
        qb, q0 = args
        t = q0 + jnp.arange(Q_BLOCK)
        dist = t[:, None] - key_pos[None, :]
        mask = dist >= 0
        bias = rel_bias[t5_bucket(dist)].astype(jnp.float32)
        bias = jnp.moveaxis(bias, -1, 0).reshape(DA_HEADS, 2, Q_BLOCK, S)
        s = jnp.einsum('bqhcd,bkhcd->bhcqk', qb, k).astype(jnp.float32) * scale + bias[None]
        pr = masked_softmax(s, mask)
        a = pr[:, :, 0] - lam_full * pr[:, :, 1]
        return jnp.einsum('bhqk,bkhe->bqhe', a.astype(v.dtype), v)

    starts = jnp.arange(S // Q_BLOCK) * Q_BLOCK
    o = merge_blocks(lax.map(block, (query_blocks(q, Q_BLOCK), starts)))
    o = rmsnorm(o, subln_g) * (1.0 - lam_init)
    return o.reshape(B, S, D_MODEL) @ w_out

def nsa_attention(h, w_in, cmp_pe, cmp_w1, cmp_w2, w_out, rel_bias):
    B, S, _ = h.shape
    G, R, hd, Qc = NSA_KV_GROUPS, NSA_GROUP_SIZE, HEAD_DIM_2, NSA_Q_CHUNK
    proj = h @ w_in
    nq = NSA_HEADS * hd
    q = proj[..., :nq].reshape(B, S, G, R, hd)
    kv = proj[..., nq:nq + 6 * NSA_KV_DIM].reshape(B, S, 6, G, hd)
    k_cmp, v_cmp, k_sel, v_sel, k_win, v_win = [kv[:, :, i] for i in range(6)]
    gates = jax.nn.sigmoid(proj[..., nq + 6 * NSA_KV_DIM:].reshape(B, S, G, R, 3))
    scale = hd ** -0.5

    n_cmp = (S - NSA_CMP_LEN) // NSA_CMP_STRIDE + 1
    tok = jnp.arange(n_cmp)[:, None] * NSA_CMP_STRIDE + jnp.arange(NSA_CMP_LEN)[None, :]

    def compress(a, pe, w1, w2):
        blk = a[:, tok] + pe[None, None, :, None, :]
        blk = jnp.moveaxis(blk, 3, 2).reshape(B, n_cmp, G, NSA_CMP_LEN * hd)
        return jax.nn.gelu(blk @ w1) @ w2

    kc = compress(k_cmp, cmp_pe[0], cmp_w1[0], cmp_w2[0])
    vc = compress(v_cmp, cmp_pe[1], cmp_w1[1], cmp_w2[1])
    cmp_start = jnp.arange(n_cmp) * NSA_CMP_STRIDE
    cmp_end = cmp_start + NSA_CMP_LEN - 1

    n_sel_blk = S // NSA_SEL_LEN
    n_top = min(NSA_TOP_N, n_sel_blk)
    sel_start = jnp.arange(n_sel_blk) * NSA_SEL_LEN
    overlap = ((cmp_start[:, None] < sel_start[None, :] + NSA_SEL_LEN)
               & (cmp_end[:, None] >= sel_start[None, :])).astype(jnp.float32)
    ks_blk = jnp.moveaxis(k_sel.reshape(B, n_sel_blk, NSA_SEL_LEN, G, hd), 3, 1)
    vs_blk = jnp.moveaxis(v_sel.reshape(B, n_sel_blk, NSA_SEL_LEN, G, hd), 3, 1)

    pad = ((0, 0), (NSA_WINDOW, 0), (0, 0), (0, 0))
    kw_pad = jnp.pad(k_win, pad)
    vw_pad = jnp.pad(v_win, pad)

    rel = rel_bias.reshape(REL_BUCKETS, G, R)
    b_idx = jnp.arange(B)[:, None, None, None]
    g_idx = jnp.arange(G)[None, :, None, None]
    j_blk = jnp.arange(n_sel_blk)
    K_sel = n_top * NSA_SEL_LEN

    def chunk(args):
        qc, gc, q0 = args
        t = q0 + jnp.arange(Qc)
        d_c = t[:, None] - cmp_end[None, :]
        m_c = d_c >= 0
        b_c = jnp.moveaxis(rel[t5_bucket(d_c)], (2, 3), (0, 1)).astype(jnp.float32)
        s_c = jnp.einsum('bqgrd,bngd->bgrqn', qc, kc).astype(jnp.float32) * scale + b_c
        p_c = masked_softmax(s_c, m_c)
        o_c = jnp.einsum('bgrqn,bngd->bqgrd', p_c.astype(vc.dtype), vc)
        imp = jnp.einsum('bgrqn,nj->bgqj', p_c, overlap)
        cur = t // NSA_SEL_LEN
        forced = (j_blk[None, :] == 0) | (j_blk[None, :] == cur[:, None]) | (j_blk[None, :] == cur[:, None] - 1)
        valid = sel_start[None, :] <= t[:, None]
        imp = jnp.where(valid, jnp.where(forced, NSA_FORCE_SCORE, imp), -1.0)
        _, sel = lax.top_k(imp, n_top)
        k_g = ks_blk[b_idx, g_idx, sel].reshape(B, G, Qc, K_sel, hd)
        v_g = vs_blk[b_idx, g_idx, sel].reshape(B, G, Qc, K_sel, hd)
        pos = (sel[..., None] * NSA_SEL_LEN + jnp.arange(NSA_SEL_LEN)).reshape(B, G, Qc, K_sel)
        d_s = t[None, None, :, None] - pos
        m_s = (d_s >= 0)[:, :, None]
        b_s = jnp.moveaxis(rel[t5_bucket(d_s), g_idx], -1, 2).astype(jnp.float32)
        s_s = jnp.einsum('bqgrd,bgqkd->bgrqk', qc, k_g).astype(jnp.float32) * scale + b_s
        p_s = masked_softmax(s_s, m_s)
        o_s = jnp.einsum('bgrqk,bgqkd->bqgrd', p_s.astype(v_g.dtype), v_g)
        kw = lax.dynamic_slice_in_dim(kw_pad, q0, NSA_WINDOW + Qc, axis=1)
        vw = lax.dynamic_slice_in_dim(vw_pad, q0, NSA_WINDOW + Qc, axis=1)
        w_pos = q0 - NSA_WINDOW + jnp.arange(NSA_WINDOW + Qc)
        d_w = t[:, None] - w_pos[None, :]
        m_w = (d_w >= 0) & (d_w < NSA_WINDOW) & (w_pos[None, :] >= 0)
        b_w = jnp.moveaxis(rel[t5_bucket(d_w)], (2, 3), (0, 1)).astype(jnp.float32)
        s_w = jnp.einsum('bqgrd,bkgd->bgrqk', qc, kw).astype(jnp.float32) * scale + b_w
        p_w = masked_softmax(s_w, m_w)
        o_w = jnp.einsum('bgrqk,bkgd->bqgrd', p_w.astype(vw.dtype), vw)
        return gc[..., 0:1] * o_c + gc[..., 1:2] * o_s + gc[..., 2:3] * o_w

    starts = jnp.arange(S // Qc) * Qc
    o = merge_blocks(lax.map(chunk, (query_blocks(q, Qc), query_blocks(gates, Qc), starts)))
    return o.reshape(B, S, D_MODEL) @ w_out

def forgetting_attention(h, w_in, b_f, w_out):
    B, S, _ = h.shape
    proj = h @ w_in
    q = proj[..., :D_MODEL].reshape(B, S, FOX_HEADS, HEAD_DIM_2)
    k = proj[..., D_MODEL:2 * D_MODEL].reshape(B, S, FOX_HEADS, HEAD_DIM_2)
    v = proj[..., 2 * D_MODEL:3 * D_MODEL].reshape(B, S, FOX_HEADS, HEAD_DIM_2)
    log_f = jax.nn.log_sigmoid((proj[..., 3 * D_MODEL:] + b_f).astype(jnp.float32))
    c = jnp.cumsum(log_f, axis=1)
    c_k = jnp.moveaxis(c, 1, 2)
    scale = HEAD_DIM_2 ** -0.5
    key_pos = jnp.arange(S)

    def block(args):
        qb, cq, q0 = args
        t = q0 + jnp.arange(Q_BLOCK)
        mask = t[:, None] >= key_pos[None, :]
        decay = jnp.moveaxis(cq, 1, 2)[..., None] - c_k[:, :, None, :]
        s = jnp.einsum('bqhd,bkhd->bhqk', qb, k).astype(jnp.float32) * scale + decay
        pr = masked_softmax(s, mask)
        return jnp.einsum('bhqk,bkhd->bqhd', pr.astype(v.dtype), v)

    starts = jnp.arange(S // Q_BLOCK) * Q_BLOCK
    o = merge_blocks(lax.map(block, (query_blocks(q, Q_BLOCK), query_blocks(c, Q_BLOCK), starts)))
    return o.reshape(B, S, D_MODEL) @ w_out

def sqrelu_mlp(h, w1, w2):
    return jnp.square(jax.nn.relu(h @ w1)) @ w2

def second_inputs(seed: int = 0) -> dict:
    key = jax.random.key(seed)
    ks = list(jax.random.split(key, 24))

    def nrm(i, shape, scale):
        return jax.random.normal(ks[i], shape, jnp.float32) * scale

    D = D_MODEL
    return {
        'x': nrm(0, (BATCH, SEQ, D), 1.0),
        'p': nrm(1, (DEPTH_2, BATCH, SEQ, PLE_DIM), 1.0),
        'rel_bias': nrm(2, (REL_BUCKETS, REL_HEADS), 0.5),
        'norm_g': 1.0 + nrm(3, (DEPTH_2, 4, D), 0.02),
        'mlp_w1': nrm(4, (DEPTH_2, D, D_FF_2), D ** -0.5),
        'mlp_w2': nrm(5, (DEPTH_2, D_FF_2, D), D_FF_2 ** -0.5),
        'ple_w': nrm(6, (DEPTH_2, PLE_DIM, D), PLE_DIM ** -0.5),
        'ple_gate_w': nrm(7, (DEPTH_2, D, D), D ** -0.5),
        'da_w_in': nrm(8, (N_DA, D, DA_IN), D ** -0.5),
        'da_lambda': nrm(9, (N_DA, 4, HEAD_DIM_2), 0.1),
        'da_subln': 1.0 + nrm(10, (N_DA, 2 * HEAD_DIM_2), 0.02),
        'da_w_out': nrm(11, (N_DA, D, D), D ** -0.5),
        'nsa_w_in': nrm(12, (N_NSA, D, NSA_IN), D ** -0.5),
        'nsa_cmp_pe': nrm(13, (N_NSA, 2, NSA_CMP_LEN, HEAD_DIM_2), 0.1),
        'nsa_cmp_w1': nrm(14, (N_NSA, 2, NSA_CMP_LEN * HEAD_DIM_2, NSA_CMP_HIDDEN), (NSA_CMP_LEN * HEAD_DIM_2) ** -0.5),
        'nsa_cmp_w2': nrm(15, (N_NSA, 2, NSA_CMP_HIDDEN, HEAD_DIM_2), NSA_CMP_HIDDEN ** -0.5),
        'nsa_w_out': nrm(16, (N_NSA, D, D), D ** -0.5),
        'fox_w_in': nrm(17, (N_FOX, D, FOX_IN), D ** -0.5),
        'fox_b_f': 3.0 + nrm(18, (N_FOX, FOX_HEADS), 1.0),
        'fox_w_out': nrm(19, (N_FOX, D, D), D ** -0.5),
    }

def second_block(x, p, rel_bias, norm_g, mlp_w1, mlp_w2, ple_w, ple_gate_w,
              da_w_in, da_lambda, da_subln, da_w_out,
              nsa_w_in, nsa_cmp_pe, nsa_cmp_w1, nsa_cmp_w2, nsa_w_out,
              fox_w_in, fox_b_f, fox_w_out):
    ia, ib, ic = 0, 0, 0
    for i in range(DEPTH_2):
        g = norm_g[i]
        h = rmsnorm(x, g[0])
        kind = i % N_MIXERS_2
        if kind == 0:
            lam_init = 0.8 - 0.6 * math.exp(-0.3 * i)
            y = diff_attention(h, da_w_in[ia], da_lambda[ia], da_subln[ia], da_w_out[ia], rel_bias, lam_init)
            ia += 1
        elif kind == 1:
            y = nsa_attention(h, nsa_w_in[ib], nsa_cmp_pe[ib], nsa_cmp_w1[ib], nsa_cmp_w2[ib], nsa_w_out[ib], rel_bias)
            ib += 1
        else:
            y = forgetting_attention(h, fox_w_in[ic], fox_b_f[ic], fox_w_out[ic])
            ic += 1
        x = x + rmsnorm(y, g[1])
        y = sqrelu_mlp(rmsnorm(x, g[2]), mlp_w1[i], mlp_w2[i])
        x = x + rmsnorm(y, g[3])
        x = x + jax.nn.sigmoid(x @ ple_gate_w[i]) * (p[i] @ ple_w[i])
    return x


def setup_inputs(seed=0):
    out = dict(first_inputs(seed))
    for name, value in second_inputs(seed + 1).items():
        if name != "x":
            out[name + "_2"] = value
    return out


def reference(
    x, c, ctx, c_ctx, w_ada, b_ada, g_mix_pre, g_mix_post, g_mlp_pre, g_mlp_post, w_pool,
    pool_scale, w_qkv, g_q, g_k, w_o, w_mlp_in, w_mlp_out, p_2, rel_bias_2, norm_g_2, mlp_w1_2,
    mlp_w2_2, ple_w_2, ple_gate_w_2, da_w_in_2, da_lambda_2, da_subln_2, da_w_out_2, nsa_w_in_2,
    nsa_cmp_pe_2, nsa_cmp_w1_2, nsa_cmp_w2_2, nsa_w_out_2, fox_w_in_2, fox_b_f_2, fox_w_out_2,
):
    x = first_block(
        x, c, ctx, c_ctx, w_ada, b_ada, g_mix_pre, g_mix_post, g_mlp_pre, g_mlp_post, w_pool,
        pool_scale, w_qkv, g_q, g_k, w_o, w_mlp_in, w_mlp_out,
    )
    return second_block(
        x, p_2, rel_bias_2, norm_g_2, mlp_w1_2, mlp_w2_2, ple_w_2, ple_gate_w_2, da_w_in_2,
        da_lambda_2, da_subln_2, da_w_out_2, nsa_w_in_2, nsa_cmp_pe_2, nsa_cmp_w1_2,
        nsa_cmp_w2_2, nsa_w_out_2, fox_w_in_2, fox_b_f_2, fox_w_out_2,
    )


_drawn_inputs = setup_inputs


def setup_inputs(seed=0):
    import zlib

    import numpy as np

    out = dict(_drawn_inputs(seed))
    spreads = {}
    factors = {'g_q': 8.0, 'g_k': 8.0, 'da_subln_2': 3.255}
    for name, (base, spread) in spreads.items():
        noise = np.random.default_rng([zlib.crc32(name.encode()), seed]).standard_normal(out[name].shape)
        drawn = base * np.exp(spread * noise) if base else spread * noise
        out[name] = __import__('jax').numpy.asarray(drawn.astype(out[name].dtype))
    for name, factor in factors.items():
        out[name] = (out[name] * factor).astype(out[name].dtype)
    return out
```

```python
import math
from contextlib import ExitStack

import numpy as np

import concourse.bass as bass
from concourse import mybir
from concourse.alu_op_type import AluOpType as ALU

F32 = mybir.dt.float32
F32R = mybir.dt.float32r
ACT = mybir.ActivationFunctionType
AX = mybir.AxisListType

P = 128
D = 1024
KT = D // P
SEQ = 256
TT = SEQ // P
FF = 4 * D
GRID_W = 64
WINDOWS = (2, 4, 8, 16)
EPS = 1e-6
HALF = 64
BUCKETS = 32
NEG8 = -8e30
CMP_LEN, CMP_STRIDE = 32, 16
N_CMP = (SEQ - CMP_LEN) // CMP_STRIDE + 1
NC = 16
BIAS_W = 384
CHUNK = 2048
QUARTERS = 4
RAW_SLOTS = 5
HI_SLOTS = 4
AHEAD = 2


def shape_constants():
    t = np.arange(SEQ)
    pool = np.zeros((len(WINDOWS), SEQ, SEQ), np.float32)
    for g, w in enumerate(WINDOWS):
        lo, hi = np.clip(t - w // 2, 0, SEQ), np.clip(t + w - w // 2, 0, SEQ)
        for j in range(SEQ):
            pool[g, lo[j]:hi[j], j] = 1.0 / (hi[j] - lo[j])
            pool[g, j, j] -= 1.0
    half = P // 2
    freq = np.power(np.float32(10000.0), -np.arange(0, half, 2, dtype=np.float32) / half)
    row, col = (t // GRID_W).astype(np.float32), (t % GRID_W).astype(np.float32)
    ar, ac = row[:, None] * freq, col[:, None] * freq
    cos = np.concatenate([np.cos(ar), np.cos(ar), np.cos(ac), np.cos(ac)], 1)
    sin = np.concatenate([-np.sin(ar), np.sin(ar), -np.sin(ac), np.sin(ac)], 1)
    dist = 255 - np.arange(BIAS_W)
    n = np.maximum(dist, 0)
    exact = BUCKETS // 2
    nf = np.maximum(n, 1).astype(np.float32)
    large = exact + (np.log(nf / np.float32(exact)) / np.float32(math.log(128 / exact))
                     * np.float32(BUCKETS - exact)).astype(np.int32)
    bucket = np.where(n < exact, n, np.minimum(large, BUCKETS - 1))
    onehot = (np.arange(BUCKETS)[:, None] == bucket[None, :]) & (dist >= 0)[None, :]
    tiles = lambda a: np.ascontiguousarray(a.reshape(TT, P, -1).transpose(1, 0, 2), dtype=np.float32)
    return {
        "k_ident": np.eye(P, dtype=np.float32),
        "k_pool": np.ascontiguousarray(pool.reshape(4, TT, P, SEQ).transpose(2, 0, 1, 3).reshape(P, 8, SEQ)),
        "k_cos": tiles(cos), "k_sin": tiles(sin),
        "k_onehot": onehot.astype(np.float32),
        "k_mask8": np.broadcast_to(np.where(dist >= 0, 0.0, NEG8).astype(np.float32), (16, BIAS_W)).copy(),
        "k_cumsum": tiles((t[:, None] <= t[None, :]).astype(np.float32)),
        "k_valid": tiles((t >= CMP_LEN - 1).astype(np.float32)[:, None]),
        "k_headrow": (np.arange(P)[:, None] // NC == np.arange(8)[None, :]).astype(np.float32),
        "k_swap": np.eye(P, dtype=np.float32)[:, (np.arange(P) + HALF) % P].copy(),
        "k_modsel": np.array([[1, 0], [0, 1], [1, 0], [0, 1], [1, 1]], np.float32),
    }


class Lane:

    def __init__(self, semaphore):
        self.semaphore, self.count, self.steps, self.passed = semaphore, 0, [], {}

    def wait(self, *tokens):
        for token in tokens:
            if token is None:
                continue
            if isinstance(token, list):
                self.wait(*token)
                continue
            semaphore, value = token
            if self.passed.get(id(semaphore), 0) < value:
                self.passed[id(semaphore)] = value
                self.steps.append(lambda e, s=semaphore, v=value: e.wait_ge(s, v))

    def quiet(self, step, *tokens):
        self.wait(*tokens)
        self.steps.append(step)

    def run(self, step, *tokens):
        self.wait(*tokens)
        self.count += 1
        self.steps.append(lambda e: step(e).then_inc(self.semaphore, 1))
        return self.semaphore, self.count

    def dma(self, out, in_, semaphore, value, *tokens):
        self.wait(*tokens)
        self.steps.append(lambda e: e.dma_start(out, in_, allow_slow_non_contiguous=True).then_inc(semaphore, 16))
        return semaphore, value


def view(base, offset, dims):
    return bass.AP(base.tensor, base.offset + offset, [list(base.ap[0])] + [list(d) for d in dims])


def build(nc, A, out):
    with ExitStack() as ctx:
        _build(nc, A, out, ctx)


def _build(nc, A, out, ctx):
    sb = lambda name, shape, dt=F32: ctx.enter_context(nc.sbuf_tensor(name, shape, dt))
    sem = lambda name: ctx.enter_context(nc.semaphore(name))

    pe, dve, act, pool, sp = (Lane(sem(f"{n}_done")) for n in ("tensor", "vector", "scalar", "gpsimd", "sync"))

    twins = {}

    def with_twin(name, shape):
        with nc.sbuf_tensor(name, shape, F32) as full:
            pass
        parts = sb(name + "_split", shape, F32R)
        twins[name], twins[name + "_split"] = parts, full
        return full, parts

    def twin(ap):
        return bass.AP(twins[ap.tensor.name], ap.offset, [list(d) for d in ap.ap])

    raw = [with_twin(f"raw{i}", [P, CHUNK])[0] for i in range(RAW_SLOTS)]
    hi = [sb(f"hi{i}", [P, CHUNK], F32R) for i in range(HI_SLOTS)]
    x_rows = sb("x_rows", [P, TT, D])
    ctx_rows, _ = with_twin("ctx_rows", [P, TT, D])
    hcols, _ = with_twin("hcols", [P, 8192])
    work, _ = with_twin("work", [P, 12288])
    gains = sb("gains", [P, 2, D])
    mods = sb("mods", [5, 2, D])
    ident = sb("ident", [P, P])
    small = sb("small", [P, 1024])
    psum = ctx.enter_context(nc.psum_tensor("psum", [P, 8, 512], F32))
    bank_free = [None] * 8
    bank = lambda i: psum[:, i, :]

    cursor = [0]

    def scalars(n):
        cursor[0] += n
        assert cursor[0] <= 1024
        return small[:, cursor[0] - n:cursor[0]]

    def load(name, out_, in_, *tokens):
        return pool.dma(out_, in_, sem("at_" + name), 16, *tokens)

    plan = []

    def cols_first(w, c0, width=256):
        return w[:, c0:c0 + width].rearrange("(k p) n -> p k n", p=P)

    def plan_stationary(w, c0, c1):
        for c in range(c0, c1, 256):
            plan.append(cols_first(w, c, 256))

    def plan_half_k(w, c0, c1):
        for c in range(c0, c1, 512):
            for k in range(2):
                plan.append(w[k * 512:(k + 1) * 512, c:c + 512].rearrange("(k p) n -> p k n", p=P))

    def plan_rows(w):
        for k in range(0, w.shape[0], 256):
            plan.append(w[k:k + 256, :].rearrange("(k p) n -> p k n", p=P))

    def plan_mlp0(w1, w2):
        for q in range(QUARTERS):
            plan_stationary(w1, q * D, q * D + D)
            for ch in range(2):
                for k in range(2):
                    r = q * D + k * 512
                    plan.append(w2[r:r + 512, ch * 512:ch * 512 + 512].rearrange("(k p) n -> p k n", p=P))

    def plan_mlp(w1, w2):
        for q in range(QUARTERS + 1):
            if q < QUARTERS:
                plan_stationary(w1, q * D, q * D + D)
            if q > 0:
                plan_rows(w2[(q - 1) * D:q * D, :])

    plan_half_k(A["w_ada"][0], 0, 6 * D)
    plan.append(A["w_pool"][0].rearrange("g (k p) n -> p (g k) n", p=P))
    plan_mlp0(A["w_mlp_in"][0], A["w_mlp_out"][0])
    plan_half_k(A["w_ada"][1], 0, 6 * D)
    plan_half_k(A["w_qkv"][0], 0, 1536)
    plan_rows(A["w_o"][0])
    plan_mlp(A["w_mlp_in"][1], A["w_mlp_out"][1])
    for i in range(4):
        if i % 3 == 0:
            w = A["da_w_in_2"][i // 3]
            plan_stationary(w, 0, 2 * D)
            plan_half_k(w, 2 * D, 3 * D)
            plan_rows(A["da_w_out_2"][i // 3])
        elif i == 1:
            w = A["nsa_w_in_2"][0]
            plan_stationary(w, 0, D)
            for c in (0, 1, 2, 4):
                plan_stationary(w, D + c * 256, D + c * 256 + 256)
            for c in (3, 5):
                plan_stationary(w, D + c * 256, D + c * 256 + 256)
            for b in range(2):
                for c in range(2):
                    plan.append(A["nsa_cmp_w1_2"][0][b][c * 1024:c * 1024 + 1024, :].rearrange("(k p) n -> p k n", p=P))
            plan_rows(A["nsa_w_out_2"][0])
        else:
            w = A["fox_w_in_2"][0]
            plan_stationary(w, 0, 2 * D)
            plan_half_k(w, 2 * D, 3 * D)
            plan_rows(A["fox_w_out_2"][0])
        plan_mlp(A["mlp_w1_2"][i], A["mlp_w2_2"][i])
        plan_rows(A["ple_gate_w_2"][i])
        plan.append(A["ple_w_2"][i].rearrange("(k p) n -> p k n", p=P))

    raw_at = [sem(f"raw_at{i}") for i in range(RAW_SLOTS)]
    loaded, split, used = [], [], []

    def load_chunk():
        n = len(loaded)
        if n < len(plan):
            src = plan[n]
            dst = raw[n % RAW_SLOTS][:, :].rearrange("p (k n) -> p k n", k=src.shape[1])
            loaded.append(sp.dma(dst, src, raw_at[n % RAW_SLOTS], 16 * (n // RAW_SLOTS + 1),
                                 used[n - RAW_SLOTS] if n >= RAW_SLOTS else None))

    def split_chunk():
        n = len(split)
        if n < len(plan):
            h, r = hi[n % HI_SLOTS][:, :], raw[n % RAW_SLOTS][:, :]
            made = act.run(lambda e: e.activation(h, r, ACT.Copy),
                           loaded[n], used[n - HI_SLOTS] if n >= HI_SLOTS else None)
            split.append(dve.run(lambda e: e.tensor_tensor(twin(r), r, h.bitcast(F32), ALU.subtract), made))

    def take():
        n = len(used)
        while len(split) < min(n + 1 + AHEAD, len(plan)):
            split_chunk()
        k = plan[n].shape[1]
        shaped = lambda a: a.rearrange("p (k n) -> p k n", k=k)
        return (shaped(hi[n % HI_SLOTS][:, :]), shaped(twin(raw[n % RAW_SLOTS][:, :]))), split[n]

    def give_back(token):
        used.append(token)
        load_chunk()

    for _ in range(RAW_SLOTS):
        load_chunk()

    at_ident = load("ident", ident[:, :], A["k_ident"])
    at_x = load("x", x_rows[:, :, :], A["x"][0].rearrange("(t p) d -> p t d", p=P))
    at_ctx = load("ctx", ctx_rows[:, :, :], A["ctx"][0].rearrange("(t p) d -> p t d", p=P))
    mod_select = sb("mod_select", [5, 2])
    at_modsel = load("modsel", mod_select[:, :], A["k_modsel"])

    minus_half = scalars(32)
    set_minus_half = pool.run(lambda e: e.memset(minus_half, -0.5))

    def column_gain(name, vector):
        dst = scalars(KT)
        return dst, load(name, dst, vector.rearrange("(k p) -> p k", p=P))

    def row_gain(name, slot, vector, *tokens):
        return load(name, gains[:, slot, :], vector.rearrange("(a d) -> a d", a=1).broadcast_to([P, D]), *tokens)

    def mm(out_, lhs, rhs, start, stop):
        return lambda e: e.matmul(out_, lhs, rhs, start=start, stop=stop, skip_group_check=True)

    def product(out_, pairs, *tokens):
        for n, (lhs, rhs) in enumerate(pairs):
            step = mm(out_, lhs, rhs, n == 0, n == len(pairs) - 1)
            if n < len(pairs) - 1:
                pe.quiet(step, *tokens)
        return pe.run(step, *tokens)

    def three(a, b):
        (ah, al), (bh, bl) = a, b
        return [(ah, bh), (ah, bl), (al, bh)]

    def inverse_root(sumsq, n, width, *tokens):
        a = pool.run(lambda e: e.tensor_scalar(sumsq, sumsq, 1.0 / n, EPS, ALU.mult, ALU.add), *tokens)
        return pool.run(lambda e: e.tensor_tensor(sumsq, sumsq, minus_half[:, 0:width], ALU.pow), a, set_minus_half)

    def sum_of_squares(src, dst, junk, *tokens):
        return act.run(lambda e: e.activation(junk, src, ACT.Square, accum_out=dst), *tokens)

    norm_scale = scalars(8)
    diag = sb("diag", [P, 4, P])

    last_to_cols = [None]

    def to_cols(tiles, normed, scale, shift, hi_cols, lo_cols, full, *tokens):
        n_tiles = len(tiles)
        tokens = list(tokens)
        ready = []
        for t, (src, at) in enumerate(tiles):
            if normed:
                ss = norm_scale[:, t:t + 1]
                a = sum_of_squares(src, ss, full[:, :, t * P:(t + 1) * P], at, tokens, last_to_cols[0])
                r = inverse_root(ss, D, 1, a)
                ready.append(dve.run(lambda e, t=t, ss=ss: e.tensor_scalar(diag[:, t, :], ident[:, :], ss, None, ALU.mult),
                                     r, at_ident, last_to_cols[0]))
            else:
                ready.append([at, at_ident])
        per_bank = 512 // (n_tiles * P)
        for b in range(KT // per_bank):
            bk = 4 + b % 4
            for j in range(per_bank):
                k = b * per_bank + j
                for t, (src, at) in enumerate(tiles):
                    o = bank(bk)[:, (j * n_tiles + t) * P:(j * n_tiles + t + 1) * P]
                    lhs = src[:, k * P:(k + 1) * P]
                    if normed:
                        got = product(o, [(lhs, diag[:, t, :])], ready[t], at, bank_free[bk])
                    else:
                        got = pe.run(lambda e, o=o, lhs=lhs: e.transpose(o, lhs, ident[:, :]), ready[t], bank_free[bk])
            ks = slice(b * per_bank, (b + 1) * per_bank)
            src = bank(bk).rearrange("p (k n) -> p k n", k=per_bank)
            h, l = hi_cols[:, ks, :], lo_cols[:, ks, :]
            if not normed:
                h_at = act.run(lambda e, h=h, src=src: e.activation(h, src, ACT.Copy), got, tokens)
                l_at = dve.run(lambda e, h=h, l=l, src=src: e.tensor_tensor(l, src, h.bitcast(F32), ALU.subtract), h_at, tokens)
                bank_free[bk] = l_at
            else:
                for j in range(per_bank):
                    k = b * per_bank + j
                    f_at = act.run(lambda e, k=k, j=j, src=src: e.activation(
                        full[:, k, :], src[:, j, :], ACT.Identity,
                        bias=shift[:, k:k + 1] if shift is not None else 0.0, scale=scale[:, k:k + 1]), got, tokens)
                f = full[:, ks, :]
                bank_free[bk] = f_at
                h_at = dve.run(lambda e, h=h, f=f: e.tensor_copy(h, f), f_at, tokens)
                l_at = dve.run(lambda e, h=h, l=l, f=f: e.tensor_tensor(l, f, h.bitcast(F32), ALU.subtract), h_at)
        last_to_cols[0] = [l_at, got]
        return l_at

    def hcols_split(n_tokens, region=None, base=0):
        r = hcols if region is None else region
        n = KT * n_tokens
        shaped = lambda o: r[:, base + o:base + o + n].rearrange("p (k n) -> p k n", k=KT)
        return twin(shaped(0)), twin(shaped(n))

    def full_scratch(n_tokens, base=8192):
        return work[:, base:base + KT * n_tokens].rearrange("p (k n) -> p k n", k=KT)

    rms_scale = scalars(4)
    last_tail = [None]

    def tail(x, t, y, gain, junk, x_at, *tokens):
        ss = rms_scale[:, t:t + 1]
        a = sum_of_squares(y, ss, junk, *tokens, last_tail[0])
        r = inverse_root(ss, D, 1, a)
        m = dve.run(lambda e: e.scalar_tensor_tensor(junk, y, ss, gain, ALU.mult, ALU.mult), r, *tokens)
        last_tail[0] = m
        return dve.run(lambda e: e.tensor_tensor(x, x, junk, ALU.add), m, x_at), m

    def y_banks(t):
        return view(bank(2 * t), 0, [[1, D]])

    def rows_product(cols, n_k, *tokens, first_bank=0, begin=True, end=True, cols_at=None):
        for n in range(n_k // 2):
            w, at = take()
            for t in range(TT):
                for ch in range(2):
                    bk = first_bank + 2 * t + ch
                    pairs = []
                    for j in range(2):
                        k = 2 * n + j
                        pairs += three(tuple(c[:, k, t * P:(t + 1) * P] for c in cols),
                                       tuple(c[:, j, ch * 512:ch * 512 + 512] for c in w))
                    start, stop = begin and n == 0, end and n == n_k // 2 - 1
                    free = bank_free[bk] if start else None
                    for m, (lhs, rhs) in enumerate(pairs):
                        step = mm(bank(bk), lhs, rhs, start and m == 0, stop and m == len(pairs) - 1)
                        if t == 1 and ch == 1 and m == len(pairs) - 1:
                            done = pe.run(step)
                        else:
                            pe.quiet(step, at, list(tokens), free, cols_at[n] if cols_at else None)
            give_back(done)
        return done

    def squared_relu(src, h, l, got, free):
        full = twin(l)
        a = act.run(lambda e: e.activation(full, src, ACT.Relu), got, free)
        s = dve.run(lambda e: e.tensor_tensor(full, full, full, ALU.mult), a)
        c = act.run(lambda e: e.activation(h, full, ACT.Copy), s)
        return a, dve.run(lambda e: e.tensor_tensor(l, full, h.bitcast(F32), ALU.subtract), c)

    def mlp(cols, cols_at, work_free):
        quarter = []
        used_at = [work_free, work_free]
        for q in range(QUARTERS + 1):
            if q < QUARTERS:
                base = (q % 2) * 4096
                shaped = lambda o: twin(work[:, base + o:base + o + 2048].rearrange("p (k n) -> p k n", k=KT))
                hh, hl = shaped(0), shaped(2048)
                ready = []
                for n in range(KT // 2):
                    w, at = take()
                    bk = 4 + n % 4
                    for j in range(2):
                        pairs = []
                        for k in range(KT):
                            pairs += three(tuple(c[:, k, j * P:(j + 1) * P] for c in w), tuple(c[:, k, :] for c in cols))
                        got = product(bank(bk)[:, j * SEQ:(j + 1) * SEQ], pairs, at, cols_at, bank_free[bk])
                    give_back(got)
                    bank_free[bk], done = squared_relu(bank(bk).rearrange("p (k n) -> p k n", k=2), hh[:, 2 * n:2 * n + 2, :],
                                                       hl[:, 2 * n:2 * n + 2, :], got, used_at[q % 2])
                    ready.append(done)
                quarter.append(((hh, hl), ready))
            if q > 0:
                parts, ready = quarter[q - 1]
                used_at[(q - 1) % 2] = rows_product(parts, KT, begin=q == 1, end=q == QUARTERS, cols_at=ready)
        return used_at[(QUARTERS - 1) % 2]

    cond = sb("cond", [P, KT, 4], F32R)
    cond_full = scalars(2 * KT).rearrange("p (k n) -> p k n", n=2)
    cond_tanh = scalars(2 * KT).rearrange("p (k n) -> p k n", n=2)
    at_c = load("c", cond_full[:, :, 0], A["c"].rearrange("a (k p) -> p (a k)", p=P))
    at_cc = load("c_ctx", cond_full[:, :, 1], A["c_ctx"].rearrange("(k p) -> p k", p=P))
    tok = act.run(lambda e: e.activation(cond_tanh, cond_full, ACT.Tanh, scale=0.5), at_c, at_cc)
    tok = dve.run(lambda e: e.scalar_tensor_tensor(cond_full, cond_tanh, 1.0, cond_full, ALU.add, ALU.mult), tok)
    tok = dve.run(lambda e: e.tensor_scalar(cond_full, cond_full, 0.5, None, ALU.mult), tok)
    tok = dve.run(lambda e: e.tensor_copy(cond[:, :, 0:2], cond_full), tok)
    cond_at = dve.run(lambda e: e.tensor_tensor(cond[:, :, 2:4], cond_full, cond[:, :, 0:2].bitcast(F32), ALU.subtract), tok)

    mods_free = [None, None]
    sel_rows = sb("sel_rows", [5, 2, P])
    sel_at = [dve.run(lambda e, n=n: e.tensor_copy(sel_rows[:, n, :], mod_select[:, n:n + 1].broadcast_to([5, P])), at_modsel)
              for n in range(2)]
    mod_cols = scalars(2 * 4 * KT * 2).rearrange("p (l m k n) -> p l m k n", l=2, m=4, k=KT)

    def modulation(layer, m, slot):
        row = mods[:, slot, :]
        b_at = load(f"b_ada{layer}{m}", row[4:5, :], A["b_ada"][layer:layer + 1, m * D:(m + 1) * D], mods_free[slot])
        parts = [b_at]
        for ch in range(2):
            bk = ch
            for half in range(2):
                w, at = take()
                for k in range(4):
                    for n, part in enumerate(w):
                        first, last = half == 0 and k == 0 and n == 0, k == 3 and n == 1
                        step = mm(bank(bk)[0:4, :], cond[:, half * 4 + k, :], part[:, k, :], first, half == 1 and last)
                        if last:
                            got = pe.run(step)
                        else:
                            pe.quiet(step, at, cond_at, bank_free[bk])
                give_back(got)
            c = act.run(lambda e, ch=ch, bk=bk: e.activation(row[0:4, ch * 512:ch * 512 + 512], bank(bk)[0:4, :], ACT.Copy),
                        got, mods_free[slot])
            bank_free[bk] = c
            parts.append(c)
        return parts

    def mod_to_cols(slot, dst, parts):
        bk = 2
        for k in range(KT):
            got = product(bank(bk)[:, 2 * k:2 * k + 2], [(mods[:, slot, k * P:(k + 1) * P], mod_select[:, :])],
                          parts, at_modsel, bank_free[bk])
        mods_free[slot] = got
        done = dve.run(lambda e: e.tensor_copy(dst, bank(bk)[:, 0:2 * KT].rearrange("p (k n) -> p k n", n=2)), got)
        bank_free[bk] = done
        return done

    def mod_to_rows(slot, which, parts, first_bank):
        for ch in range(2):
            got = product(bank(first_bank + ch), [(sel_rows[:, which, :], mods[:, slot, ch * 512:ch * 512 + 512])],
                          parts, sel_at, bank_free[first_bank + ch])
        return got

    def gate_gain(slot, which, parts, g, g_at, first_bank):
        got = mod_to_rows(slot, which, parts, first_bank)
        done = dve.run(lambda e: e.tensor_tensor(gains[:, g, :], view(bank(first_bank), 0, [[1, D]]), gains[:, g, :], ALU.mult),
                       got, g_at)
        for b in range(2):
            bank_free[first_bank + b] = done
        return done, got

    PH, PA, PM = 0, 4096, 8192
    pool_m = work[:, PM:PM + 2048].rearrange("p (g n) -> p g n", g=8)
    at_pool = load("pool", pool_m, A["k_pool"])
    g_pre_row = work[:, PM + 2048:PM + 3072]
    at_gpre = load("gpre0", g_pre_row, A["g_mix_pre"][0:1, :].broadcast_to([P, D]))
    pool_scale = work[:, PM + 3072:PM + 4096]
    at_pscale = load("pscale", pool_scale, A["pool_scale"][0:1, :].broadcast_to([P, D]))
    stats0 = scalars(4)
    seqs = [(x_rows, at_x), (ctx_rows, at_ctx)]
    sq_at = []
    for n, (rows, at) in enumerate(seqs):
        for t in range(TT):
            junk = hcols[:, (2 * n + t) * D:(2 * n + t + 1) * D]
            sq_at.append(sum_of_squares(rows[:, t, :], stats0[:, 2 * n + t:2 * n + t + 1], junk, at))
    rstd0_at = inverse_root(stats0, D, 4, sq_at)
    g0_at = [row_gain(f"gpost0_{s}", s, A["g_mix_post"][0]) for s in range(2)]

    shift_parts = modulation(0, 0, 0)
    shift_at = [mod_to_rows(0, n, shift_parts, 4 + 2 * n) for n in range(2)]
    mods_free[0] = shift_at[1]
    scale_parts = modulation(0, 1, 1)
    h_at = []
    for n, (rows, at) in enumerate(seqs):
        a_row = work[:, PA + n * D:PA + (n + 1) * D]
        got = mod_to_rows(1, n, scale_parts, 2)
        a_at = dve.run(lambda e, a_row=a_row: e.scalar_tensor_tensor(a_row, view(bank(2), 0, [[1, D]]), 1.0, g_pre_row, ALU.add, ALU.mult),
                       got, at_gpre)
        bank_free[2] = bank_free[3] = a_at
        mods_free[1] = got
        for t in range(TT):
            i = 2 * n + t
            h = work[:, PH + i * D:PH + (i + 1) * D]
            m = dve.run(lambda e, h=h, i=i, t=t, rows=rows, a_row=a_row: e.scalar_tensor_tensor(
                h, rows[:, t, :], stats0[:, i:i + 1], a_row, ALU.mult, ALU.mult), a_at, rstd0_at, at)
            s_at = dve.run(lambda e, h=h, n=n: e.tensor_tensor(h, h, view(bank(4 + 2 * n), 0, [[1, D]]), ALU.add),
                           m, shift_at[n])
        bank_free[4 + 2 * n] = bank_free[5 + 2 * n] = s_at
        h_at.append(s_at)

    gt1_parts = modulation(0, 2, 0)
    g0_at = [gate_gain(0, n, gt1_parts, n, g0_at[n], 2)[0] for n in range(2)]
    mods_free[0] = g0_at

    g_mlp_pre = [column_gain(f"g_mlp_pre{l}", A["g_mlp_pre"][l]) for l in range(2)]
    sh2_at = mod_to_cols(1, mod_cols[:, 0, 2, :, :], modulation(0, 3, 1))
    sc2_at = mod_to_cols(0, mod_cols[:, 0, 3, :, :], modulation(0, 4, 0))

    def pre_scale(layer, m, gain, gain_at, at):
        return [dve.run(lambda e, n=n: e.scalar_tensor_tensor(mod_cols[:, layer, m, :, n], mod_cols[:, layer, m, :, n], 1.0,
                                                             gain, ALU.add, ALU.mult), at, gain_at) for n in range(2)]

    sc2_at = pre_scale(0, 3, *g_mlp_pre[0], sc2_at)
    gt2_parts = modulation(0, 5, 1)

    dh, dl = hcols_split(2 * SEQ)
    diff_at = []
    for n in range(2):
        for c in range(KT):
            i = n * KT + c
            bk = 4 + (i // 2) % 4
            o = bank(bk)[:, (i % 2) * SEQ:(i % 2 + 1) * SEQ]
            got = product(o, [(work[:, PH + (2 * n + t) * D + c * P:PH + (2 * n + t) * D + (c + 1) * P], pool_m[:, (c // 2) * 2 + t, :])
                              for t in range(TT)], h_at[n], at_pool, bank_free[bk])
            if i % 2:
                cs, ts = slice(c - 1, c + 1), slice(n * SEQ, (n + 1) * SEQ)
                src = bank(bk).rearrange("p (k n) -> p k n", k=2)
                a = act.run(lambda e, cs=cs, ts=ts, src=src: e.activation(dh[:, cs, ts], src, ACT.Copy), got)
                d_at = dve.run(lambda e, cs=cs, ts=ts, src=src: e.tensor_tensor(dl[:, cs, ts], src, dh[:, cs, ts].bitcast(F32), ALU.subtract), a)
                bank_free[bk] = d_at
        diff_at.append(d_at)
    w, at = take()
    for n in range(2):
        for t in range(TT):
            tile = slice((2 * n + t) * P, (2 * n + t + 1) * P)
            for g in range(4):
                bk = 4 * n + 2 * t + g // 2
                pairs = []
                for k in range(2):
                    pairs += three(tuple(c[:, 2 * g + k, tile] for c in (dh, dl)), tuple(c[:, 2 * g + k, :] for c in w))
                got = product(bank(bk)[:, (g % 2) * 256:(g % 2 + 1) * 256], pairs, at, diff_at, bank_free[bk])
    give_back(got)
    new_at = []
    for n, (rows, _) in enumerate(seqs):
        for t in range(TT):
            i = 2 * n + t
            y = work[:, PH + i * D:PH + (i + 1) * D]
            junk = hcols[:, i * D:(i + 1) * D]
            y_at = dve.run(lambda e, y=y, i=i: e.tensor_tensor(y, view(bank(2 * i), 0, [[1, D]]), pool_scale, ALU.mult), got, at_pscale)
            bank_free[2 * i] = bank_free[2 * i + 1] = y_at
            new_at.append(tail(rows[:, t, :], i, y, gains[:, n, :], junk, [], y_at, g0_at)[0])
    x_at = new_at

    tail_done = new_at[-1]
    g0_at = [row_gain(f"gpost0m_{s}", s, A["g_mlp_post"][0], tail_done) for s in range(2)]
    hh, hl = hcols_split(2 * SEQ)
    for n, (rows, _) in enumerate(seqs):
        ts = slice(n * SEQ, (n + 1) * SEQ)
        cols_at = to_cols([(rows[:, t, :], x_at[2 * n + t]) for t in range(TT)], True,
                          mod_cols[:, 0, 3, :, n], mod_cols[:, 0, 2, :, n], hh[:, :, ts], hl[:, :, ts],
                          full_scratch(SEQ, n * KT * SEQ), sh2_at, sc2_at, tail_done)
    g0_at = [gate_gain(1, n, gt2_parts, n, g0_at[n], 2 * n)[0] for n in range(2)]
    mods_free[1] = g0_at

    y_rows = work[:, 8192:12288].rearrange("p (i d) -> p i d", i=4)
    shaped = lambda o: twin(work[:, o:o + 4096].rearrange("p (k n) -> p k n", k=KT))
    fh, fl = shaped(0), shaped(4096)
    hidden_free = cols_at
    y_at = [[cols_at, cols_at] for _ in range(4)]
    for q in range(QUARTERS):
        ready = []
        for n in range(KT // 2):
            w, at = take()
            for j in range(2):
                f = 2 * n + j
                bk = 4 + f % 4
                pairs = []
                for k in range(KT):
                    pairs += three(tuple(c[:, k, j * P:(j + 1) * P] for c in w), (hh[:, k, :], hl[:, k, :]))
                got = product(bank(bk), pairs, at, cols_at, bank_free[bk])
                bank_free[bk], done = squared_relu(bank(bk), fh[:, f, :], fl[:, f, :], got, hidden_free)
                ready.append(done)
            give_back(got)
        for ch in range(2):
            for n in range(2):
                w, at = take()
                for i in range(4):
                    pairs = []
                    for j in range(4):
                        pairs += three(tuple(c[:, 4 * n + j, i * P:(i + 1) * P] for c in (fh, fl)), tuple(c[:, j, :] for c in w))
                    for m, (lhs, rhs) in enumerate(pairs):
                        step = mm(bank(i), lhs, rhs, n == 0 and m == 0, n == 1 and m == len(pairs) - 1)
                        if m == len(pairs) - 1:
                            got = pe.run(step)
                        else:
                            pe.quiet(step, at, ready[4 * n + m // 3], bank_free[i] if n == 0 else None)
                    if n == 1:
                        seg = y_rows[:, i, ch * 512:ch * 512 + 512]
                        if q == 0:
                            e_at = act.run(lambda e, seg=seg, i=i: e.activation(seg, bank(i), ACT.Copy), got, y_at[i][ch])
                        else:
                            e_at = dve.run(lambda e, seg=seg, i=i: e.tensor_tensor(seg, bank(i), seg, ALU.add), got, y_at[i][ch])
                        y_at[i][ch] = e_at
                        bank_free[i] = e_at
                give_back(got)
        hidden_free = got
    x_at = [tail(seqs[i // 2][0][:, i % 2, :], i, y_rows[:, i, :], gains[:, i // 2, :], work[:, i * D:(i + 1) * D],
                 x_at[i], y_at[i], hidden_free, g0_at)[0] for i in range(4)]

    tail_done = x_at[-1]
    g1_at = [row_gain("gpost1", 0, A["g_mix_post"][1], tail_done), row_gain("gpost1m", 1, A["g_mlp_post"][1], tail_done)]
    g_pre1 = column_gain("g_pre1", A["g_mix_pre"][1])
    sh1_at = mod_to_cols(0, mod_cols[:, 1, 0, :, :], modulation(1, 0, 0))
    sc1_at = pre_scale(1, 1, *g_pre1, mod_to_cols(1, mod_cols[:, 1, 1, :, :], modulation(1, 1, 1)))
    g1_at[0], mods_free[0] = gate_gain(0, 0, modulation(1, 2, 0), 0, g1_at[0], 2)
    sh2_at = mod_to_cols(1, mod_cols[:, 1, 2, :, :], modulation(1, 3, 1))
    sc2_at = pre_scale(1, 3, *g_mlp_pre[1], mod_to_cols(0, mod_cols[:, 1, 3, :, :], modulation(1, 4, 0)))
    g1_at[1], mods_free[1] = gate_gain(1, 0, modulation(1, 5, 1), 1, g1_at[1], 2)

    for n, (rows, _) in enumerate(seqs):
        ts = slice(n * SEQ, (n + 1) * SEQ)
        cols_at = to_cols([(rows[:, t, :], x_at[2 * n + t]) for t in range(TT)], True,
                          mod_cols[:, 1, 1, :, n], mod_cols[:, 1, 0, :, n], hh[:, :, ts], hl[:, :, ts],
                          full_scratch(SEQ, n * KT * SEQ), sh1_at, sc1_at, tail_done)

    HQ, HKV, HD = 8, 2, P
    AT = 2 * TT
    q_rows = work[:, 0:2048].rearrange("p (t n) -> p t n", t=TT)
    kv_rows = work[:, 2048:4096].rearrange("p (t n) -> p t n", t=AT)
    scratch = work[:, 4096:6144]
    q_cols = work[:, 6144:8192].rearrange("p (h n) -> p h n", h=HQ)
    k_cols = work[:, 8192:9216].rearrange("p (h n) -> p h n", h=HKV)
    rope = work[:, 9216:10240].rearrange("p (i t n) -> p i t n", i=4, t=TT)
    e_buf = [work[:, 10240 + i * 512:10752 + i * 512] for i in range(2)]
    cols_done = [cols_at]
    got = None
    evac = []
    for c in range(3):
        tiles = TT if c < 2 else AT
        for half in range(2):
            w, at = take()
            for i in range(tiles):
                pairs = []
                for j in range(4):
                    pairs += three(tuple(h[:, 4 * half + j, i * P:(i + 1) * P] for h in (hh, hl)), tuple(h[:, j, :] for h in w))
                for m, (lhs, rhs) in enumerate(pairs):
                    bk = i if c != 1 else 4 + i
                    step = mm(bank(bk), lhs, rhs, half == 0 and m == 0, half == 1 and m == len(pairs) - 1)
                    if m == len(pairs) - 1:
                        got = pe.run(step)
                    else:
                        pe.quiet(step, at, cols_at, bank_free[bk] if half == 0 else None)
                if half == 1:
                    dst = q_rows[:, i, c * 512:c * 512 + 512] if c < 2 else kv_rows[:, i, :]
                    bank_free[bk] = act.run(lambda e, dst=dst, bk=bk: e.activation(dst, bank(bk), ACT.Copy), got, cols_at)
                    evac.append(bank_free[bk])
            give_back(got)
    qkv_at = evac[-1]

    gqk = sb("gqk", [P, 2, P])
    at_gq = load("g_q", gqk[:, 0, :], A["g_q"][0:1, :].broadcast_to([P, P]))
    at_gk = load("g_k", gqk[:, 1, :], A["g_k"][0:1, :].broadcast_to([P, P]))
    at_rope = [load(f"rope{i}", rope[:, i, :, :], A["k_cos"] if i % 2 == 0 else A["k_sin"], cols_at) for i in range(4)]
    rope_at = []
    for i in range(2):
        for t in range(TT):
            cos, sin = rope[:, 2 * i, t, :], rope[:, 2 * i + 1, t, :]
            g = gqk[:, i, :]
            rope_at.append(dve.run(lambda e, cos=cos, g=g: e.tensor_tensor(cos, cos, g, ALU.mult), at_gq, at_gk, at_rope))
            pair = lambda a, o: view(a, o, [[64, 2], [1, 32]])
            for o in range(2):
                rope_at.append(dve.run(lambda e, sin=sin, g=g, o=o: e.tensor_tensor(
                    pair(sin, 32 * o), pair(sin, 32 * o), pair(g, 32 - 32 * o), ALU.mult)))

    head_ss = scalars(24)
    k_heads = view(kv_rows, 0, [[512, AT], [P, HKV], [1, HD]])
    q_heads = view(q_rows, 0, [[D, TT], [P, HQ], [1, HD]])
    k_scr = view(scratch, 0, [[256, AT], [P, HKV], [1, HD]])
    q_scr = view(scratch, 0, [[D, TT], [P, HQ], [1, HD]])
    tok = dve.run(lambda e: e.tensor_tensor(q_scr, q_heads, q_heads, ALU.mult), qkv_at, tail_done)
    tok = dve.run(lambda e: e.tensor_reduce(head_ss[:, 0:16], view(scratch, 0, [[P, 16], [1, P]]), AX.X, ALU.add), tok)
    tok = dve.run(lambda e: e.tensor_tensor(k_scr, k_heads, k_heads, ALU.mult), tok)
    ss_at = dve.run(lambda e: e.tensor_reduce(head_ss[:, 16:24], view(scratch, 0, [[P, 8], [1, P]]), AX.X, ALU.add), tok)
    r_at = inverse_root(head_ss, HD, 24, ss_at)
    tok = dve.run(lambda e: e.tensor_tensor(q_heads, q_heads, view(head_ss, 0, [[HQ, TT], [1, HQ], [0, HD]]), ALU.mult), r_at)
    k_at = dve.run(lambda e: e.tensor_tensor(k_heads, k_heads, view(head_ss, 16, [[HKV, AT], [1, HKV], [0, HD]]), ALU.mult), r_at)

    def rotate(heads, scr, n_heads, row, table, *tokens):
        tokens = list(tokens)
        """heads = heads * cos + swapped heads * sin, for the latent token tiles."""
        for t in range(TT):
            part = lambda a, stride, o, t=t: view(a, t * stride + o, [[P, n_heads], [64, 2], [1, 32]])
            tbl = lambda o, t=t: view(rope, ((2 * table + 1) * TT + t) * P + o, [[0, n_heads], [64, 2], [1, 32]])
            for o in range(2):
                s_at = dve.run(lambda e, t=t, o=o, part=part, tbl=tbl: e.tensor_tensor(
                    part(scr, n_heads * P, 32 * o), part(heads, row, 32 - 32 * o), tbl(32 * o), ALU.mult), rope_at, k_at, tokens)
            whole = lambda a, stride, t=t: view(a, t * stride, [[P, n_heads], [1, P]])
            cos = view(rope, (2 * table * TT + t) * P, [[0, n_heads], [1, P]])
            c_at = dve.run(lambda e, whole=whole, cos=cos: e.tensor_tensor(whole(heads, row), whole(heads, row), cos, ALU.mult), s_at)
            done = dve.run(lambda e, whole=whole: e.tensor_tensor(whole(heads, row), whole(heads, row), whole(scr, n_heads * P), ALU.add), c_at)
        return done

    rk_at = rotate(kv_rows, scratch, HKV, 512, 1, tok)
    for t in range(TT, AT):
        kc = view(kv_rows, t * 512, [[P, HKV], [1, P]])
        kc_at = dve.run(lambda e, kc=kc: e.tensor_tensor(kc, kc, view(gqk[:, :, :], P, [[0, HKV], [1, P]]), ALU.mult), k_at)
    rq_at = rotate(q_rows, scratch, HQ, D, 0, rk_at)

    for h in range(HKV):
        bk = 4 + h
        for t in range(AT):
            got = pe.run(lambda e, bk=bk, h=h, t=t: e.transpose(bank(bk)[:, t * P:(t + 1) * P], kv_rows[:, t, h * P:(h + 1) * P], ident[:, :]),
                         rk_at, kc_at, bank_free[bk])
        kT_at = act.run(lambda e, bk=bk, h=h: e.activation(k_cols[:, h, :], bank(bk), ACT.Copy), got)
        bank_free[bk] = kT_at
    for b in range(HQ // 2):
        bk = 4 + (b + 2) % 4
        for j in range(2):
            for t in range(TT):
                got = pe.run(lambda e, bk=bk, b=b, j=j, t=t: e.transpose(bank(bk)[:, (2 * j + t) * P:(2 * j + t + 1) * P],
                             q_rows[:, t, (2 * b + j) * P:(2 * b + j + 1) * P], ident[:, :]), rq_at, bank_free[bk])
        qT_at = act.run(lambda e, bk=bk, b=b: e.activation(q_cols[:, 2 * b:2 * b + 2, :], bank(bk).rearrange("p (h n) -> p h n", h=2), ACT.Copy), got)
        bank_free[bk] = qT_at
    q_used = got

    scale = HD ** -0.5
    oh, ol = hcols_split(SEQ)
    p_cols = work[:, 0:2048].rearrange("p (i k n) -> p i k n", i=2, k=AT)
    stat = scalars(3 * 16)
    diag_free_at = [last_to_cols[0]] * 4
    e_free, pc_free = [None, None], [q_used, q_used]
    for h in range(HQ):
        for t in range(TT):
            i = h * TT + t
            bk = i % 2
            s_at = product(bank(bk), [(q_cols[:, h, t * P:(t + 1) * P], k_cols[:, h // (HQ // HKV), :])], qT_at, kT_at, bank_free[bk])
            m, s, r = (stat[:, j * 16 + i:j * 16 + i + 1] for j in range(3))
            tok = dve.run(lambda e, bk=bk, m=m: e.tensor_reduce(m, bank(bk), AX.X, ALU.max), s_at)
            tok = dve.run(lambda e, m=m: e.tensor_scalar(m, m, -scale, None, ALU.mult), tok)
            e_at = act.run(lambda e, bk=bk, i=i, m=m, s=s: e.activation(e_buf[i % 2], bank(bk), ACT.Exp, bias=m, scale=scale, accum_out=s),
                           tok, e_free[i % 2])
            bank_free[bk] = e_at
            tok = dve.run(lambda e, r=r, s=s: e.reciprocal(r, s), e_at)
            d_at = dve.run(lambda e, i=i, r=r: e.tensor_scalar(diag[:, i % 4, :], ident[:, :], r, None, ALU.mult), tok, diag_free_at[i % 4])
            pk = 2 + i % 2
            for k in range(AT):
                got = product(bank(pk)[:, k * P:(k + 1) * P], [(e_buf[i % 2][:, k * P:(k + 1) * P], diag[:, i % 4, :])], d_at, e_at, bank_free[pk])
            e_free[i % 2] = diag_free_at[i % 4] = got
            c_at = act.run(lambda e, pk=pk, h=h, t=t: e.activation(p_cols[:, h % 2, :, t * P:(t + 1) * P],
                           bank(pk).rearrange("p (k n) -> p k n", k=AT), ACT.Copy), got, pc_free[h % 2])
            bank_free[pk] = c_at
        ok = 4 + h % 2
        got = product(bank(ok)[:, 0:SEQ], [(kv_rows[:, k, (HKV + h // (HQ // HKV)) * P:(HKV + h // (HQ // HKV) + 1) * P], p_cols[:, h % 2, k, :])
                                           for k in range(AT)], c_at, qkv_at, bank_free[ok])
        pc_free[h % 2] = got
        a = act.run(lambda e, ok=ok, h=h: e.activation(oh[:, h, :], bank(ok)[:, 0:SEQ], ACT.Copy), got)
        o_at = dve.run(lambda e, ok=ok, h=h: e.tensor_tensor(ol[:, h, :], bank(ok)[:, 0:SEQ], oh[:, h, :].bitcast(F32), ALU.subtract), a)
        bank_free[ok] = o_at
    last_to_cols[0] = [last_to_cols[0], got]
    attn_done = got
    got = rows_product((oh, ol), KT, o_at)

    def add_y(got, gain_slot, g_at, x_at, base=10240):
        new = []
        for t in range(TT):
            n, m = tail(x_rows[:, t, :], t, y_banks(t), gains[:, gain_slot, :], work[:, base + t * D:base + (t + 1) * D], x_at[t], got, g_at)
            bank_free[2 * t] = bank_free[2 * t + 1] = m
            new.append(n)
        return new

    def mlp_half(x_at, scale, shift, gain_slot, g_at, *tokens):
        mh, ml = hcols_split(SEQ)
        cols_at = to_cols([(x_rows[:, t, :], x_at[t]) for t in range(TT)], True, scale, shift, mh, ml, full_scratch(SEQ), *tokens)
        got = mlp((mh, ml), cols_at, list(tokens))
        return add_y(got, gain_slot, g_at, x_at), got

    x_at = add_y(got, 0, g1_at[0], x_at)
    x_at, got = mlp_half(x_at, mod_cols[:, 1, 3, :, 0], mod_cols[:, 1, 2, :, 0], 1, g1_at[1], sh2_at, sc2_at, got, x_at[-1])

    onehot = work[0:BUCKETS, 8192:8192 + BIAS_W]
    rel = work[0:BUCKETS, 8768:8784]
    mask_row = work[0:16, 8832:8832 + BIAS_W]
    by_dist = work[0:16, 9408:9408 + BIAS_W]
    at_oh = load("onehot", onehot, A["k_onehot"], x_at)
    at_rel = load("rel", rel, A["rel_bias_2"], x_at)
    at_mask = load("mask8", mask_row, A["k_mask8"], x_at)
    table_dram = nc.dram_tensor("bias_tiles", [16, P, SEQ], F32)
    got_b = product(bank(4)[0:16, 0:BIAS_W], [(rel, onehot)], at_oh, at_rel, bank_free[4])
    b_at = dve.run(lambda e: e.scalar_tensor_tensor(by_dist, bank(4)[0:16, 0:BIAS_W], 8.0, mask_row, ALU.mult, ALU.add), got_b, at_mask)
    bank_free[4] = b_at
    stored = pool.dma(table_dram.ap(), view(by_dist, P - 1, [[-1, P], [1, SEQ]]), sem("table_stored"), 16, b_at)
    bias8 = hcols[:, 4096:8192].rearrange("p (h j) -> p h j", h=16)
    bias_at = load("bias8", bias8, table_dram.ap().rearrange("h p j -> p h j"), stored, x_at)
    bias_block = lambda h, t: bias8[:, h, P:SEQ] if t == 0 else bias8[:, h, :]

    blocks = lambda a, t: a[:, 0:P] if t == 0 else a[:, P:3 * P]
    g2 = []
    for i in range(4):
        g2.append((column_gain(f"n0_{i}", A["norm_g_2"][i, 0]), column_gain(f"n2_{i}", A["norm_g_2"][i, 2])))
    stats2 = scalars(2 * 32)

    def columns_product(w, cols, at, cols_at, n, evacuate, dup=None):
        bk = 4 + n % 4
        for j in range(2):
            pairs = []
            for k in range(KT):
                if dup is None:
                    lw = tuple(c[:, k, j * P:(j + 1) * P] for c in w)
                else:
                    o, dims = dup[j]
                    lw = tuple(view(c, k * 256 + o, dims) for c in w)
                pairs += three(lw, tuple(c[:, k, :] for c in cols))
            got = product(bank(bk)[:, j * SEQ:(j + 1) * SEQ], pairs, at, cols_at, bank_free[bk])
        bank_free[bk] = evacuate(bank(bk).rearrange("p (k n) -> p k n", k=2), got)
        return got, bank_free[bk]

    def copy_out(dst, *tokens):
        return lambda src, got: act.run(lambda e: e.activation(dst, src, ACT.Copy), got, *tokens)

    def softmax_part(h_bias, bk, e_out, cols, s_at, e_free, cq=None):
        tok = []
        for t in range(TT):
            m = stats2[:, cols + t:cols + t + 1]
            if cq is None:
                a = dve.run(lambda e, t=t, m=m: e.tensor_tensor_reduce(blocks(e_out, t), blocks(bank(bk), t), bias_block(h_bias, t),
                            1.0, -3e38, ALU.add, ALU.max, m), s_at, e_free, bias_at)
            else:
                a = dve.run(lambda e, t=t: e.scalar_tensor_tensor(blocks(e_out, t), blocks(bank(bk), t), cq[:, t:t + 1], mask8(t),
                            ALU.add, ALU.add), s_at, e_free)
                a = dve.run(lambda e, t=t, m=m: e.tensor_reduce(m, blocks(e_out, t), AX.X, ALU.max), a)
            tok.append(a)
        bank_free[bk] = tok[-1]
        ms = stats2[:, cols:cols + TT]
        n_at = dve.run(lambda e: e.tensor_scalar(ms, ms, -0.125, None, ALU.mult), tok)
        for t in range(TT):
            e_at = act.run(lambda e, t=t: e.activation(blocks(e_out, t), blocks(e_out, t), ACT.Exp, bias=stats2[:, cols + t:cols + t + 1],
                           scale=0.125, accum_out=stats2[:, 32 + cols + t:33 + cols + t]), n_at)
        return e_at

    mask_src = sb("mask_src", [P, SEQ])
    mask8 = lambda t: mask_src[:, P:SEQ] if t == 0 else mask_src[:, :]
    at_msrc = pool.run(lambda e: e.memset(mask_src[:, :], 0.0))
    mask_at = pool.run(lambda e: e.affine_select(out=mask_src[:, :], in_=mask_src[:, :], compare_op=ALU.is_ge, fill=NEG8, base=P,
                       pattern=[[-1, SEQ]], channel_multiplier=1), at_msrc)

    def diag_of(slot, scalar, *tokens):
        d_at = dve.run(lambda e: e.tensor_scalar(diag[:, slot, :], ident[:, :], scalar, None, ALU.mult), diag_free_at[slot], *tokens)
        return d_at

    def query_blocks(a):
        return [(a[:, 0:P], 0), (a[:, P:2 * P], 1), (a[:, 2 * P:3 * P], 1)]

    def differential(i, n_da, cols, cols_at, free):
        q_cols = work[:, 0:2048].rearrange("p (h n) -> p h n", h=KT)
        k_cols = work[:, 2048:4096].rearrange("p (h n) -> p h n", h=KT)
        v_rows = work[:, 4096:6144].rearrange("p (t n) -> p t n", t=TT)
        e_buf = [[work[:, 6144 + (2 * a + c) * 384:6528 + (2 * a + c) * 384] for c in range(2)] for a in range(2)]
        a_cols = [work[:, 7680 + a * 384:8064 + a * 384] for a in range(2)]
        o_rows = work[:, 8448:10496].rearrange("p (t n) -> p t n", t=TT)
        lam_init = 0.8 - 0.6 * math.exp(-0.3 * i)
        lam_in = work[:, 10496:10752]
        lam = scalars(4)
        at_l = load(f"lambda{i}", lam_in, A["da_lambda_2"][n_da:n_da + 1].rearrange("a b c -> a (b c)").broadcast_to([P, 4 * HALF]), free)
        tok = dve.run(lambda e: e.tensor_tensor(view(lam_in, 0, [[P, 2], [1, HALF]]), view(lam_in, 0, [[P, 2], [1, HALF]]),
                      view(lam_in, HALF, [[P, 2], [1, HALF]]), ALU.mult), at_l)
        tok = dve.run(lambda e: e.tensor_reduce(lam[:, 0:2], view(lam_in, 0, [[P, 2], [1, HALF]]), AX.X, ALU.add), tok)
        tok = act.run(lambda e: e.activation(lam[:, 0:2], lam[:, 0:2], ACT.Exp), tok)
        tok = dve.run(lambda e: e.tensor_tensor(lam[:, 2:3], lam[:, 1:2], lam[:, 0:1], ALU.subtract), tok)
        lam_at = dve.run(lambda e: e.tensor_scalar(lam[:, 2:3], lam[:, 2:3], -lam_init, None, ALU.add), tok)
        sub_g = scalars(1)
        at_sg = load(f"subln{i}", sub_g, A["da_subln_2"][n_da].rearrange("(p a) -> p a", a=1))
        sg_at = dve.run(lambda e: e.tensor_scalar(sub_g, sub_g, 1.0 - lam_init, None, ALU.mult), at_sg)

        for n in range(8):
            w, at = take()
            dst = (q_cols if n < 4 else k_cols)[:, 2 * (n % 4):2 * (n % 4) + 2, :]
            got, qk_at = columns_product(w, cols, at, cols_at, n, copy_out(dst, free))
            give_back(got)
        for ch in range(2):
            for half in range(2):
                w, at = take()
                for t in range(TT):
                    pairs = []
                    for j in range(4):
                        pairs += three(tuple(c[:, 4 * half + j, t * P:(t + 1) * P] for c in cols), tuple(c[:, j, :] for c in w))
                    bk = 2 * ch + t
                    for m, (lhs, rhs) in enumerate(pairs):
                        step = mm(bank(bk), lhs, rhs, half == 0 and m == 0, half == 1 and m == len(pairs) - 1)
                        if m == len(pairs) - 1:
                            got = pe.run(step)
                        else:
                            pe.quiet(step, at, cols_at, bank_free[bk] if half == 0 else None)
                    if half == 1:
                        bank_free[bk] = v_at = act.run(lambda e, t=t, ch=ch, bk=bk: e.activation(
                            v_rows[:, t, ch * 512:ch * 512 + 512], bank(bk), ACT.Copy), got, free)
                give_back(got)
        e_free, ac_free = [free, free], [free, free]
        for h in range(KT):
            e_at = [None, None]
            for c in range(2):
                bk = 4 + c
                part = slice(HALF * c, HALF * c + HALF)
                for t in range(TT):
                    s_at = product(blocks(bank(bk), t), [(q_cols[part, h, t * P:(t + 1) * P], k_cols[part, h, 0:(t + 1) * P])],
                                   qk_at, bank_free[bk])
                e_at[c] = softmax_part(2 * h + c, bk, e_buf[h % 2][c], (2 * h + c) * TT, s_at, e_free[h % 2])
            sums = stats2[:, 32 + 4 * h:36 + 4 * h]
            r = recips[:, 4 * h:4 * h + 4]
            tok = dve.run(lambda e, r=r, sums=sums: e.reciprocal(r, sums), e_at)
            tok = dve.run(lambda e, r=r: e.tensor_scalar(r[:, 2:4], r[:, 2:4], lam[:, 2:3], None, ALU.mult), tok, lam_at)
            d_at = [diag_of(j, r[:, j:j + 1], tok) for j in range(4)]
            bk = 6 + h % 2
            for b, ((e0, t), (e1, _)) in enumerate(zip(query_blocks(e_buf[h % 2][0]), query_blocks(e_buf[h % 2][1]))):
                got = product(bank(bk)[:, b * P:(b + 1) * P], [(e0, diag[:, t, :]), (e1, diag[:, 2 + t, :])], d_at, bank_free[bk])
            e_free[h % 2] = got
            for j in range(4):
                diag_free_at[j] = got
            a_at = act.run(lambda e, h=h, bk=bk: e.activation(a_cols[h % 2], bank(bk)[:, 0:3 * P], ACT.Copy), got, ac_free[h % 2])
            bank_free[bk] = a_at
            for t in range(TT):
                ob = 2 * t + h // 4
                ks = [0] if t == 0 else [0, 1]
                got = product(bank(ob)[:, (h % 4) * P:(h % 4 + 1) * P],
                              [(a_cols[h % 2][:, (t + k) * P:(t + k + 1) * P], v_rows[:, k, h * P:(h + 1) * P]) for k in ks],
                              a_at, v_at, bank_free[ob])
            ac_free[h % 2] = got
        oss = scalars(16)
        sq = work[:, 6144:8192].rearrange("p (t n) -> p t n", t=TT)
        tok = []
        for t in range(TT):
            tok.append(act.run(lambda e, t=t: e.activation(sq[:, t, :], y_banks(t), ACT.Square), got))
        tok = dve.run(lambda e: e.tensor_reduce(oss, view(sq, 0, [[P, 16], [1, P]]), AX.X, ALU.add), tok)
        r_at = inverse_root(oss, P, 16, tok)
        for t in range(TT):
            o_at = dve.run(lambda e, t=t: e.tensor_tensor(view(o_rows, t * D, [[P, 8], [1, P]]), view(bank(2 * t), 0, [[P, 8], [1, P]]),
                           view(oss, 8 * t, [[1, 8], [0, P]]), ALU.mult), r_at, got, free)
            bank_free[2 * t] = bank_free[2 * t + 1] = o_at
        oh, ol = hcols_split(SEQ)
        for b in range(KT // 2):
            bk = 4 + b % 4
            for j in range(2):
                for t in range(TT):
                    got = pe.run(lambda e, bk=bk, j=j, t=t, b=b: e.transpose(bank(bk)[:, (2 * j + t) * P:(2 * j + t + 1) * P],
                                 o_rows[:, t, (2 * b + j) * P:(2 * b + j + 1) * P], ident[:, :]), o_at, bank_free[bk])
            src = bank(bk).rearrange("p (k n) -> p k n", k=2)
            h_, l_ = oh[:, 2 * b:2 * b + 2, :], ol[:, 2 * b:2 * b + 2, :]
            a = act.run(lambda e, h_=h_, src=src: e.activation(h_, src, ACT.Copy, scale=sub_g), got, sg_at)
            l_at = dve.run(lambda e, h_=h_, l_=l_, src=src: e.scalar_tensor_tensor(l_, src, sub_g, h_.bitcast(F32), ALU.mult, ALU.subtract), a)
            bank_free[bk] = l_at
        return rows_product((oh, ol), KT, l_at)

    recips = scalars(32)

    def forgetting(i, cols, cols_at, free):
        q_cols = work[:, 0:2048].rearrange("p (h n) -> p h n", h=KT)
        k_cols = work[:, 2048:4096].rearrange("p (h n) -> p h n", h=KT)
        v_pad = work[:, 4096:7168].rearrange("p (t g n) -> p t g n", t=TT, g=8)
        e_buf = [work[:, 7168 + a * 384:7552 + a * 384] for a in range(2)]
        p_cols = [work[:, 7936 + a * 384:8320 + a * 384] for a in range(4)]
        z_at = pool.run(lambda e: e.memset(v_pad[:, :, :, HALF:P], 0.0), free)
        wf = work[:, 9472:9600].rearrange("p (k n) -> p k n", k=KT)
        wf_h = wf_hi[:, :].rearrange("p (k n) -> p k n", k=KT)
        at_wf = load("w_f", wf, A["fox_w_in_2"][0][:, 3 * D:3 * D + 16].rearrange("(k p) n -> p k n", p=P), free)
        cum = work[:, 9600:10112].rearrange("p (t n) -> p t n", t=TT)
        at_cum = load("cum", cum, A["k_cumsum"], free)
        b_f = work[:, 10112:10128]
        at_bf = load("b_f", b_f, A["fox_b_f_2"][0:1, :].broadcast_to([P, 16]), free)
        z = work[:, 10128:10160].rearrange("p (t n) -> p t n", t=TT)
        az = work[:, 10160:10192].rearrange("p (t n) -> p t n", t=TT)
        c8 = work[:, 10192:10224].rearrange("p (h t) -> p h t", t=TT)
        ck = [work[o:o + 16, 10240:10496] for o in (0, HALF)]
        tok = dve.run(lambda e: e.tensor_copy(wf_h, wf), at_wf)
        wf_l = twin(wf)
        wf_at = dve.run(lambda e: e.tensor_tensor(wf_l, wf, wf_h.bitcast(F32), ALU.subtract), tok)
        for t in range(TT):
            pairs = []
            for k in range(KT):
                pairs += three(tuple(c[:, k, t * P:(t + 1) * P] for c in cols), (wf_h[:, k, :], wf_l[:, k, :]))
            got = product(bank(0)[:, t * 16:(t + 1) * 16], pairs, wf_at, cols_at, bank_free[0])
        tok = dve.run(lambda e: e.tensor_tensor(z, bank(0)[:, 0:32].rearrange("p (t n) -> p t n", t=TT),
                      view(b_f, 0, [[0, TT], [1, 16]]), ALU.add), got, at_bf)
        bank_free[0] = tok
        tok = act.run(lambda e: e.activation(az, z, ACT.Abs), tok)
        tok = act.run(lambda e: e.activation(az, az, ACT.Exp, scale=-1.0), tok)
        tok = act.run(lambda e: e.activation(az, az, ACT.Ln, bias=1.0), tok)
        lf_at = dve.run(lambda e: e.scalar_tensor_tensor(z, z, 0.0, az, ALU.min, ALU.subtract), tok)
        got = product(bank(1)[0:16, 0:SEQ], [(z[:, s, :], cum[:, s, :]) for s in range(TT)], lf_at, at_cum, bank_free[1])
        for t in range(TT):
            got = product(bank(1)[:, SEQ + t * 16:SEQ + (t + 1) * 16], [(cum[:, s, t * P:(t + 1) * P], z[:, s, :]) for s in range(TT)])
        for k in ck:
            dve.run(lambda e, k=k: e.tensor_scalar(k, bank(1)[0:16, 0:SEQ], -8.0, None, ALU.mult), got)
        c_at = dve.run(lambda e: e.tensor_scalar(view(c8, 0, [[1, TT], [TT, 16]]), view(bank(1), SEQ, [[16, TT], [1, 16]]), 8.0, None, ALU.mult), got)
        bank_free[1] = c_at

        for n in range(8):
            w, at = take()
            dst = (q_cols if n < 4 else k_cols)[:, 2 * (n % 4):2 * (n % 4) + 2, :]
            got, qk_at = columns_product(w, cols, at, cols_at, n, copy_out(dst, free))
            give_back(got)
        for ch in range(2):
            for half in range(2):
                w, at = take()
                for t in range(TT):
                    pairs = []
                    for j in range(4):
                        pairs += three(tuple(c[:, 4 * half + j, t * P:(t + 1) * P] for c in cols), tuple(c[:, j, :] for c in w))
                    bk = 2 * ch + t
                    for m, (lhs, rhs) in enumerate(pairs):
                        step = mm(bank(bk), lhs, rhs, half == 0 and m == 0, half == 1 and m == len(pairs) - 1)
                        if m == len(pairs) - 1:
                            got = pe.run(step)
                        else:
                            pe.quiet(step, at, cols_at, bank_free[bk] if half == 0 else None)
                    if half == 1:
                        dst = view(v_pad, (t * 8 + ch * 4) * 192, [[192, 4], [P, 2], [1, HALF]])
                        bank_free[bk] = v_at = act.run(lambda e, dst=dst, bk=bk: e.activation(
                            dst, view(bank(bk), 0, [[P, 4], [HALF, 2], [1, HALF]]), ACT.Copy), got, free)
                give_back(got)
        oh, ol = hcols_split(SEQ)
        e_free, pc_free = [free, free], [free] * 4
        for h in range(16):
            part = slice(HALF * (h % 2), HALF * (h % 2) + HALF)
            bk = h % 2
            for t in range(TT):
                ks = slice(0, (t + 1) * P)
                s_at = product(blocks(bank(bk), t), [(q_cols[part, h // 2, t * P:(t + 1) * P], k_cols[part, h // 2, ks]),
                                                     (view(ident[HALF * (h % 2):HALF * (h % 2) + 16, :], HALF * (h % 2) + h, [[0, P]]), ck[h % 2][:, ks])], qk_at, c_at, bank_free[bk])
            e_at = softmax_part(h, bk, e_buf[h % 2], h * TT, s_at, e_free[h % 2], cq=c8[:, h, :])
            r = recips[:, 2 * h:2 * h + 2]
            tok = dve.run(lambda e, r=r, h=h: e.reciprocal(r, stats2[:, 32 + 2 * h:34 + 2 * h]), e_at)
            d_at = [diag_of(2 * (h % 2) + t, r[:, t:t + 1], tok) for t in range(TT)]
            pk = 2 + h % 2
            for b, (src, t) in enumerate(query_blocks(e_buf[h % 2])):
                got = product(bank(pk)[:, b * P:(b + 1) * P], [(src, diag[:, 2 * (h % 2) + t, :])], d_at, e_at, bank_free[pk])
            e_free[h % 2] = diag_free_at[2 * (h % 2)] = diag_free_at[2 * (h % 2) + 1] = got
            pc = p_cols[h % 4]
            a_at = act.run(lambda e, pc=pc, pk=pk: e.activation(pc, bank(pk)[:, 0:3 * P], ACT.Copy), got, pc_free[h % 4])
            bank_free[pk] = a_at
            if h % 2:
                ob = 4 + (h // 2) % 2
                steps = []
                for par in range(2):
                    pc = p_cols[(h - 1 + par) % 4]
                    lhs = lambda t: v_pad[:, t, h // 2, par * HALF:par * HALF + P]
                    steps.append(mm(bank(ob)[:, 0:SEQ], lhs(0), pc[:, 0:SEQ], par == 0, False))
                    steps.append(mm(bank(ob)[:, P:SEQ], lhs(1), pc[:, SEQ:3 * P], False, par == 1))
                for s in steps[:-1]:
                    pe.quiet(s, a_at, v_at, z_at, bank_free[ob])
                got = pe.run(steps[-1])
                pc_free[h % 4] = pc_free[(h - 1) % 4] = got
                a = act.run(lambda e, ob=ob, h=h: e.activation(oh[:, h // 2, :], bank(ob)[:, 0:SEQ], ACT.Copy), got)
                o_at = dve.run(lambda e, ob=ob, h=h: e.tensor_tensor(ol[:, h // 2, :], bank(ob)[:, 0:SEQ], oh[:, h // 2, :].bitcast(F32), ALU.subtract), a)
                bank_free[ob] = o_at
        return rows_product((oh, ol), KT, o_at)

    def sparse(i, cols, cols_at, free):
        G, R = 4, 4
        q_cols = work[:, 0:2048].rearrange("p (h n) -> p h n", h=KT)
        k_cols = work[:, 2048:4096].rearrange("p (b s m n) -> p b s m n", b=2, s=2, m=2)
        v_pad = work[:, 4096:7168].rearrange("p (b t g n) -> p b t g n", b=2, t=TT, g=G)
        shifted = [work[:, 7168 + b * D:8192 + b * D].rearrange("p (g n) -> p g n", g=G) for b in range(2)]
        s_cmp = work[:, 7168:7680]
        p_cmp = work[:, 7680:8192]
        e_buf = [[work[:, 7168 + (2 * a + b) * 384:7552 + (2 * a + b) * 384] for b in range(2)] for a in range(2)]
        p_cols = [[work[:, 8704 + (2 * a + b) * 384:9088 + (2 * a + b) * 384] for b in range(2)] for a in range(2)]
        pc_cols = work[:, 10240:10752].rearrange("p (m n) -> p m n", m=2)
        v_block = work[:, 10752:11776].rearrange("p (m h d) -> p m h d", m=2, h=8)
        natural = work[:, 9216:9728].rearrange("p (m n) -> p m n", m=2)
        swap = work[:, 9728:9856]
        w2k = work[:, 9856:10112].rearrange("p (k n) -> p k n", k=2)
        at_swap = load("swap", swap, A["k_swap"], free)
        misc = work[:, 11776:12288]
        blk_h = ctx_rows[:, 0, :].rearrange("p (k n) -> p k n", k=16)
        blk_l = ctx_rows[:, 1, :].rearrange("p (k n) -> p k n", k=16)
        w_g, g_rows = misc[:, 0:384].rearrange("p (k n) -> p k n", k=KT), misc[:, 384:480]
        pe_cols = scalars(16)
        w2 = [scalars(128).rearrange("p (k n) -> p k n", k=2) for _ in range(2)]
        z_at = [pool.run(lambda e: e.memset(v_pad[:, :, :, :, :], 0.0), free)]

        at_wg = load("w_g", w_g, A["nsa_w_in_2"][0][:, 2560:2608].rearrange("(k p) n -> p k n", p=P), free)
        wg_h = wf_hi3[:, :].rearrange("p (k n) -> p k n", k=KT)
        tok = dve.run(lambda e: e.tensor_copy(wg_h, w_g), at_wg)
        wg_l = twin(w_g)
        wg_at = dve.run(lambda e: e.tensor_tensor(wg_l, w_g, wg_h.bitcast(F32), ALU.subtract), tok)
        for t in range(TT):
            pairs = []
            for k in range(KT):
                pairs += three(tuple(c[:, k, t * P:(t + 1) * P] for c in cols), (wg_h[:, k, :], wg_l[:, k, :]))
            got = product(bank(0)[:, t * 48:(t + 1) * 48], pairs, wg_at, cols_at, bank_free[0])
        tok = act.run(lambda e: e.activation(g_rows, bank(0)[:, 0:96], ACT.Tanh, scale=0.5), got, free)
        bank_free[0] = tok
        gate_at = dve.run(lambda e: e.tensor_scalar(g_rows, g_rows, 1.0, 0.5, ALU.add, ALU.mult), tok)
        gate = lambda t, h, b: g_rows[:, t * 48 + h * 3 + b:t * 48 + h * 3 + b + 1]

        for n in range(4):
            w, at = take()
            got, q_at = columns_product(w, cols, at, cols_at, n, copy_out(q_cols[:, 2 * n:2 * n + 2, :], free))
            give_back(got)

        kc_cols = misc[:, 0:64]
        hid = [ctx_hid[:, b * 128:(b + 1) * 128].rearrange("p (k n) -> p k n", k=2) for b in range(2)]
        blk_free = free
        blocks_at = []
        cmp_at = []
        n_free = free
        for b in range(2):
            w, at = take()
            got, n_at = columns_product(w, cols, at, cols_at, b, copy_out(natural, n_free))
            give_back(got)
            nb, sb_ = 4 + b, 6 + b
            got = product(bank(sb_), [(swap, natural.rearrange("p m n -> p (m n)"))], n_at, at_swap, bank_free[sb_])
            n_free = got
            for m in range(2):
                for par in range(2):
                    g = 2 * m + par
                    upper, lower = (nb, sb_) if par == 0 else (sb_, nb)
                    a0 = act.run(lambda e, g=g, b=b, m=m, upper=upper: e.activation(
                        shifted[b][0:HALF, g, :], bank(upper)[0:HALF, m * SEQ:(m + 1) * SEQ], ACT.Copy), got, free)
                    a1 = act.run(lambda e, g=g, b=b, m=m, lower=lower: e.activation(
                        shifted[b][HALF:P, g, 0:SEQ - 1], bank(lower)[HALF:P, m * SEQ + 1:(m + 1) * SEQ], ACT.Copy), got, free)
            bank_free[nb] = bank_free[sb_] = a1
            cmp_at.append(a1)
        for n, b in enumerate((0, 1)):
            w, at = take()
            got, n_at = columns_product(w, cols, at, cols_at, n, copy_out(k_cols[:, b, 0, :, :], free))
            give_back(got)
            got = product(bank(6 + n), [(swap, k_cols[:, b, 0, :, :].rearrange("p m n -> p (m n)"))], n_at, bank_free[6 + n])
            bank_free[6 + n] = k_at = act.run(lambda e, b=b, n=n: e.activation(
                k_cols[:, b, 1, :, :], bank(6 + n).rearrange("p (m n) -> p m n", m=2), ACT.Copy), got, free)
        for b in range(2):
            w, at = take()
            for t in range(TT):
                bk = 2 + t
                pairs = []
                for k in range(KT):
                    pairs += three(tuple(c[:, k, t * P:(t + 1) * P] for c in cols), tuple(c[:, k, :] for c in w))
                got = product(bank(bk)[:, 0:256], pairs, at, cols_at, bank_free[bk])
                dst = view(v_pad, (b * TT + t) * G * 192 + HALF, [[192, G], [1, HALF]])
                bank_free[bk] = v_at = act.run(lambda e, dst=dst, bk=bk: e.activation(dst, view(bank(bk), 0, [[HALF, G], [1, HALF]]), ACT.Copy), got, z_at)
            give_back(got)

        for b in range(2):
            at_pe = load(f"cmp_pe{b}", pe_cols, A["nsa_cmp_pe_2"][0][b].rearrange("(l a) d -> (a d) l", a=2), blk_free)
            at_w2 = load(f"cmp_w2{b}", w2[b], A["nsa_cmp_w2_2"][0][b].rearrange("(k p) n -> p k n", p=P))
            full = blk_l
            z0 = pool.run(lambda e: e.memset(ctx_rows[:, 1, :], 0.0), blk_free)
            for g in range(G):
                f_at = dve.run(lambda e, g=g, b=b: e.tensor_tensor(view(full, g * NC, [[64, 16], [1, N_CMP]]),
                               view(shifted[b], g * SEQ, [[2, 16], [CMP_STRIDE, N_CMP]]), view(pe_cols, 0, [[1, 16], [0, N_CMP]]), ALU.add),
                               z0, at_pe, cmp_at[b])
            h_at = act.run(lambda e: e.activation(twin(blk_h), full, ACT.Copy), f_at)
            l_at = dve.run(lambda e: e.tensor_tensor(twin(blk_l), full, twin(blk_h).bitcast(F32), ALU.subtract), h_at)
            for c in range(2):
                w, at = take()
                for j in range(2):
                    for k in range(8):
                        for m, (lhs, rhs) in enumerate(three(tuple(x[:, k, j * P:(j + 1) * P] for x in w),
                                                            (twin(blk_h)[:, 8 * c + k, :], twin(blk_l)[:, 8 * c + k, :]))):
                            last = k == 7 and m == 2
                            step = mm(bank(j)[:, 0:64], lhs, rhs, c == 0 and k == 0 and m == 0, c == 1 and last)
                            if last:
                                got = pe.run(step)
                            else:
                                pe.quiet(step, at, l_at, bank_free[j])
                give_back(got)
            blk_free = got
            u, v = gelu_tmp[:, 0:128].rearrange("p (k n) -> p k n", k=2), gelu_tmp[:, 128:256].rearrange("p (k n) -> p k n", k=2)
            for j in range(2):
                tok = dve.run(lambda e, j=j: e.tensor_copy(u[:, j, :], bank(j)[:, 0:64]), got, blocks_at)
            bank_free[0] = bank_free[1] = tok
            tok = dve.run(lambda e: e.tensor_tensor(v, u, u, ALU.mult), tok)
            tok = dve.run(lambda e: e.tensor_tensor(v, v, u, ALU.mult), tok)
            tok = dve.run(lambda e: e.scalar_tensor_tensor(v, v, 0.044715, u, ALU.mult, ALU.add), tok)
            tok = act.run(lambda e: e.activation(v, v, ACT.Tanh, scale=math.sqrt(2 / math.pi)), tok)
            tok = dve.run(lambda e: e.scalar_tensor_tensor(v, v, 1.0, u, ALU.add, ALU.mult), tok)
            hid_at = dve.run(lambda e, b=b: e.tensor_scalar(hid[b], v, 0.5, None, ALU.mult), tok)
            if b == 0:
                at_w2k = [load(f"w2k{c}", w2k[:, :, c * HALF:(c + 1) * HALF], A["nsa_cmp_w2_2"][0][0].rearrange("(k p) n -> p k n", p=P), free)
                          for c in range(2)]
                got = product(bank(2)[:, 0:64], [(w2k[:, k, :], hid[0][:, k, :]) for k in range(2)], hid_at, at_w2k, bank_free[2])
                kc_at = act.run(lambda e: e.activation(kc_cols, bank(2)[:, 0:64], ACT.Copy), got, gate_at)
                bank_free[2] = kc_at
            else:
                at_hr = load("headrow", head_row[:, :], A["k_headrow"])
                spread_hid = blk_h.rearrange("p k n -> p (k n)")[:, 0:512].rearrange("p (m k n) -> p m k n", m=2, k=2)
                for m in range(2):
                    for k in range(2):
                        for gg in range(2):
                            sp_at = dve.run(lambda e, m=m, k=k, gg=gg: e.tensor_copy(
                                view(spread_hid, (2 * m + k) * P + gg * 64, [[NC, R], [1, NC]]),
                                view(hid[1], k * HALF + (2 * m + gg) * NC, [[0, R], [1, NC]])), hid_at, blk_free)
                for m in range(2):
                    got = product(bank(2)[:, m * HALF:(m + 1) * HALF],
                                  [(spread_hid[:, m, k, :], w2[1][:, k, :]) for k in range(2)], sp_at, at_w2, bank_free[2])
                for m in range(2):
                    vb_at = dve.run(lambda e, m=m: e.tensor_tensor(v_block[:, m, :, :], view(bank(2), m * HALF, [[0, 8], [1, HALF]]),
                                    view(head_row[:, :], 0, [[1, 8], [0, HALF]]), ALU.mult), got, at_hr, free)
                bank_free[2] = vb_at
            blocks_at = [hid_at, got]

        bc = cmp_bias[:, :]
        b0_at = pool.run(lambda e: e.memset(bc, NEG8))
        at_bc = []
        for t, first in ((1, CMP_LEN - 1), (0, P + CMP_LEN - 1)):
            n = len(range(first, SEQ, CMP_STRIDE))
            at_bc.append(dve.run(lambda e, t=t, first=first, n=n: e.tensor_copy(
                view(bc, t * 256, [[NC, 16], [1, n]]), view(bias8, first, [[SEQ, 16], [CMP_STRIDE, n]])), b0_at, bias_at))
        at_valid = load("valid", valid[:, :], A["k_valid"].rearrange("p t a -> p (t a)"))
        for t in range(TT):
            for h in range(16):
                g = h // R
                part = slice(HALF * (h % 2), HALF * (h % 2) + HALF)
                bk = 3 - h % 2
                s_at = product(bank(bk)[:, (t * 8 + h // 2) * NC:(t * 8 + h // 2 + 1) * NC],
                               [(q_cols[part, h // 2, t * P:(t + 1) * P], kc_cols[part, g * NC:(g + 1) * NC])], q_at, kc_at, bank_free[bk])
        by_head = lambda a: view(a, 0, [[NC, 32], [1, NC]])
        m32 = stats2[:, 0:32]
        s32 = stats2[:, 32:64]
        spread = lambda a: view(a, 0, [[1, 32], [0, NC]])
        for par in range(2):
            heads = lambda a, par=par: view(a, par * NC, [[256, TT], [2 * NC, 8], [1, NC]])
            tok = dve.run(lambda e, heads=heads, par=par: e.tensor_tensor(heads(s_cmp), view(bank(3 - par), 0, [[P, TT], [NC, 8], [1, NC]]),
                          heads(bc), ALU.add), s_at, at_bc, f_at)
            bank_free[3 - par] = tok
        tok = dve.run(lambda e: e.tensor_reduce(m32, by_head(s_cmp), AX.X, ALU.max), tok)
        tok = dve.run(lambda e: e.tensor_tensor(by_head(s_cmp), by_head(s_cmp), spread(m32), ALU.subtract), tok)
        tok = act.run(lambda e: e.activation(p_cmp, s_cmp, ACT.Exp, scale=0.125), tok)
        tok = dve.run(lambda e: e.tensor_reduce(s32, by_head(p_cmp), AX.X, ALU.add), tok)
        tok = dve.run(lambda e: e.reciprocal(s32, s32), tok)
        for t in range(TT):
            tok = dve.run(lambda e, t=t: e.scalar_tensor_tensor(s32[:, 16 * t:16 * t + 16], s32[:, 16 * t:16 * t + 16], valid[:, t:t + 1],
                          view(g_rows, t * 48, [[3, 16]]), ALU.mult, ALU.mult), tok, at_valid, gate_at)
        pn_at = dve.run(lambda e: e.tensor_tensor(by_head(p_cmp), by_head(p_cmp), spread(s32), ALU.mult), tok)
        for m in range(2):
            for t in range(TT):
                got = pe.run(lambda e, m=m, t=t: e.transpose(bank(2)[:, m * SEQ + t * P:m * SEQ + (t + 1) * P],
                             p_cmp[:, t * 256 + m * P:t * 256 + (m + 1) * P], ident[:, :]), pn_at, bank_free[2])
        pc_at = act.run(lambda e: e.activation(pc_cols, bank(2).rearrange("p (m n) -> p m n", m=2), ACT.Copy), got, free)
        bank_free[2] = pc_at

        oh, ol = hcols_split(SEQ)
        e_free, pc_free = [pn_at, pn_at], [free, free]
        for h in range(16):
            g = h // R
            part = slice(HALF * (h % 2), HALF * (h % 2) + HALF)
            swapped = (h + g) % 2
            a_at = []
            for b in range(2):
                bk = b
                for t in range(TT):
                    s_at = product(blocks(bank(bk), t), [(q_cols[part, h // 2, t * P:(t + 1) * P], k_cols[part, b, swapped, g // 2, 0:(t + 1) * P])],
                                   q_at, k_at, bank_free[bk])
                e_out = e_buf[h % 2][b]
                e_at = softmax_part(h, bk, e_out, 4 * (h % 4) + 2 * b, s_at, e_free[h % 2])
                c0 = 4 * (h % 4) + 2 * b
                rr = recips[:, c0:c0 + 2]
                tok = dve.run(lambda e, rr=rr, c0=c0: e.reciprocal(rr, stats2[:, 32 + c0:34 + c0]), e_at)
                gates = view(g_rows, h * 3 + 1 + b, [[48, TT]])
                tok = dve.run(lambda e, rr=rr, gates=gates: e.tensor_tensor(rr, rr, gates, ALU.mult), tok)
                d_at = [diag_of(2 * b + t, rr[:, t:t + 1], tok) for t in range(TT)]
                pk = 2 + b
                for n, (src, t) in enumerate(query_blocks(e_out)):
                    got = product(bank(pk)[:, n * P:(n + 1) * P], [(src, diag[:, 2 * b + t, :])], d_at, e_at, bank_free[pk])
                diag_free_at[2 * b] = diag_free_at[2 * b + 1] = got
                a = act.run(lambda e, h=h, b=b, pk=pk: e.activation(p_cols[h % 2][b], bank(pk)[:, 0:3 * P], ACT.Copy), got, pc_free[h % 2])
                bank_free[pk] = a
                a_at.append(a)
            e_free[h % 2] = got
            if h % 2:
                j = h // 2
                ob = 4 + j % 2
                steps = [mm(bank(ob)[:, 0:SEQ], v_block[:, j // 4, 2 * (j % 4):2 * (j % 4) + 2, :].rearrange("p h d -> p (h d)"),
                            pc_cols[:, j // 4, :], True, False)]
                for par in range(2):
                    for b in range(2):
                        pc = p_cols[par][b]
                        lhs = lambda t: v_pad[:, b, t, g, HALF - par * HALF:HALF - par * HALF + P]
                        steps.append(mm(bank(ob)[:, 0:SEQ], lhs(0), pc[:, 0:SEQ], False, False))
                        steps.append(mm(bank(ob)[:, P:SEQ], lhs(1), pc[:, SEQ:3 * P], False, par == 1 and b == 1))
                for s in steps[:-1]:
                    pe.quiet(s, a_at, v_at, vb_at, pc_at, bank_free[ob])
                got = pe.run(steps[-1])
                pc_free = [got, got]
                a = act.run(lambda e, ob=ob, j=j: e.activation(oh[:, j, :], bank(ob)[:, 0:SEQ], ACT.Copy), got)
                o_at = dve.run(lambda e, ob=ob, j=j: e.tensor_tensor(ol[:, j, :], bank(ob)[:, 0:SEQ], oh[:, j, :].bitcast(F32), ALU.subtract), a)
                bank_free[ob] = o_at
        return rows_product((oh, ol), KT, o_at)

    wf_hi = sb("wf_hi", [P, 128], F32R)
    wf_hi3 = sb("wg_hi", [P, 384], F32R)
    head_row = sb("head_row", [P, 8])
    valid = sb("valid", [P, TT])
    cmp_bias = sb("cmp_bias", [P, 512])
    gelu_tmp = sb("gelu_tmp", [P, 256])
    ctx_hid = sb("ctx_hid", [P, 256])

    p_raw = gelu_tmp
    for i in range(4):
        (g0, g0_c), (g_2, g2_c) = g2[i]
        ra = row_gain(f"n1_{i}", 0, A["norm_g_2"][i, 1], x_at)
        rb = row_gain(f"n3_{i}", 1, A["norm_g_2"][i, 3], x_at)
        free = [x_at[-1], x_at[0], got, stored]
        mh, ml = hcols_split(SEQ)
        cols_at = to_cols([(x_rows[:, t, :], x_at[t]) for t in range(TT)], True, g0, None, mh, ml, full_scratch(SEQ), g0_c, free)
        free = free + [cols_at]
        if i % 3 == 0:
            got = differential(i, i // 3, (mh, ml), cols_at, free)
        elif i == 1:
            got = sparse(i, (mh, ml), cols_at, free)
        else:
            got = forgetting(i, (mh, ml), cols_at, free)
        x_at = add_y(got, 0, ra, x_at)
        x_at, got = mlp_half(x_at, g_2, None, 1, rb, g2_c, got, x_at[-1])

        p_rows = work[:, 8192:8704].rearrange("p (t n) -> p t n", t=TT)
        pl = lambda o: twin(work[:, 8704 + o:9216 + o].rearrange("p (k n) -> p k n", k=2))
        ph, plo = pl(0), pl(512)
        at_p = load(f"p{i}", p_rows, A["p_2"][i, 0].rearrange("(t p) n -> p t n", p=P), x_at, got)
        cols_at = to_cols([(x_rows[:, t, :], x_at[t]) for t in range(TT)], False, None, None, mh, ml, None, got)
        for k in range(2):
            for t in range(TT):
                tp = pe.run(lambda e, k=k, t=t: e.transpose(bank(4)[:, (2 * k + t) * P:(2 * k + t + 1) * P], p_rows[:, t, k * P:(k + 1) * P], ident[:, :]),
                            at_p, bank_free[4])
        src = bank(4).rearrange("p (k n) -> p k n", k=2)
        a = act.run(lambda e, src=src: e.activation(ph, src, ACT.Copy), tp, x_at)
        pl_at = dve.run(lambda e, src=src: e.tensor_tensor(plo, src, ph.bitcast(F32), ALU.subtract), a)
        bank_free[4] = pl_at
        got = rows_product((mh, ml), KT, cols_at)
        got2 = rows_product((ph, plo), 2, pl_at, first_bank=4)
        new = []
        for t in range(TT):
            th = work[:, t * D:(t + 1) * D]
            a = act.run(lambda e, t=t, th=th: e.activation(th, y_banks(t), ACT.Tanh, scale=0.5), got, x_at)
            bank_free[2 * t] = bank_free[2 * t + 1] = a
            m = dve.run(lambda e, t=t, th=th: e.scalar_tensor_tensor(th, th, 1.0, y_banks(2 + t), ALU.add, ALU.mult), a, got2)
            bank_free[4 + 2 * t] = bank_free[5 + 2 * t] = m
            new.append(dve.run(lambda e, t=t, th=th: e.scalar_tensor_tensor(x_rows[:, t, :], th, 0.5, x_rows[:, t, :], ALU.mult, ALU.add), m, x_at[t]))
        x_at = new
        got = got2
    assert len(used) == len(plan), (len(used), len(plan))

    out_at = sp.dma(out.rearrange("a (t p) d -> p (a t) d", p=P), x_rows[:, :, :], sem("out_stored"), 16, x_at)
    sp.wait(out_at)

    block = ctx.enter_context(nc.Block())
    for decorate, lane in ((block.sync, sp), (block.gpsimd, pool), (block.scalar, act), (block.vector, dve), (block.tensor, pe)):
        def program(e, lane=lane):
            for step in lane.steps:
                step(e)
        decorate(program)


_CONSTANTS = ("k_ident", "k_pool", "k_cos", "k_sin", "k_onehot", "k_mask8", "k_cumsum", "k_valid", "k_headrow", "k_swap", "k_modsel")
_INPUTS = (
    "x", "c", "ctx", "c_ctx", "w_ada", "b_ada", "g_mix_pre", "g_mix_post", "g_mlp_pre", "g_mlp_post", "w_pool",
    "pool_scale", "w_qkv", "g_q", "g_k", "w_o", "w_mlp_in", "w_mlp_out", "p_2", "rel_bias_2", "norm_g_2", "mlp_w1_2",
    "mlp_w2_2", "ple_w_2", "ple_gate_w_2", "da_w_in_2", "da_lambda_2", "da_subln_2", "da_w_out_2", "nsa_w_in_2",
    "nsa_cmp_pe_2", "nsa_cmp_w1_2", "nsa_cmp_w2_2", "nsa_w_out_2", "fox_w_in_2", "fox_b_f_2", "fox_w_out_2")


def kernel(**inputs):
    import concourse.bacc as bacc
    from concourse.bass_utils import run_bass_kernel_spmd

    nc = bacc.Bacc("TRN2", target_bir_lowering=False, num_devices=1)
    arrays, aps = {}, {}
    for name, value in [(n, inputs[n]) for n in _INPUTS] + list(shape_constants().items()):
        a = np.ascontiguousarray(value)
        arrays["in_" + name] = a
        aps[name] = nc.dram_tensor("in_" + name, a.shape, F32, kind="ExternalInput").ap()
    out = nc.dram_tensor("out", (1, SEQ, D), F32, kind="ExternalOutput").ap()
    build(nc, aps, out)
    result = run_bass_kernel_spmd(nc, [arrays], core_ids=[0])
    return result.results[0]["out"]
```

```python
import math
from contextlib import ExitStack

import numpy as np

import concourse.bass as bass
from concourse import mybir
from concourse.alu_op_type import AluOpType as ALU

F32 = mybir.dt.float32
F32R = mybir.dt.float32r
ACT = mybir.ActivationFunctionType
AX = mybir.AxisListType

P = 128
D = 1024
KT = D // P
SEQ = 256
TT = SEQ // P
GRID_W = 64
WINDOWS = (2, 4, 8, 16)
EPS = 1e-6
HALF = 64
BUCKETS = 32
NEG8 = -8e30
CMP_LEN, CMP_STRIDE = 32, 16
N_CMP = (SEQ - CMP_LEN) // CMP_STRIDE + 1
NC = 16
BIAS_W = 384
CHUNK = 2048
MOD_ORDER = (0, 1, 3, 4, 2, 5)
QUARTERS = 4
RAW_SLOTS = 5
HI_SLOTS = 4
AHEAD = 2


def shape_constants():
    t = np.arange(SEQ)
    pool = np.zeros((len(WINDOWS), SEQ, SEQ), np.float32)
    for g, w in enumerate(WINDOWS):
        lo, hi = np.clip(t - w // 2, 0, SEQ), np.clip(t + w - w // 2, 0, SEQ)
        for j in range(SEQ):
            pool[g, lo[j]:hi[j], j] = 1.0 / (hi[j] - lo[j])
            pool[g, j, j] -= 1.0
    half = P // 2
    freq = np.power(np.float32(10000.0), -np.arange(0, half, 2, dtype=np.float32) / half)
    row, col = (t // GRID_W).astype(np.float32), (t % GRID_W).astype(np.float32)
    ar, ac = row[:, None] * freq, col[:, None] * freq
    cos = np.concatenate([np.cos(ar), np.cos(ar), np.cos(ac), np.cos(ac)], 1)
    sin = np.concatenate([-np.sin(ar), np.sin(ar), -np.sin(ac), np.sin(ac)], 1)
    dist = 255 - np.arange(BIAS_W)
    n = np.maximum(dist, 0)
    exact = BUCKETS // 2
    nf = np.maximum(n, 1).astype(np.float32)
    large = exact + (np.log(nf / np.float32(exact)) / np.float32(math.log(128 / exact))
                     * np.float32(BUCKETS - exact)).astype(np.int32)
    bucket = np.where(n < exact, n, np.minimum(large, BUCKETS - 1))
    onehot = (np.arange(BUCKETS)[:, None] == bucket[None, :]) & (dist >= 0)[None, :]
    tiles = lambda a: np.ascontiguousarray(a.reshape(TT, P, -1).transpose(1, 0, 2), dtype=np.float32)
    return {
        "k_ident": np.eye(P, dtype=np.float32),
        "k_pool": np.ascontiguousarray(pool.reshape(4, TT, P, SEQ).transpose(2, 0, 1, 3).reshape(P, 8, SEQ)),
        "k_cos": tiles(cos), "k_sin": tiles(sin),
        "k_onehot": onehot.astype(np.float32),
        "k_mask8": np.broadcast_to(np.where(dist >= 0, 0.0, NEG8).astype(np.float32), (16, BIAS_W)).copy(),
        "k_cumsum": tiles((t[:, None] <= t[None, :]).astype(np.float32)),
        "k_valid": tiles((t >= CMP_LEN - 1).astype(np.float32)[:, None]),
        "k_headrow": (np.arange(P)[:, None] // NC == np.arange(8)[None, :]).astype(np.float32),
        "k_swap": np.eye(P, dtype=np.float32)[:, (np.arange(P) + HALF) % P].copy(),
        "k_modsel": np.array([[1, 0], [0, 1], [1, 0], [0, 1], [1, 1]], np.float32),
    }


class Lane:

    def __init__(self, semaphore):
        self.semaphore, self.count, self.steps, self.passed = semaphore, 0, [], {}

    def wait(self, *tokens):
        for token in tokens:
            if token is None:
                continue
            if isinstance(token, list):
                self.wait(*token)
                continue
            semaphore, value = token
            if self.passed.get(id(semaphore), 0) < value:
                self.passed[id(semaphore)] = value
                self.steps.append(lambda e, s=semaphore, v=value: e.wait_ge(s, v))

    def quiet(self, step, *tokens):
        self.wait(*tokens)
        self.steps.append(step)

    def run(self, step, *tokens):
        self.wait(*tokens)
        self.count += 1
        self.steps.append(lambda e: step(e).then_inc(self.semaphore, 1))
        return self.semaphore, self.count

    def dma(self, out, in_, semaphore, value, *tokens):
        self.wait(*tokens)
        self.steps.append(lambda e: e.dma_start(out, in_, allow_slow_non_contiguous=True).then_inc(semaphore, 16))
        return semaphore, value


def view(base, offset, dims):
    return bass.AP(base.tensor, base.offset + offset, [list(base.ap[0])] + [list(d) for d in dims])


def build(nc, A, out):
    with ExitStack() as ctx:
        _build(nc, A, out, ctx)


def _build(nc, A, out, ctx):
    sb = lambda name, shape, dt=F32: ctx.enter_context(nc.sbuf_tensor(name, shape, dt))
    sem = lambda name: ctx.enter_context(nc.semaphore(name))

    pe, dve, act, pool, sp = (Lane(sem(f"{n}_done")) for n in ("tensor", "vector", "scalar", "gpsimd", "sync"))

    twins = {}

    def with_twin(name, shape):
        with nc.sbuf_tensor(name, shape, F32) as full:
            pass
        parts = sb(name + "_split", shape, F32R)
        twins[name], twins[name + "_split"] = parts, full
        return full, parts

    def twin(ap):
        return bass.AP(twins[ap.tensor.name], ap.offset, [list(d) for d in ap.ap])

    raw = [with_twin(f"raw{i}", [P, CHUNK])[0] for i in range(RAW_SLOTS)]
    hi = [sb(f"hi{i}", [P, CHUNK], F32R) for i in range(HI_SLOTS)]
    x_rows = sb("x_rows", [P, TT, D])
    ctx_rows, _ = with_twin("ctx_rows", [P, TT, D])
    hcols, _ = with_twin("hcols", [P, 8192])
    work, _ = with_twin("work", [P, 12288])
    gains = sb("gains", [P, 2, D])
    mods = sb("mods", [5, 2, D])
    ident = sb("ident", [P, P])
    small = sb("small", [P, 1024])
    psum = ctx.enter_context(nc.psum_tensor("psum", [P, 8, 512], F32))
    bank_free = [None] * 8
    bank = lambda i: psum[:, i, :]

    cursor = [0]

    def scalars(n):
        cursor[0] += n
        assert cursor[0] <= 1024
        return small[:, cursor[0] - n:cursor[0]]

    def load(name, out_, in_, *tokens):
        return pool.dma(out_, in_, sem("at_" + name), 16, *tokens)

    plan = []

    def cols_first(w, c0, width=256):
        return w[:, c0:c0 + width].rearrange("(k p) n -> p k n", p=P)

    def plan_stationary(w, c0, c1):
        for c in range(c0, c1, 256):
            plan.append(cols_first(w, c, 256))

    def plan_half_k(w, c0, c1):
        for c in range(c0, c1, 512):
            for k in range(2):
                plan.append(w[k * 512:(k + 1) * 512, c:c + 512].rearrange("(k p) n -> p k n", p=P))

    def plan_rows(w):
        for k in range(0, w.shape[0], 256):
            plan.append(w[k:k + 256, :].rearrange("(k p) n -> p k n", p=P))

    def plan_modulation(w, m):
        plan_half_k(w, m * D, m * D + D)

    def plan_mlp0(w1, w2, w_mod):
        halves = [m * D + ch * 512 for m in MOD_ORDER for ch in range(2)]
        for q in range(QUARTERS):
            for n in range(4):
                plan_stationary(w1, q * D + n * 256, q * D + n * 256 + 256)
                if n < 3:
                    c = halves.pop(0)
                    plan_half_k(w_mod, c, c + 512)
            for ch in range(2):
                for k in range(2):
                    r = q * D + k * 512
                    plan.append(w2[r:r + 512, ch * 512:ch * 512 + 512].rearrange("(k p) n -> p k n", p=P))

    def plan_mlp(w1, w2):
        for q in range(QUARTERS + 1):
            if q < QUARTERS:
                plan_stationary(w1, q * D, q * D + D)
            if q > 0:
                plan_rows(w2[(q - 1) * D:q * D, :])

    for m in range(4):
        plan_modulation(A["w_ada"][0], m)
    plan.append(A["w_pool"][0].rearrange("g (k p) n -> p (g k) n", p=P))
    for m in range(4, 6):
        plan_modulation(A["w_ada"][0], m)
    plan_mlp0(A["w_mlp_in"][0], A["w_mlp_out"][0], A["w_ada"][1])
    plan_half_k(A["w_qkv"][0], 1024, 1536)
    plan_half_k(A["w_qkv"][0], 0, 1024)
    plan_rows(A["w_o"][0])
    plan_mlp(A["w_mlp_in"][1], A["w_mlp_out"][1])
    for i in range(4):
        if i % 3 == 0:
            w = A["da_w_in_2"][i // 3]
            plan_stationary(w, 0, 2 * D)
            plan_half_k(w, 2 * D, 3 * D)
            plan_rows(A["da_w_out_2"][i // 3])
        elif i == 1:
            w = A["nsa_w_in_2"][0]
            part = lambda c: plan_stationary(w, c * 256, c * 256 + 256)
            w1 = lambda b: [plan.append(A["nsa_cmp_w1_2"][0][b][c * 1024:c * 1024 + 1024, :].rearrange("(k p) n -> p k n", p=P))
                            for c in range(2)]
            for c in (4, 5, 0, 1):
                part(c)
            w1(0)
            for c in (2, 3, 6):
                part(c)
            w1(1)
            for c in (8, 7, 9):
                part(c)
            plan_rows(A["nsa_w_out_2"][0])
        else:
            w = A["fox_w_in_2"][0]
            plan_stationary(w, 0, 2 * D)
            plan_half_k(w, 2 * D, 3 * D)
            plan_rows(A["fox_w_out_2"][0])
        plan_mlp(A["mlp_w1_2"][i], A["mlp_w2_2"][i])
        plan.append(A["ple_w_2"][i].rearrange("(k p) n -> p k n", p=P))
        plan_rows(A["ple_gate_w_2"][i])

    raw_at = [sem(f"raw_at{i}") for i in range(RAW_SLOTS)]
    loaded, split, used = [], [], []

    def load_chunk():
        n = len(loaded)
        if n < len(plan):
            src = plan[n]
            dst = raw[n % RAW_SLOTS][:, :].rearrange("p (k n) -> p k n", k=src.shape[1])
            loaded.append(sp.dma(dst, src, raw_at[n % RAW_SLOTS], 16 * (n // RAW_SLOTS + 1),
                                 used[n - RAW_SLOTS] if n >= RAW_SLOTS else None))

    def split_chunk():
        n = len(split)
        if n < len(plan):
            h, r = hi[n % HI_SLOTS][:, :], raw[n % RAW_SLOTS][:, :]
            made = act.run(lambda e: e.activation(h, r, ACT.Copy),
                           loaded[n], used[n - HI_SLOTS] if n >= HI_SLOTS else None)
            split.append(dve.run(lambda e: e.tensor_tensor(twin(r), r, h.bitcast(F32), ALU.subtract), made))

    ahead = [AHEAD]

    def take():
        return peek(0)

    def peek(later):
        n = len(used) + later
        while len(split) < min(n + 1 + ahead[0], len(plan)):
            split_chunk()
        k = plan[n].shape[1]
        shaped = lambda a: a.rearrange("p (k n) -> p k n", k=k)
        return (shaped(hi[n % HI_SLOTS][:, :]), shaped(twin(raw[n % RAW_SLOTS][:, :]))), split[n]

    def give_back(token):
        used.append(token)
        load_chunk()

    at_ident = sp.dma(ident[:, :], A["k_ident"], sem("at_ident"), 16)
    mod_select = sb("mod_select", [5, 2])
    at_modsel = sp.dma(mod_select[:, :], A["k_modsel"], sem("at_modsel"), 16)

    minus_half = scalars(32)
    set_minus_half = pool.run(lambda e: e.memset(minus_half, -0.5))

    vectors = [("c", A["c"][0]), ("c_ctx", A["c_ctx"]), ("mix1", A["g_mix_pre"][1]), ("mlp0", A["g_mlp_pre"][0]), ("mlp1", A["g_mlp_pre"][1])]
    vectors += [(f"n{j}_{i}", A["norm_g_2"][i, j]) for i in range(4) for j in (0, 2)]
    vector_rows = sb("vector_rows", [KT * len(vectors), P])
    vector_cols = sb("vector_cols", [P, KT * len(vectors)])

    def load_vectors(first, last):
        arrived, count = sem(f"at_vectors{first}"), 16 * (last - first)
        for n in range(first, last):
            sp.dma(vector_rows[n * KT:(n + 1) * KT, :], vectors[n][1].rearrange("(k p) -> k p", p=P), arrived, count)
        return arrived, count

    def turn_vectors(first, last, *tokens):
        rows = KT * last
        got = pe.run(lambda e: e.transpose(bank(0)[:, 0:rows], vector_rows[0:rows, :], ident[0:rows, 0:rows]), *tokens, at_ident, bank_free[0])
        bank_free[0] = act.run(lambda e: e.activation(vector_cols[:, first * KT:rows], bank(0)[:, first * KT:rows], ACT.Copy), got)
        return bank_free[0]

    at_cond = load_vectors(0, 2)
    for _ in range(RAW_SLOTS):
        load_chunk()
    at_vectors = load_vectors(2, len(vectors))
    at_x = load("x", x_rows[:, :, :], A["x"][0].rearrange("(t p) d -> p t d", p=P), loaded[1])
    at_ctx = load("ctx", ctx_rows[:, :, :], A["ctx"][0].rearrange("(t p) d -> p t d", p=P), loaded[1])
    cond_cols_at = turn_vectors(0, 2, at_cond)

    def column(name):
        n = [v for v, _ in vectors].index(name)
        return vector_cols[:, n * KT:(n + 1) * KT]

    def row_gain(name, slot, vector, *tokens):
        return load(name, gains[:, slot, :], vector.rearrange("(a d) -> a d", a=1).broadcast_to([P, D]), *tokens)

    def mm(out_, lhs, rhs, start, stop):
        return lambda e: e.matmul(out_, lhs, rhs, start=start, stop=stop, skip_group_check=True)

    def product(out_, pairs, *tokens, each=None):
        for n, (lhs, rhs) in enumerate(pairs):
            step = mm(out_, lhs, rhs, n == 0, n == len(pairs) - 1)
            if each and n % 3 == 0:
                pe.wait(*tokens, each[n // 3])
            if n < len(pairs) - 1:
                pe.quiet(step, *tokens)
        return pe.run(step, *tokens)

    def pipelined(n, *stages):
        order = list(reversed(range(2, len(stages)))) + [0, 1]
        for turn in range(n + len(stages) - 1):
            for lag in order:
                if stages[lag] and 0 <= turn - lag < n:
                    stages[lag](turn - lag)

    def three(a, b):
        (ah, al), (bh, bl) = a, b
        return [(ah, bh), (ah, bl), (al, bh)]

    def inverse_root(sumsq, n, width, *tokens):
        a = pool.run(lambda e: e.tensor_scalar(sumsq, sumsq, 1.0 / n, EPS, ALU.mult, ALU.add), *tokens)
        return pool.run(lambda e: e.tensor_tensor(sumsq, sumsq, minus_half[:, 0:width], ALU.pow), a, set_minus_half)

    def sum_of_squares(src, dst, junk, *tokens):
        return act.run(lambda e: e.activation(junk, src, ACT.Square, accum_out=dst), *tokens)

    norm_scale = scalars(8)
    square_out = sb("square_out", [P, D])[:, :]
    diag = sb("diag", [P, 4, P])

    last_to_cols = [None]

    def to_cols(tiles, scale, shift, hi_cols, lo_cols, full, *tokens, first_bank=4):
        tokens, ready, done = list(tokens), [], []
        for t, (src, at) in enumerate(tiles):
            ss = norm_scale[:, t:t + 1]
            a = sum_of_squares(src, ss, full[:, :, t * P:(t + 1) * P], at, tokens, last_to_cols[0])
            r = inverse_root(ss, D, 1, a)
            ready.append(dve.run(lambda e, t=t, ss=ss: e.tensor_scalar(diag[:, t, :], ident[:, :], ss, None, ALU.mult),
                                 r, at_ident, last_to_cols[0]))
        for b in range(KT // 2):
            bk = first_bank + b
            for j in range(2):
                k = 2 * b + j
                for t, (src, at) in enumerate(tiles):
                    got = product(bank(bk)[:, (2 * j + t) * P:(2 * j + t + 1) * P], [(src[:, k * P:(k + 1) * P], diag[:, t, :])],
                                  ready[t], at, bank_free[bk])
            src = bank(bk).rearrange("p (k n) -> p k n", k=2)
            for dst in (full, hi_cols):
                for j in range(2):
                    a = act.run(lambda e, k=2 * b + j, j=j, src=src, dst=dst: e.activation(
                        dst[:, k, :], src[:, j, :], ACT.Identity, bias=shift[:, k:k + 1], scale=scale[:, k:k + 1]), got, tokens)
            bank_free[bk] = a
            h, l, f = (x[:, 2 * b:2 * b + 2, :] for x in (hi_cols, lo_cols, full))
            l_at = dve.run(lambda e, h=h, l=l, f=f: e.tensor_tensor(l, f, h.bitcast(F32), ALU.subtract), a, tokens)
            done += [l_at, l_at]
        last_to_cols[0] = [l_at, got]
        return done

    def hcols_split(n_tokens, region=None, base=0):
        r = hcols if region is None else region
        n = KT * n_tokens
        shaped = lambda o: r[:, base + o:base + o + n].rearrange("p (k n) -> p k n", k=KT)
        return twin(shaped(0)), twin(shaped(n))

    def full_scratch(n_tokens, base=8192):
        return work[:, base:base + KT * n_tokens].rearrange("p (k n) -> p k n", k=KT)

    rms_scale, rms_parts = scalars(4), scalars(8)
    last_tail, last_square = [None] * 4, [None]
    half = lambda a, ch: a[:, ch * 512:ch * 512 + 512]

    def tail(x, t, y, y_at, gain, junk, x_at, *tokens, unscaled=None):
        ss, squares, read = rms_scale[:, t:t + 1], [], []
        for ch in range(2):
            last_square[0] = sum_of_squares(half(y, ch), rms_parts[:, 2 * t + ch:2 * t + ch + 1], half(square_out, ch),
                                            y_at[ch], last_tail[t], last_square[0])
            squares.append(last_square[0])
        r = pool.run(lambda e: e.tensor_tensor(ss, rms_parts[:, 2 * t:2 * t + 1], rms_parts[:, 2 * t + 1:2 * t + 2], ALU.add), squares, last_tail[t])
        if unscaled:
            r = pool.run(lambda e: e.tensor_tensor(ss, ss, unscaled[1], ALU.mult), r)
        r = inverse_root(ss, D, 1, r)
        if unscaled:
            r = pool.run(lambda e: e.tensor_tensor(ss, ss, unscaled[0], ALU.mult), r)
        for ch in range(2):
            read.append(dve.run(lambda e, ch=ch: e.tensor_tensor(half(junk, ch), half(y, ch), half(gain, ch), ALU.mult), squares[ch], *tokens))
        new = [dve.run(lambda e, ch=ch: e.scalar_tensor_tensor(half(x, ch), half(junk, ch), ss, half(x, ch), ALU.mult, ALU.add), r, read[ch], x_at)
               for ch in range(2)]
        last_tail[t] = new[1]
        return new, read

    def y_banks(t):
        return view(bank(2 * t), 0, [[1, D]])

    def rows_product(cols, n_k, *tokens, first_bank=0, begin=True, end=True, cols_at=None, first_k=0):
        n_chunks = n_k // 2
        groups = [[n] for n in range(n_chunks)]
        if end and n_chunks > 1:
            groups[-2:] = [[n_chunks - 2, n_chunks - 1]]
        for group in groups:
            chunks = [peek(n - group[0]) for n in group]
            done = [[None, None], [None, None]]
            for t in range(TT):
                for ch in range(2):
                    bk = first_bank + 2 * t + ch
                    start, stop = begin and group[0] == 0, end and group[-1] == n_chunks - 1
                    steps = []
                    for n, (w, at) in zip(group, chunks):
                        for j in range(2):
                            for lhs, rhs in three(tuple(c[:, first_k + 2 * n + j, t * P:(t + 1) * P] for c in cols),
                                                  tuple(c[:, j, ch * 512:ch * 512 + 512] for c in w)):
                                steps.append((lhs, rhs, [at, cols_at[n] if cols_at else None]))
                    for m, (lhs, rhs, needs) in enumerate(steps):
                        step = mm(bank(bk), lhs, rhs, start and m == 0, stop and m == len(steps) - 1)
                        pe.wait(list(tokens), bank_free[bk] if start else None, needs)
                        if m == len(steps) - 1 and (stop or (t == 1 and ch == 1)):
                            done[t][ch] = pe.run(step)
                        else:
                            pe.quiet(step)
            for _ in group:
                give_back(done[1][1])
        return done

    def squared_relu(src, h, l, got, free):
        full = twin(l)
        a = act.run(lambda e: e.activation(full, src, ACT.Relu), got, free)
        s = dve.run(lambda e: e.tensor_tensor(full, full, full, ALU.mult), a)
        c = act.run(lambda e: e.activation(h, full, ACT.Copy), s)
        return a, dve.run(lambda e: e.tensor_tensor(l, full, h.bitcast(F32), ALU.subtract), c)

    def mlp(cols, cols_at, work_free, meanwhile=None):
        quarter = []
        used_at = [work_free, work_free]
        for q in range(QUARTERS + 1):
            if q < QUARTERS:
                base = (q % 2) * 4096
                shaped = lambda o: twin(work[:, base + o:base + o + 2048].rearrange("p (k n) -> p k n", k=KT))
                hh, hl = shaped(0), shaped(2048)
                ready = []
                for n in range(KT // 2):
                    w, at = take()
                    bk = 4 + n % 4
                    for j in range(2):
                        pairs = []
                        for k in range(KT):
                            pairs += three(tuple(c[:, k, j * P:(j + 1) * P] for c in w), tuple(c[:, k, :] for c in cols))
                        got = product(bank(bk)[:, j * SEQ:(j + 1) * SEQ], pairs, at, bank_free[bk], each=cols_at)
                    give_back(got)
                    bank_free[bk], done = squared_relu(bank(bk).rearrange("p (k n) -> p k n", k=2), hh[:, 2 * n:2 * n + 2, :],
                                                       hl[:, 2 * n:2 * n + 2, :], got, used_at[q % 2])
                    ready.append(done)
                quarter.append(((hh, hl), ready))
            if q == 1 and meanwhile:
                meanwhile()
            if q > 0:
                parts, ready = quarter[q - 1]
                used_at[(q - 1) % 2] = rows_product(parts, KT, begin=q == 1, end=q == QUARTERS, cols_at=ready)
        return used_at[(QUARTERS - 1) % 2]

    cond = sb("cond", [P, KT, 4], F32R)
    cond_in = view(vector_cols[:, :], 0, [[1, KT], [KT, 2]])
    cond_full = scalars(2 * KT).rearrange("p (k n) -> p k n", n=2)
    cond_tanh = scalars(2 * KT).rearrange("p (k n) -> p k n", n=2)
    tok = act.run(lambda e: e.activation(cond_tanh, cond_in, ACT.Tanh, scale=0.5), cond_cols_at)
    tok = dve.run(lambda e: e.scalar_tensor_tensor(cond_full, cond_tanh, 1.0, cond_in, ALU.add, ALU.mult), tok)
    tok = dve.run(lambda e: e.tensor_scalar(cond_full, cond_full, 0.5, None, ALU.mult), tok)
    tok = dve.run(lambda e: e.tensor_copy(cond[:, :, 0:2], cond_full), tok)
    cond_at = dve.run(lambda e: e.tensor_tensor(cond[:, :, 2:4], cond_full, cond[:, :, 0:2].bitcast(F32), ALU.subtract), tok)

    mods_free = [None, None]
    sel_rows = sb("sel_rows", [5, 2, P])
    sel_at = [dve.run(lambda e, n=n: e.tensor_copy(sel_rows[:, n, :], mod_select[:, n:n + 1].broadcast_to([5, P])), at_modsel)
              for n in range(2)]
    mod_cols = scalars(2 * 4 * KT * 2).rearrange("p (l m k n) -> p l m k n", l=2, m=4, k=KT)

    def half_modulation(layer, m, slot, ch):
        row = mods[:, slot, :]
        parts = []
        if ch == 0:
            parts.append(load(f"b_ada{layer}{m}", row[4:5, :], A["b_ada"][layer:layer + 1, m * D:(m + 1) * D], mods_free[slot]))
        bk = ch
        for half in range(2):
            w, at = take()
            for k in range(4):
                for n, part in enumerate(w):
                    first, last = half == 0 and k == 0 and n == 0, k == 3 and n == 1
                    step = mm(bank(bk)[0:4, :], cond[:, half * 4 + k, :], part[:, k, :], first, half == 1 and last)
                    if last:
                        got = pe.run(step)
                    else:
                        pe.quiet(step, at, cond_at, bank_free[bk])
            give_back(got)
        bank_free[bk] = act.run(lambda e: e.activation(row[0:4, ch * 512:ch * 512 + 512], bank(bk)[0:4, :], ACT.Copy),
                                got, mods_free[slot])
        return parts + [bank_free[bk]]

    def modulation(layer, m, slot):
        return half_modulation(layer, m, slot, 0) + half_modulation(layer, m, slot, 1)

    def mod_to_cols(slot, dst, parts):
        bk = 2
        for k in range(KT):
            got = product(bank(bk)[:, 2 * k:2 * k + 2], [(mods[:, slot, k * P:(k + 1) * P], mod_select[:, :])],
                          parts, at_modsel, bank_free[bk])
        mods_free[slot] = got
        done = dve.run(lambda e: e.tensor_copy(dst, bank(bk)[:, 0:2 * KT].rearrange("p (k n) -> p k n", n=2)), got)
        bank_free[bk] = done
        return done

    def mod_to_rows(slot, which, parts, first_bank):
        for ch in range(2):
            got = product(bank(first_bank + ch), [(sel_rows[:, which, :], mods[:, slot, ch * 512:ch * 512 + 512])],
                          parts, sel_at, bank_free[first_bank + ch])
        return got

    def gate_gain(slot, which, parts, g, g_at, first_bank):
        got = mod_to_rows(slot, which, parts, first_bank)
        done = dve.run(lambda e: e.tensor_tensor(gains[:, g, :], view(bank(first_bank), 0, [[1, D]]), gains[:, g, :], ALU.mult),
                       got, g_at)
        for b in range(2):
            bank_free[first_bank + b] = done
        return done, got

    seqs = [(x_rows, at_x), (ctx_rows, at_ctx)]
    PH, PA, PM = 0, 4096, 8192
    pool_m = work[:, PM:PM + 2048].rearrange("p (g n) -> p g n", g=8)
    at_pool = load("pool", pool_m, A["k_pool"], loaded[4])
    g_pre_row = work[:, PM + 2048:PM + 3072]
    at_gpre = load("gpre0", g_pre_row, A["g_mix_pre"][0:1, :].broadcast_to([P, D]))
    pool_scale = work[:, PM + 3072:PM + 4096]
    at_pscale = load("pscale", pool_scale, A["pool_scale"][0:1, :].broadcast_to([P, D]))
    g0_at = [row_gain(f"gpost0_{s}", s, A["g_mix_post"][0]) for s in range(2)]

    shift_parts = modulation(0, 0, 0)
    stats0 = scalars(4)
    sq_at = []
    for n, (rows, at) in enumerate(seqs):
        for t in range(TT):
            junk = hcols[:, (2 * n + t) * D:(2 * n + t + 1) * D]
            sq_at.append(sum_of_squares(rows[:, t, :], stats0[:, 2 * n + t:2 * n + t + 1], junk, at))
    rstd0_at = inverse_root(stats0, D, 4, sq_at)
    scale_parts = modulation(0, 1, 1)
    shift_at = [mod_to_rows(0, n, shift_parts, 4 + 2 * n) for n in range(2)]
    mods_free[0] = shift_at[1]
    h_at = []
    for n, (rows, at) in enumerate(seqs):
        a_row = work[:, PA + n * D:PA + (n + 1) * D]
        got = mod_to_rows(1, n, scale_parts, 2)
        a_at = dve.run(lambda e, a_row=a_row: e.scalar_tensor_tensor(a_row, view(bank(2), 0, [[1, D]]), 1.0, g_pre_row, ALU.add, ALU.mult),
                       got, at_gpre)
        bank_free[2] = bank_free[3] = a_at
        mods_free[1] = got
        for t in range(TT):
            i = 2 * n + t
            h = work[:, PH + i * D:PH + (i + 1) * D]
            m = dve.run(lambda e, h=h, i=i, t=t, rows=rows, a_row=a_row: e.scalar_tensor_tensor(
                h, rows[:, t, :], stats0[:, i:i + 1], a_row, ALU.mult, ALU.mult), a_at, rstd0_at, at)
            s_at = dve.run(lambda e, h=h, n=n: e.tensor_tensor(h, h, view(bank(4 + 2 * n), 0, [[1, D]]), ALU.add),
                           m, shift_at[n])
        bank_free[4 + 2 * n] = bank_free[5 + 2 * n] = s_at
        h_at.append(s_at)

    gt1_parts = modulation(0, 2, 0)
    g0_at = [gate_gain(0, n, gt1_parts, n, g0_at[n], 2)[0] for n in range(2)]
    mods_free[0] = g0_at
    sh2_at = mod_to_cols(1, mod_cols[:, 0, 2, :, :], modulation(0, 3, 1))

    vectors_at = turn_vectors(2, len(vectors), list((at_cond, at_vectors)))
    ahead[0] = AHEAD + 1
    onehot, mask_row, by_dist = (hcols[0:n, 4096 + o:4096 + o + BIAS_W] for n, o in ((BUCKETS, 0), (16, BIAS_W), (16, 2 * BIAS_W)))
    rel = hcols[0:BUCKETS, 4096 + 3 * BIAS_W:4096 + 3 * BIAS_W + 16]
    at_oh = load("onehot", onehot, A["k_onehot"])
    at_rel = load("rel", rel, A["rel_bias_2"])
    at_mask = load("mask8", mask_row, A["k_mask8"])
    table_dram = nc.dram_tensor("bias_tiles", [16, P, SEQ], F32)
    got = product(bank(0)[0:16, 0:BIAS_W], [(rel, onehot)], at_oh, at_rel, bank_free[0])
    bank_free[0] = b_at = dve.run(lambda e: e.scalar_tensor_tensor(by_dist, bank(0)[0:16, 0:BIAS_W], 8.0, mask_row, ALU.mult, ALU.add),
                                  got, at_mask)
    stored = pool.dma(table_dram.ap(), view(by_dist, P - 1, [[-1, P], [1, SEQ]]), sem("table_stored"), 16, b_at)
    bias8 = hcols[:, 4096:8192].rearrange("p (h j) -> p h j", h=16)

    dh, dl = hcols_split(2 * SEQ)
    diff_at = []
    for n in range(2):
        for c in range(KT):
            i = n * KT + c
            bk = 4 + (i // 2) % 4
            o = bank(bk)[:, (i % 2) * SEQ:(i % 2 + 1) * SEQ]
            got = product(o, [(work[:, PH + (2 * n + t) * D + c * P:PH + (2 * n + t) * D + (c + 1) * P], pool_m[:, (c // 2) * 2 + t, :])
                              for t in range(TT)], h_at[n], at_pool, bank_free[bk])
            if i % 2:
                cs, ts = slice(c - 1, c + 1), slice(n * SEQ, (n + 1) * SEQ)
                src = bank(bk).rearrange("p (k n) -> p k n", k=2)
                a = act.run(lambda e, cs=cs, ts=ts, src=src: e.activation(dh[:, cs, ts], src, ACT.Copy), got)
                d_at = dve.run(lambda e, cs=cs, ts=ts, src=src: e.tensor_tensor(dl[:, cs, ts], src, dh[:, cs, ts].bitcast(F32), ALU.subtract), a, stored)
                bank_free[bk] = d_at
        diff_at.append(d_at)
    w, at = take()
    for n in range(2):
        for t in range(TT):
            tile = slice((2 * n + t) * P, (2 * n + t + 1) * P)
            for g in range(4):
                bk = 4 * n + 2 * t + g // 2
                pairs = []
                for k in range(2):
                    pairs += three(tuple(c[:, 2 * g + k, tile] for c in (dh, dl)), tuple(c[:, 2 * g + k, :] for c in w))
                got = product(bank(bk)[:, (g % 2) * 256:(g % 2 + 1) * 256], pairs, at, diff_at, bank_free[bk])
    give_back(got)
    pooled = got

    def pre_scale(layer, m, gain, at):
        return [dve.run(lambda e, n=n: e.scalar_tensor_tensor(mod_cols[:, layer, m, :, n], mod_cols[:, layer, m, :, n], 1.0,
                                                             gain, ALU.add, ALU.mult), at, vectors_at) for n in range(2)]

    x_at, parts = [], []
    for n, (rows, _) in enumerate(seqs):
        for t in range(TT):
            i = 2 * n + t
            y = work[:, PH + i * D:PH + (i + 1) * D]
            y_at = dve.run(lambda e, y=y, i=i: e.tensor_tensor(y, view(bank(2 * i), 0, [[1, D]]), pool_scale, ALU.mult), pooled, at_pscale)
            bank_free[2 * i] = bank_free[2 * i + 1] = y_at
            x_at.append(tail(rows[:, t, :], i, y, [y_at, y_at], gains[:, n, :], hcols[:, i * D:(i + 1) * D], [], g0_at)[0])
            parts.append(half_modulation(0, 4 + n, n, t))
    sc2_at = pre_scale(0, 3, column("mlp0"), mod_to_cols(0, mod_cols[:, 0, 3, :, :], parts[0] + parts[1]))

    tail_done = x_at[-1]
    g0_at = [row_gain(f"gpost0m_{s}", s, A["g_mlp_post"][0], tail_done) for s in range(2)]
    hh, hl = hcols_split(2 * SEQ)
    cols_at = []
    hidden_pairs = lambda w, j, ts: [p for k in range(KT) for p in
                                    three(tuple(c[:, k, j * P:(j + 1) * P] for c in w), (hh[:, k, ts], hl[:, k, ts]))]
    for n, (rows, _) in enumerate(seqs):
        ts = slice(n * SEQ, (n + 1) * SEQ)
        cols_at.append(to_cols([(rows[:, t, :], x_at[2 * n + t]) for t in range(TT)],
                               mod_cols[:, 0, 3, :, n], mod_cols[:, 0, 2, :, n], hh[:, :, ts], hl[:, :, ts],
                               full_scratch(SEQ, n * KT * SEQ), sh2_at, sc2_at, tail_done, first_bank=4 - 4 * n))
        if n == 0:
            w, at = take()
            for j in range(2):
                product(bank(4 + j)[:, ts], hidden_pairs(w, j, ts), at, bank_free[4 + j], each=cols_at[0])
    g0_at = [gate_gain(1, n, parts[2] + parts[3], n, g0_at[n], 2 * n)[0] for n in range(2)]
    mods_free[1] = g0_at

    y_rows = work[:, 8192:12288].rearrange("p (i d) -> p i d", i=4)
    shaped = lambda o: twin(work[:, o:o + 4096].rearrange("p (k n) -> p k n", k=KT))
    fh, fl = shaped(0), shaped(4096)
    hidden_free = cols_at
    y_at = [[cols_at, cols_at] for _ in range(4)]
    halves = [(n % 2, m, ch) for n, m in enumerate(MOD_ORDER) for ch in range(2)]
    parts, mod1_at, pending = [], {}, []

    def next_half_modulation():
        finish_modulation()
        slot, m, ch = halves.pop(0)
        parts.extend(half_modulation(1, m, slot, ch))
        if ch == 1:
            if m in (2, 5):
                mod1_at[m] = list(parts)
            else:
                pending.append((slot, m, list(parts)))
            parts.clear()

    def finish_modulation():
        for slot, m, whole in pending:
            at = mod_to_cols(slot, mod_cols[:, 1, m if m < 2 else m - 1, :, :], whole)
            mod1_at[m] = at if m in (0, 3) else pre_scale(1, 1 if m == 1 else 3, column("mix1" if m == 1 else "mlp1"), at)
        pending.clear()

    for q in range(QUARTERS):
        ready = []
        for n in range(KT // 2):
            w, at = take()
            for j in range(2):
                f = 2 * n + j
                bk = 4 + f % 4
                ts = slice(SEQ, 2 * SEQ) if q == 0 and n == 0 else slice(0, 2 * SEQ)
                got = product(bank(bk)[:, ts], hidden_pairs(w, j, ts), at, bank_free[bk], each=cols_at[1])
                bank_free[bk], done = squared_relu(bank(bk), fh[:, f, :], fl[:, f, :], got, hidden_free)
                ready.append(done)
            give_back(got)
            if n < 3:
                next_half_modulation()
        for ch in range(2):
            for n in range(2):
                w, at = take()
                for i in range(4):
                    pairs = []
                    for j in range(4):
                        pairs += three(tuple(c[:, 4 * n + j, i * P:(i + 1) * P] for c in (fh, fl)), tuple(c[:, j, :] for c in w))
                    for m, (lhs, rhs) in enumerate(pairs):
                        step = mm(bank(i), lhs, rhs, n == 0 and m == 0, n == 1 and m == len(pairs) - 1)
                        if m == len(pairs) - 1:
                            got = pe.run(step)
                        else:
                            pe.quiet(step, at, ready[4 * n + m // 3], bank_free[i] if n == 0 else None)
                    if n == 1:
                        seg = y_rows[:, i, ch * 512:ch * 512 + 512]
                        if q == 0:
                            e_at = act.run(lambda e, seg=seg, i=i: e.activation(seg, bank(i), ACT.Copy), got, y_at[i][ch])
                        else:
                            e_at = dve.run(lambda e, seg=seg, i=i: e.tensor_tensor(seg, bank(i), seg, ALU.add), got, y_at[i][ch])
                        y_at[i][ch] = e_at
                        bank_free[i] = e_at
                give_back(got)
        hidden_free = got
    ahead[0] = AHEAD

    def project(tiles, first_bank, chunks, needs):
        done = []
        for i in tiles:
            steps = []
            for c, (w, at) in enumerate(chunks):
                for j in range(4):
                    steps += [(p, at) for p in three(tuple(h[:, 4 * c + j, i * P:(i + 1) * P] for h in (hh, hl)), tuple(h[:, j, :] for h in w))]
            for m, ((lhs, rhs), at) in enumerate(steps):
                step = mm(bank(first_bank + i), lhs, rhs, m == 0, m == len(steps) - 1)
                pe.wait(at, needs, bank_free[first_bank + i])
                if m < len(steps) - 1:
                    pe.quiet(step)
            done.append(pe.run(step))
        return done

    sh1_at, sc1_at, sh2_at, sc2_at = (mod1_at[m] for m in (0, 1, 3, 4))
    cols_at = []
    for n, (rows, _) in enumerate(seqs):
        for i in (2 * n, 2 * n + 1):
            x_at[i] = tail(rows[:, i % 2, :], i, y_rows[:, i, :], y_at[i], gains[:, n, :], work[:, i * D:(i + 1) * D],
                           x_at[i], hidden_free, g0_at)[0]
        ts = slice(n * SEQ, (n + 1) * SEQ)
        cols_at.append(to_cols([(rows[:, t, :], x_at[2 * n + t]) for t in range(TT)],
                               mod_cols[:, 1, 1, :, n], mod_cols[:, 1, 0, :, n], hh[:, :, ts], hl[:, :, ts],
                               full_scratch(SEQ, n * KT * SEQ), sh1_at, sc1_at, x_at[2 * n + 1]))
        if n == 0:
            kv_done = project((0, 1), 0, [peek(0), peek(1)], cols_at[0])
    kv_done += project((2, 3), 0, [peek(0), peek(1)], cols_at[1])
    for _ in range(2):
        give_back(kv_done[-1])
    tail_done = x_at[-1]
    g1_at = [row_gain("gpost1", 0, A["g_mix_post"][1], tail_done), row_gain("gpost1m", 1, A["g_mlp_post"][1], tail_done)]

    HQ, HKV, HD = 8, 2, P
    AT = 2 * TT
    q_rows = work[:, 0:2048].rearrange("p (t n) -> p t n", t=TT)
    kv_rows = work[:, 2048:4096].rearrange("p (t n) -> p t n", t=AT)
    scratch = work[:, 4096:6144]
    q_cols = work[:, 6144:8192].rearrange("p (h n) -> p h n", h=HQ)
    k_cols = work[:, 8192:9216].rearrange("p (h n) -> p h n", h=HKV)
    rope = work[:, 9216:10240].rearrange("p (i t n) -> p i t n", i=4, t=TT)
    e_buf = [work[:, 10240 + i * 512:10752 + i * 512] for i in range(3)] + [square_out[:, 0:512]]
    scratch_k, scratch_q = scratch[:, 0:1024], scratch[:, 1024:2048]

    gqk = sb("gqk", [P, 2, P])
    at_gq = load("g_q", gqk[:, 0, :], A["g_q"][0:1, :].broadcast_to([P, P]))
    at_gk = load("g_k", gqk[:, 1, :], A["g_k"][0:1, :].broadcast_to([P, P]))
    at_rope = [load(f"rope{i}", rope[:, i, :, :], A["k_cos"] if i % 2 == 0 else A["k_sin"], tail_done) for i in range(4)]
    rope_at = []
    for i in range(2):
        for t in range(TT):
            cos, sin = rope[:, 2 * i, t, :], rope[:, 2 * i + 1, t, :]
            g = gqk[:, i, :]
            rope_at.append(dve.run(lambda e, cos=cos, g=g: e.tensor_tensor(cos, cos, g, ALU.mult), at_gq, at_gk, at_rope))
            pair = lambda a, o: view(a, o, [[64, 2], [1, 32]])
            for o in range(2):
                rope_at.append(dve.run(lambda e, sin=sin, g=g, o=o: e.tensor_tensor(
                    pair(sin, 32 * o), pair(sin, 32 * o), pair(g, 32 - 32 * o), ALU.mult)))

    def normalize_heads(src, dst, ss, got):
        n = len(src)
        for i in range(n):
            last_square[0] = sum_of_squares(src[i], ss[:, i:i + 1], square_out[:, 0:HD], got[i], last_square[0])
        tok = inverse_root(ss, HD, n, last_square[0])
        for i in range(n):
            tok = act.run(lambda e, i=i: e.activation(dst[i], src[i], ACT.Copy, scale=ss[:, i:i + 1]), tok, cols_at)
        return tok

    def rotate(rows_t, scr, n_heads, table, *tokens):
        for t in range(TT):
            heads = rows_t(t)
            part = lambda a, o: view(a, o, [[P, n_heads], [64, 2], [1, 32]])
            tbl = lambda o: view(rope, ((2 * table + 1) * TT + t) * P + o, [[0, n_heads], [64, 2], [1, 32]])
            for o in range(2):
                s_at = dve.run(lambda e, o0=part(scr, t * n_heads * P + 32 * o), i0=part(heads, 32 - 32 * o), i1=tbl(32 * o):
                               e.tensor_tensor(o0, i0, i1, ALU.mult), rope_at, *tokens)
            whole = view(heads, 0, [[P, n_heads], [1, P]])
            swapped = view(scr, t * n_heads * P, [[P, n_heads], [1, P]])
            cos = view(rope, (2 * table * TT + t) * P, [[0, n_heads], [1, P]])
            c_at = dve.run(lambda e, whole=whole, cos=cos: e.tensor_tensor(whole, whole, cos, ALU.mult), s_at)
            done = dve.run(lambda e, whole=whole, swapped=swapped: e.tensor_tensor(whole, whole, swapped, ALU.add), c_at)
        return done

    head_ss = scalars(24)
    done = kv_done
    of = [(t, h) for t in range(AT) for h in range(HKV)]
    for t in range(AT):
        kv_at = act.run(lambda e, t=t: e.activation(kv_rows[:, t, 256:512], bank(t)[:, 256:512], ACT.Copy), done[t], cols_at)
    k_at = normalize_heads([bank(t)[:, h * HD:(h + 1) * HD] for t, h in of], [kv_rows[:, t, h * HD:(h + 1) * HD] for t, h in of],
                           head_ss[:, 0:8], [done[t] for t, h in of])
    bank_free[0:AT] = [k_at] * AT
    rk_at = rotate(lambda t: kv_rows[:, t, :], scratch_k, HKV, 1, k_at)
    for t in range(TT, AT):
        kc = view(kv_rows, t * 512, [[P, HKV], [1, P]])
        kc_at = dve.run(lambda e, kc=kc: e.tensor_tensor(kc, kc, view(gqk[:, :, :], P, [[0, HKV], [1, P]]), ALU.mult), k_at)
    rq_at = []
    for c in range(2):
        done = project(range(TT), 4 + 2 * c, [peek(0), peek(1)], cols_at)
        got = done[-1]
        for _ in range(2):
            give_back(got)
        of = [(t, h) for t in range(TT) for h in range(4)]
        n_at = normalize_heads([bank(4 + 2 * c + t)[:, h * HD:(h + 1) * HD] for t, h in of],
                               [q_rows[:, t, (4 * c + h) * HD:(4 * c + h + 1) * HD] for t, h in of],
                               head_ss[:, 8 + 8 * c:16 + 8 * c], [done[t] for t, h in of])
        bank_free[4 + 2 * c:6 + 2 * c] = [n_at] * TT
        rq_at.append(rotate(lambda t: q_rows[:, t, c * 512:c * 512 + 512], scratch_q, 4, 0, n_at, rq_at))
    bias_at = load("bias8", bias8, table_dram.ap().rearrange("h p j -> p h j"), stored, got)

    for h in range(HKV):
        for t in range(AT):
            got = pe.run(lambda e, h=h, t=t: e.transpose(bank(h)[:, t * P:(t + 1) * P], kv_rows[:, t, h * P:(h + 1) * P], ident[:, :]),
                         rk_at, kc_at, bank_free[h])
        bank_free[h] = kT_at = act.run(lambda e, h=h: e.activation(k_cols[:, h, :], bank(h), ACT.Copy), got)

    def turn_queries(c):
        for b in (2 * c, 2 * c + 1):
            bk = 6 + b % 2
            for j in range(2):
                for t in range(TT):
                    got = pe.run(lambda e, bk=bk, b=b, j=j, t=t: e.transpose(bank(bk)[:, (2 * j + t) * P:(2 * j + t + 1) * P],
                                 q_rows[:, t, (2 * b + j) * P:(2 * b + j + 1) * P], ident[:, :]), rq_at[c], bank_free[bk])
            bank_free[bk] = act.run(lambda e, bk=bk, b=b: e.activation(q_cols[:, 2 * b:2 * b + 2, :], bank(bk).rearrange("p (h n) -> p h n", h=2), ACT.Copy), got)
        return bank_free[bk]

    qT_at = [turn_queries(0)]

    scale = HD ** -0.5
    oh, ol = hcols_split(SEQ)
    p_cols = scratch.rearrange("p (i k n) -> p i k n", i=2, k=AT)
    stat = scalars(3 * 16)
    units = HQ * TT
    exp_at, norm_at, e_free = [None] * units, [None] * units, [last_square[0]] * 4
    pcols_at, pc_free = [None] * units, [rq_at, rq_at]
    o_done = []

    def scores1(i):
        h, t, bk = i // TT, i % TT, i % 2
        if i == units // 4:
            qT_at.append(turn_queries(1))
        s_at = product(bank(bk), [(q_cols[:, h, t * P:(t + 1) * P], k_cols[:, h // (HQ // HKV), :])], qT_at[2 * i // units], kT_at, bank_free[bk])
        m, total = stat[:, i:i + 1], stat[:, units + i:units + i + 1]
        tok = dve.run(lambda e: e.tensor_reduce(m, bank(bk), AX.X, ALU.max), s_at)
        tok = dve.run(lambda e: e.tensor_scalar(m, m, -scale, None, ALU.mult), tok)
        exp_at[i] = bank_free[bk] = act.run(lambda e: e.activation(e_buf[i % 4], bank(bk), ACT.Exp, bias=m, scale=scale, accum_out=total),
                                            tok, e_free[i % 4])

    def normalize1(i):
        total, r = stat[:, units + i:units + i + 1], stat[:, 2 * units + i:2 * units + i + 1]
        tok = dve.run(lambda e: e.reciprocal(r, total), exp_at[i])
        norm_at[i] = dve.run(lambda e: e.tensor_scalar(e_buf[i % 4], e_buf[i % 4], r, None, ALU.mult), tok)

    def transpose1(i):
        h, t, bk = i // TT, i % TT, 2 + i % 2
        for k in range(AT):
            got = pe.run(lambda e, k=k: e.transpose(bank(bk)[:, k * P:(k + 1) * P], e_buf[i % 4][:, k * P:(k + 1) * P], ident[:, :]),
                         norm_at[i], bank_free[bk])
        e_free[i % 4] = got
        pcols_at[i] = bank_free[bk] = act.run(lambda e: e.activation(
            p_cols[:, h % 2, :, t * P:(t + 1) * P], bank(bk).rearrange("p (k n) -> p k n", k=AT), ACT.Copy), got, pc_free[h % 2])

    def values1(i):
        if i % TT == 0:
            return
        h = i // TT
        v, ok = HKV + h // (HQ // HKV), 4 + h % 2
        got = product(bank(ok)[:, 0:SEQ], [(kv_rows[:, k, v * P:(v + 1) * P], p_cols[:, h % 2, k, :]) for k in range(AT)],
                      pcols_at[i], kv_at, bank_free[ok])
        pc_free[h % 2] = got
        a = act.run(lambda e: e.activation(oh[:, h, :], bank(ok)[:, 0:SEQ], ACT.Copy), got)
        bank_free[ok] = dve.run(lambda e: e.tensor_tensor(ol[:, h, :], bank(ok)[:, 0:SEQ], oh[:, h, :].bitcast(F32), ALU.subtract), a)
        o_done.append((bank_free[ok], got))

    pipelined(units, scores1, normalize1, None, transpose1, values1)
    o_at, got = o_done[-1]
    last_to_cols[0] = [last_to_cols[0], got]
    g1_at[0], mods_free[0] = gate_gain(0, 0, mod1_at[2], 0, g1_at[0], 6)
    g1_at[1], mods_free[1] = gate_gain(1, 0, mod1_at[5], 1, g1_at[1], 4)
    got = rows_product((oh, ol), KT, o_at)

    def add_y(got, gain_slot, g_at, x_at, base=10240, unscaled=(None, None), first_bank=0):
        new = []
        for t in range(TT):
            n, read = tail(x_rows[:, t, :], t, y_banks(t + first_bank // 2), got[t], gains[:, gain_slot, :], work[:, base + t * D:base + (t + 1) * D], x_at[t],
                           g_at, unscaled=unscaled[t])
            bank_free[first_bank + 2 * t:first_bank + 2 * t + 2] = read
            new.append(n)
        return new

    def turn_cols(x_at, gain, hi_cols, lo_cols, *tokens, first_bank=4):
        ready, tokens = [], list(tokens)
        for b in range(KT // 2):
            bk = first_bank + b
            for j in range(2):
                k = 2 * b + j
                for t in range(TT):
                    got = pe.run(lambda e, k=k, j=j, t=t, bk=bk: e.transpose(bank(bk)[:, (2 * j + t) * P:(2 * j + t + 1) * P],
                                 x_rows[:, t, k * P:(k + 1) * P], ident[:, :]), x_at[t][k // 4], bank_free[bk])
            both = slice(2 * b, 2 * b + 2)
            src = bank(bk).rearrange("p (k n) -> p k n", k=2)
            if gain is None:
                a = act.run(lambda e, both=both, src=src: e.activation(hi_cols[:, both, :], src, ACT.Copy), got, tokens)
                l_at = dve.run(lambda e, both=both, src=src: e.tensor_tensor(lo_cols[:, both, :], src, hi_cols[:, both, :].bitcast(F32),
                                                                            ALU.subtract), a, tokens)
            else:
                for j in range(2):
                    a = act.run(lambda e, k=2 * b + j, j=j, src=src: e.activation(hi_cols[:, k, :], src[:, j, :], ACT.Identity,
                                                                                 scale=gain[:, k:k + 1]), got, tokens)
                for j in range(2):
                    l_at = dve.run(lambda e, k=2 * b + j, j=j, src=src: e.scalar_tensor_tensor(
                        lo_cols[:, k, :], src[:, j, :], gain[:, k:k + 1], hi_cols[:, k, :].bitcast(F32), ALU.mult, ALU.subtract), a, tokens)
            bank_free[bk] = l_at
            ready += [l_at, l_at]
        return ready

    def inverse_rms(x_at):
        r = scalars(TT)
        for t in range(TT):
            last_square[0] = sum_of_squares(x_rows[:, t, :], r[:, t:t + 1], square_out, x_at[t], last_square[0])
        return r, inverse_root(r, D, TT, last_square[0])

    def mlp_half(x_at, scale, shift, gain_slot, g_at, *tokens, meanwhile=None, then=None, turn_in=4):
        mh, ml = hcols_split(SEQ)
        unscaled = (None, None)
        if shift is None:
            cols_at = turn_cols(x_at, scale, mh, ml, *tokens, first_bank=turn_in)
            r, r_at = inverse_rms(x_at)
            s1, s2 = scalars(TT), scalars(TT)
            r_at = pool.run(lambda e: e.tensor_tensor(s1, r, r, ALU.mult), r_at)
            r_at = pool.run(lambda e: e.tensor_tensor(s2, s1, s1, ALU.mult), r_at)
            unscaled = [(s1[:, t:t + 1], s2[:, t:t + 1]) for t in range(TT)]
        else:
            cols_at = to_cols([(x_rows[:, t, :], x_at[t]) for t in range(TT)], scale, shift, mh, ml, full_scratch(SEQ), *tokens)
        got = mlp((mh, ml), cols_at, list(tokens), meanwhile)
        other = then() if then else None
        return add_y(got, gain_slot, g_at, x_at, unscaled=unscaled), got, other

    x_at = add_y(got, 0, g1_at[0], x_at)
    x_at, got, _ = mlp_half(x_at, mod_cols[:, 1, 3, :, 0], mod_cols[:, 1, 2, :, 0], 1, g1_at[1], sh2_at, sc2_at, got, x_at[-1])

    bias_block = lambda h, t: bias8[:, h, P:SEQ] if t == 0 else bias8[:, h, :]

    blocks = lambda a, t: a[:, 0:P] if t == 0 else a[:, P:3 * P]
    stats2 = scalars(2 * 32)

    def columns_product(w, cols, at, cols_at, n, evacuate, dup=None, bk=None):
        bk = 4 + n % 4 if bk is None else bk
        for j in range(2):
            pairs = []
            for k in range(KT):
                if dup is None:
                    lw = tuple(c[:, k, j * P:(j + 1) * P] for c in w)
                else:
                    o, dims = dup[j]
                    lw = tuple(view(c, k * 256 + o, dims) for c in w)
                pairs += three(lw, tuple(c[:, k, :] for c in cols))
            got = product(bank(bk)[:, j * SEQ:(j + 1) * SEQ], pairs, at, bank_free[bk], each=cols_at)
        if not r_row_at:
            turn_scales()
        bank_free[bk] = evacuate(bank(bk).rearrange("p (k n) -> p k n", k=2), got)
        return got, bank_free[bk]

    r_row = sb("r_row", [P, SEQ])
    token_r, token_r_at, r_row_at, r_row_used = [None], [None], [], [None]

    def turn_scales():
        for t in range(TT):
            a = dve.run(lambda e, t=t, r=token_r[0]: e.tensor_copy(diag[:, t, :], r[:, t:t + 1].broadcast_to([P, P])), token_r_at[0], r_row_used[0])
            r_row_used[0] = product(bank(1)[:, t * P:(t + 1) * P], [(diag[:, t, :], ident[:, :])], a, bank_free[1])
        bank_free[1] = act.run(lambda e: e.activation(r_row[:, :], bank(1)[:, 0:SEQ], ACT.Copy), r_row_used[0], scaled_at[0])
        r_row_at.append(bank_free[1])

    scaled_at = [None]

    def copy_out(dst, *tokens):
        def evacuate(src, got):
            scaled_at[0] = dve.run(lambda e: e.tensor_tensor(dst, src, view(r_row[:, :], 0, [[0, 2], [1, SEQ]]), ALU.mult), got, r_row_at, *tokens)
            return scaled_at[0]
        return evacuate

    def softmax_part(h_bias, bk, e_out, cols, s_at, e_free, cq=None):
        tok = []
        for t in range(TT):
            m = stats2[:, cols + t:cols + t + 1]
            if cq is None:
                a = dve.run(lambda e, t=t, m=m: e.tensor_tensor_reduce(blocks(e_out, t), blocks(bank(bk), t), bias_block(h_bias, t),
                            1.0, -3e38, ALU.add, ALU.max, m), s_at, e_free, bias_at)
            else:
                a = dve.run(lambda e, t=t: e.scalar_tensor_tensor(blocks(e_out, t), blocks(bank(bk), t), cq[:, t:t + 1], mask8(t),
                            ALU.add, ALU.add), s_at, e_free, mask_at)
                a = dve.run(lambda e, t=t, m=m: e.tensor_reduce(m, blocks(e_out, t), AX.X, ALU.max), a)
            tok.append(a)
        bank_free[bk] = tok[-1]
        ms = stats2[:, cols:cols + TT]
        n_at = dve.run(lambda e: e.tensor_scalar(ms, ms, -0.125, None, ALU.mult), tok)
        for t in range(TT):
            e_at = act.run(lambda e, t=t: e.activation(blocks(e_out, t), blocks(e_out, t), ACT.Exp, bias=stats2[:, cols + t:cols + t + 1],
                           scale=0.125, accum_out=stats2[:, 32 + cols + t:33 + cols + t]), n_at)
        return e_at

    mask_src = sb("mask_src", [P, SEQ])
    mask8 = lambda t: mask_src[:, P:SEQ] if t == 0 else mask_src[:, :]
    at_msrc = pool.run(lambda e: e.memset(mask_src[:, :], 0.0))
    mask_at = pool.run(lambda e: e.affine_select(out=mask_src[:, :], in_=mask_src[:, :], compare_op=ALU.is_ge, fill=NEG8, base=P,
                       pattern=[[-1, SEQ]], channel_multiplier=1), at_msrc)

    def scale_blocks(e_out, r, *tokens):
        for t in range(TT):
            done = dve.run(lambda e, t=t: e.tensor_scalar(blocks(e_out, t), blocks(e_out, t), r[:, t:t + 1], None, ALU.mult), *tokens)
        return done

    def pair_values(steps, ob, o_hi, o_lo, *tokens):
        for step in steps[:-1]:
            pe.quiet(step, *tokens, bank_free[ob])
        got = pe.run(steps[-1])
        a = act.run(lambda e: e.activation(o_hi, bank(ob)[:, 0:SEQ], ACT.Copy), got)
        bank_free[ob] = dve.run(lambda e: e.tensor_tensor(o_lo, bank(ob)[:, 0:SEQ], o_hi.bitcast(F32), ALU.subtract), a)
        return got, bank_free[ob]

    def transpose_blocks(bk, src, *tokens):
        for b in range(3):
            got = pe.run(lambda e, b=b: e.transpose(bank(bk)[:, b * P:(b + 1) * P], src[:, b * P:(b + 1) * P], ident[:, :]),
                         *tokens, bank_free[bk])
        return got

    spare_e = [square_out[:, a * 384:a * 384 + 384] for a in range(2)]

    def differential(i, n_da, cols, cols_at, free):
        q_cols = work[:, 0:2048].rearrange("p (h n) -> p h n", h=KT)
        k_cols = work[:, 2048:4096].rearrange("p (h n) -> p h n", h=KT)
        v_rows = work[:, 4096:6144].rearrange("p (t n) -> p t n", t=TT)
        e_buf = [[work[:, 6144 + (2 * a + c) * 384:6528 + (2 * a + c) * 384] for c in range(2)] for a in range(3)]
        e_buf.append(spare_e)
        a_cols = [work[:, 8448 + a * 384:8832 + a * 384] for a in range(2)]
        o_rows = work[:, 9216:11264].rearrange("p (t n) -> p t n", t=TT)
        lam_init = 0.8 - 0.6 * math.exp(-0.3 * i)
        lam_in = work[:, 11264:11520]
        lam = scalars(4)
        at_l = load(f"lambda{i}", lam_in, A["da_lambda_2"][n_da:n_da + 1].rearrange("a b c -> a (b c)").broadcast_to([P, 4 * HALF]), free)
        sub_g, r = scalars(1), token_r[0]
        at_sg = load(f"subln{i}", sub_g, A["da_subln_2"][n_da].rearrange("(p a) -> p a", a=1))
        for n in range(8):
            w, at = take()
            dst = (q_cols if n < 4 else k_cols)[:, 2 * (n % 4):2 * (n % 4) + 2, :]
            got, qk_at = columns_product(w, cols, at, cols_at, n, copy_out(dst, free))
            give_back(got)
        tok = dve.run(lambda e: e.tensor_tensor(view(lam_in, 0, [[P, 2], [1, HALF]]), view(lam_in, 0, [[P, 2], [1, HALF]]),
                      view(lam_in, HALF, [[P, 2], [1, HALF]]), ALU.mult), at_l)
        tok = dve.run(lambda e: e.tensor_reduce(lam[:, 0:2], view(lam_in, 0, [[P, 2], [1, HALF]]), AX.X, ALU.add), tok)
        tok = act.run(lambda e: e.activation(lam[:, 0:2], lam[:, 0:2], ACT.Exp), tok)
        tok = dve.run(lambda e: e.tensor_tensor(lam[:, 2:3], lam[:, 1:2], lam[:, 0:1], ALU.subtract), tok)
        lam_at = dve.run(lambda e: e.tensor_scalar(lam[:, 2:3], lam[:, 2:3], -lam_init, None, ALU.add), tok)
        sg_at = dve.run(lambda e: e.tensor_scalar(sub_g, sub_g, 1.0 - lam_init, None, ALU.mult), at_sg)
        for ch in range(2):
            for half in range(2):
                w, at = take()
                for t in range(TT):
                    pairs = []
                    for j in range(4):
                        pairs += three(tuple(c[:, 4 * half + j, t * P:(t + 1) * P] for c in cols), tuple(c[:, j, :] for c in w))
                    bk = 2 * ch + t
                    for m, (lhs, rhs) in enumerate(pairs):
                        step = mm(bank(bk), lhs, rhs, half == 0 and m == 0, half == 1 and m == len(pairs) - 1)
                        if m == len(pairs) - 1:
                            got = pe.run(step)
                        else:
                            pe.quiet(step, at, cols_at, bank_free[bk] if half == 0 else None)
                    if half == 1:
                        bank_free[bk] = v_at = act.run(lambda e, t=t, ch=ch, bk=bk: e.activation(
                            v_rows[:, t, ch * 512:ch * 512 + 512], bank(bk), ACT.Copy, scale=r[:, t:t + 1]), got, token_r_at, free)
                give_back(got)
        e_free, ac_free = [[free, last_square[0]]] * 4, [free] * 2
        exp_at, mix_at, turned_at, o_done = {}, {}, {}, {}

        def scores(h):
            for c in range(2):
                bk = 4 + c
                part = slice(HALF * c, HALF * c + HALF)
                for t in range(TT):
                    s_at = product(blocks(bank(bk), t), [(q_cols[part, h, t * P:(t + 1) * P], k_cols[part, h, 0:(t + 1) * P])],
                                   qk_at, bank_free[bk])
                exp_at[h, c] = softmax_part(2 * h + c, bk, e_buf[h % 4][c], (2 * h + c) * TT, s_at, e_free[h % 4])

        def mix(h):
            e0, e1 = e_buf[h % 4]
            r = recips[:, 4 * h:4 * h + 4]
            tok = dve.run(lambda e: e.reciprocal(r, stats2[:, 32 + 4 * h:36 + 4 * h]), exp_at[h, 0], exp_at[h, 1])
            tok = dve.run(lambda e: e.tensor_scalar(r[:, 2:4], r[:, 2:4], lam[:, 2:3], None, ALU.mult), tok, lam_at)
            for t in range(TT):
                a = dve.run(lambda e, t=t: e.tensor_scalar(blocks(e0, t), blocks(e0, t), r[:, t:t + 1], None, ALU.mult), tok)
                mix_at[h] = dve.run(lambda e, t=t: e.scalar_tensor_tensor(blocks(e0, t), blocks(e1, t), r[:, 2 + t:3 + t], blocks(e0, t),
                                                                         ALU.mult, ALU.add), a)

        def turn(h):
            bk = 6 + h % 2
            e_free[h % 4] = got = transpose_blocks(bk, e_buf[h % 4][0], mix_at[h])
            turned_at[h] = bank_free[bk] = act.run(lambda e: e.activation(a_cols[h % 2], bank(bk)[:, 0:3 * P], ACT.Copy), got, ac_free[h % 2])

        def values(h):
            for t in range(TT):
                ob = 2 * t + h // 4
                got = product(bank(ob)[:, (h % 4) * P:(h % 4 + 1) * P],
                              [(a_cols[h % 2][:, (t + k) * P:(t + k + 1) * P], v_rows[:, k, h * P:(h + 1) * P]) for k in range(t + 1)],
                              turned_at[h], v_at, bank_free[ob])
            ac_free[h % 2] = got
            if h == 3:
                first_half.append(sub_norm(0, got))
            if first_half and h < 6:
                next(first_half[0])
            if h == 7:
                for _ in sub_norm(1, got):
                    pass

        first_half, normed_at, head_squares = [], [], [scalars(8) for _ in range(2)]
        squares = work[:, 11264:12288]

        def sub_norm(part, got):
            ss, tok = head_squares[part], []
            for t in range(TT):
                tok.append(act.run(lambda e, t=t: e.activation(squares[:, t * 512:t * 512 + 512], bank(2 * t + part), ACT.Square),
                                   got, lam_at, normed_at))
            yield
            tok = dve.run(lambda e: e.tensor_reduce(ss, view(squares, 0, [[P, 8], [1, P]]), AX.X, ALU.add), tok)
            tok = inverse_root(ss, P, 8, tok)
            yield
            for t in range(TT):
                bank_free[2 * t + part] = dve.run(lambda e, t=t: e.tensor_tensor(
                    view(o_rows, t * D + part * 512, [[P, 4], [1, P]]), view(bank(2 * t + part), 0, [[P, 4], [1, P]]),
                    view(ss, 4 * t, [[1, 4], [0, P]]), ALU.mult), tok, free)
            normed_at.append(bank_free[2 * t + part])
            yield

        pipelined(KT, scores, mix, None, turn, values)
        oh, ol = hcols_split(SEQ)
        parts_at = []

        def turn_o(b):
            bk = (0, 2, 1, 3)[b]
            for j in range(2):
                for t in range(TT):
                    got = pe.run(lambda e, j=j, t=t: e.transpose(bank(bk)[:, (2 * j + t) * P:(2 * j + t + 1) * P],
                                 o_rows[:, t, (2 * b + j) * P:(2 * b + j + 1) * P], ident[:, :]), normed_at[b // 2], bank_free[bk])
            src = bank(bk).rearrange("p (k n) -> p k n", k=2)
            h_, l_ = oh[:, 2 * b:2 * b + 2, :], ol[:, 2 * b:2 * b + 2, :]
            a = act.run(lambda e: e.activation(h_, src, ACT.Copy, scale=sub_g), got, sg_at)
            bank_free[bk] = dve.run(lambda e: e.scalar_tensor_tensor(l_, src, sub_g, h_.bitcast(F32), ALU.mult, ALU.subtract), a)
            parts_at.append(bank_free[bk])

        turn_o(0)
        turn_o(1)
        rows_product((oh, ol), 4, first_bank=4, end=False, cols_at=parts_at)
        turn_o(2)
        turn_o(3)
        return rows_product((oh, ol), 4, first_bank=4, begin=False, cols_at=parts_at[2:], first_k=4), 4

    recips = scalars(32)

    def forgetting(i, cols, cols_at, free):
        q_cols = work[:, 0:2048].rearrange("p (h n) -> p h n", h=KT)
        k_cols = work[:, 2048:4096].rearrange("p (h n) -> p h n", h=KT)
        v_pad = work[:, 4096:7168].rearrange("p (t g n) -> p t g n", t=TT, g=8)
        e_buf = [work[:, 7168 + a * 384:7552 + a * 384] for a in range(3)] + spare_e[0:1]
        p_cols = [work[:, 8320 + a * 384:8704 + a * 384] for a in range(4)]
        z_at = pool.run(lambda e: e.memset(v_pad[:, :, :, HALF:P], 0.0), free)
        wf = work[:, 9856:9984].rearrange("p (k n) -> p k n", k=KT)
        wf_h = wf_hi[:, :].rearrange("p (k n) -> p k n", k=KT)
        at_wf = load("w_f", wf, A["fox_w_in_2"][0][:, 3 * D:3 * D + 16].rearrange("(k p) n -> p k n", p=P), free)
        cum = work[:, 9984:10496].rearrange("p (t n) -> p t n", t=TT)
        at_cum = load("cum", cum, A["k_cumsum"], free)
        b_f = work[:, 10496:10512]
        at_bf = load("b_f", b_f, A["fox_b_f_2"][0:1, :].broadcast_to([P, 16]), free)
        z = work[:, 10512:10544].rearrange("p (t n) -> p t n", t=TT)
        az = work[:, 10544:10576].rearrange("p (t n) -> p t n", t=TT)
        c8 = work[:, 10576:10608].rearrange("p (h t) -> p h t", t=TT)
        ck = [work[o:o + 16, 10624:10880] for o in (0, HALF)]
        for n in range(8):
            w, at = take()
            dst = (q_cols if n < 4 else k_cols)[:, 2 * (n % 4):2 * (n % 4) + 2, :]
            got, qk_at = columns_product(w, cols, at, cols_at, n, copy_out(dst, free))
            give_back(got)
        tok = dve.run(lambda e: e.tensor_copy(wf_h, wf), at_wf)
        wf_l = twin(wf)
        wf_at = dve.run(lambda e: e.tensor_tensor(wf_l, wf, wf_h.bitcast(F32), ALU.subtract), tok)
        pairs = []
        for k in range(KT):
            pairs += three((wf_h[:, k, :], wf_l[:, k, :]), tuple(c[:, k, :] for c in cols))
        got = product(bank(0)[0:16, 0:SEQ], pairs, wf_at, cols_at, bank_free[0])
        bank_free[0] = zt_at = act.run(lambda e: e.activation(gate_turn[0:16, :], bank(0)[0:16, 0:SEQ], ACT.Copy), got)

        def log_forget():
            for t in range(TT):
                got = pe.run(lambda e, t=t: e.transpose(bank(4)[:, t * 16:(t + 1) * 16], gate_turn[0:16, t * P:(t + 1) * P], ident[0:16, 0:16]),
                             zt_at, bank_free[4])
            for t in range(TT):
                tok = dve.run(lambda e, t=t, r=token_r[0]: e.scalar_tensor_tensor(z[:, t, :], bank(4)[:, t * 16:t * 16 + 16], r[:, t:t + 1], b_f,
                                                                                  ALU.mult, ALU.add), got, at_bf, token_r_at)
            bank_free[4] = tok
            tok = act.run(lambda e: e.activation(az, z, ACT.Abs), tok)
            tok = act.run(lambda e: e.activation(az, az, ACT.Exp, scale=-1.0), tok)
            tok = act.run(lambda e: e.activation(az, az, ACT.Ln, bias=1.0), tok)
            return dve.run(lambda e: e.scalar_tensor_tensor(z, z, 0.0, az, ALU.min, ALU.subtract), tok)

        for ch in range(2):
            for half in range(2):
                w, at = take()
                for t in range(TT):
                    pairs = []
                    for j in range(4):
                        pairs += three(tuple(c[:, 4 * half + j, t * P:(t + 1) * P] for c in cols), tuple(c[:, j, :] for c in w))
                    bk = 2 * ch + t
                    for m, (lhs, rhs) in enumerate(pairs):
                        step = mm(bank(bk), lhs, rhs, half == 0 and m == 0, half == 1 and m == len(pairs) - 1)
                        if m == len(pairs) - 1:
                            got = pe.run(step)
                        else:
                            pe.quiet(step, at, cols_at, bank_free[bk] if half == 0 else None)
                    if half == 1:
                        dst = view(v_pad, (t * 8 + ch * 4) * 192, [[192, 4], [P, 2], [1, HALF]])
                        bank_free[bk] = v_at = act.run(lambda e, dst=dst, bk=bk, t=t, r=token_r[0]: e.activation(
                            dst, view(bank(bk), 0, [[P, 4], [HALF, 2], [1, HALF]]), ACT.Copy, scale=r[:, t:t + 1]), got, token_r_at, free)
                give_back(got)
            if ch == 0:
                lf_at = log_forget()
        got = product(bank(1)[0:16, 0:SEQ], [(z[:, s, :], cum[:, s, :]) for s in range(TT)], lf_at, at_cum, bank_free[1])
        for t in range(TT):
            got = product(bank(1)[:, SEQ + t * 16:SEQ + (t + 1) * 16], [(cum[:, s, t * P:(t + 1) * P], z[:, s, :]) for s in range(TT)])
        for k in ck:
            dve.run(lambda e, k=k: e.tensor_scalar(k, bank(1)[0:16, 0:SEQ], -8.0, None, ALU.mult), got)
        c_at = dve.run(lambda e: e.tensor_scalar(view(c8, 0, [[1, TT], [TT, 16]]), view(bank(1), SEQ, [[16, TT], [1, 16]]), 8.0, None, ALU.mult), got)
        bank_free[1] = c_at

        oh, ol = hcols_split(SEQ)
        e_free, pc_free = [[free, last_square[0]]] * 4, [free] * 4
        exp_at, norm_at, turned_at, o_done = {}, {}, {}, []

        def scores(h):
            part, bk = slice(HALF * (h % 2), HALF * (h % 2) + HALF), h % 2
            pick_head = view(ident[HALF * (h % 2):HALF * (h % 2) + 16, :], HALF * (h % 2) + h, [[0, P]])
            for t in range(TT):
                ks = slice(0, (t + 1) * P)
                s_at = product(blocks(bank(bk), t), [(q_cols[part, h // 2, t * P:(t + 1) * P], k_cols[part, h // 2, ks]),
                                                     (pick_head, ck[h % 2][:, ks])], qk_at, c_at, bank_free[bk])
            exp_at[h] = softmax_part(h, bk, e_buf[h % 4], h * TT, s_at, e_free[h % 4], cq=c8[:, h, :])

        def normalize(h):
            r = recips[:, 2 * h:2 * h + 2]
            tok = dve.run(lambda e: e.reciprocal(r, stats2[:, 32 + 2 * h:34 + 2 * h]), exp_at[h])
            norm_at[h] = scale_blocks(e_buf[h % 4], r, tok)

        def turn(h):
            bk = 2 + h % 2
            e_free[h % 4] = got = transpose_blocks(bk, e_buf[h % 4], norm_at[h])
            turned_at[h] = bank_free[bk] = act.run(lambda e: e.activation(p_cols[h % 4], bank(bk)[:, 0:3 * P], ACT.Copy), got, pc_free[h % 4])

        def values(h):
            if h % 2 == 0:
                return
            j, ob = h // 2, 4 + (h // 2) % 2
            steps = []
            for par in range(2):
                pc = p_cols[(h - 1 + par) % 4]
                v = lambda t: v_pad[:, t, j, par * HALF:par * HALF + P]
                steps.append(mm(bank(ob)[:, 0:SEQ], v(0), pc[:, 0:SEQ], par == 0, False))
                steps.append(mm(bank(ob)[:, P:SEQ], v(1), pc[:, SEQ:3 * P], False, par == 1))
            o_done.append(pair_values(steps, ob, oh[:, j, :], ol[:, j, :], turned_at[h - 1], turned_at[h], v_at, z_at))
            pc_free[h % 4] = pc_free[(h - 1) % 4] = o_done[-1][0]

        pipelined(16, scores, normalize, None, turn, values)
        o_at = o_done[-1][1]
        return rows_product((oh, ol), KT, o_at)

    def sparse(i, cols, cols_at, free):
        G, R = 4, 4
        q_cols = work[:, 0:2048].rearrange("p (h n) -> p h n", h=KT)
        k_cols = work[:, 2048:4096].rearrange("p (b s m n) -> p b s m n", b=2, s=2, m=2)
        v_pad = work[:, 4096:7168].rearrange("p (b t g n) -> p b t g n", b=2, t=TT, g=G)
        shifted = [work[:, 7168 + b * D:8192 + b * D].rearrange("p (g n) -> p g n", g=G) for b in range(2)]
        s_cmp = work[:, 10112:10624]
        p_cmp = work[:, 10624:11136]
        e_buf = [[work[:, 7168 + (2 * a + b) * 384:7552 + (2 * a + b) * 384] for b in range(2)] for a in range(3)]
        e_buf.append(spare_e)
        p_cols = [[work[:, 9472 + (2 * a + b) * 384:9856 + (2 * a + b) * 384] for b in range(2)] for a in range(3)]
        pc_cols = ctx_rows[:, 0, 512:1024].rearrange("p (m n) -> p m n", m=2)
        v_block = ctx_rows[:, 1, :].rearrange("p (m h d) -> p m h d", m=2, h=8)
        natural = [work[:, o:o + 512].rearrange("p (m n) -> p m n", m=2) for o in (9216, 10112)]
        swap = work[:, 9728:9856]
        w2k = work[:, 9856:10112].rearrange("p (k n) -> p k n", k=2)
        at_swap = load("swap", swap, A["k_swap"], free)
        misc = work[:, 11776:12288]
        blk_h = ctx_rows[:, 0, :].rearrange("p (k n) -> p k n", k=16)
        blk_l = ctx_rows[:, 1, :].rearrange("p (k n) -> p k n", k=16)
        w_g, g_rows = misc[:, 0:384].rearrange("p (k n) -> p k n", k=KT), misc[:, 384:480]
        pe_cols = [scalars(16) for _ in range(2)]
        w2v = scalars(128).rearrange("p (k n) -> p k n", k=2)
        at_pe = [load(f"cmp_pe{b}", pe_cols[b], A["nsa_cmp_pe_2"][0][b].rearrange("(l a) d -> (a d) l", a=2)) for b in range(2)]
        w2_rows = lambda b: A["nsa_cmp_w2_2"][0][b].rearrange("(k p) n -> p k n", p=P)
        at_w2v = load("cmp_w2v", w2v, w2_rows(1))
        at_w2k = [load(f"w2k{c}", w2k[:, :, c * HALF:(c + 1) * HALF], w2_rows(0), free) for c in range(2)]
        at_hr = load("headrow", head_row[:, :], A["k_headrow"])
        at_wg = load("w_g", w_g, A["nsa_w_in_2"][0][:, 2560:2608].rearrange("(k p) n -> p k n", p=P), free)
        z_at = [pool.run(lambda e: e.memset(v_pad[:, :, :, :, :], 0.0), free)]

        half_r = scalars(TT)

        def gate_product():
            pairs = []
            for k in range(KT):
                pairs += three((wg_h[:, k, :], wg_l[:, k, :]), tuple(c[:, k, :] for c in cols))
            got = product(bank(1)[0:48, 0:SEQ], pairs, wg_at, cols_at, bank_free[1])
            bank_free[1] = act.run(lambda e: e.activation(gate_turn[0:48, :], bank(1)[0:48, 0:SEQ], ACT.Copy), got)
            return bank_free[1]

        def turn_gates(at):
            for t in range(TT):
                got = pe.run(lambda e, t=t: e.transpose(bank(1)[:, t * 48:(t + 1) * 48], gate_turn[0:48, t * P:(t + 1) * P], ident[0:48, 0:48]),
                             at, bank_free[1])
            tok = dve.run(lambda e, r=token_r[0]: e.tensor_scalar(half_r, r, 0.5, None, ALU.mult), token_r_at)
            for t in range(TT):
                bank_free[1] = act.run(lambda e, t=t: e.activation(g_rows[:, 48 * t:48 * t + 48], bank(1)[:, 48 * t:48 * t + 48], ACT.Tanh,
                                                                  scale=half_r[:, t:t + 1]), got, tok, free)
            return dve.run(lambda e: e.tensor_scalar(g_rows, g_rows, 1.0, 0.5, ALU.add, ALU.mult), bank_free[1])

        def make_q(n):
            w, at = take()
            bk = 2 + n % 2
            got, q_at = columns_product(w, cols, at, cols_at, n, copy_out(q_cols[:, 2 * n:2 * n + 2, :], free), bk=bk)
            give_back(got)
            return q_at

        def make_k(b):
            w, at = take()
            got, n_at = columns_product(w, cols, at, cols_at, b, copy_out(k_cols[:, b, 0, :, :], free))
            give_back(got)
            return n_at

        def swap_k(b, n_at):
            bk = 6 + b
            got = product(bank(bk), [(swap, k_cols[:, b, 0, :, :].rearrange("p m n -> p (m n)"))], n_at, bank_free[bk])
            bank_free[bk] = act.run(lambda e: e.activation(
                k_cols[:, b, 1, :, :], bank(bk).rearrange("p (m n) -> p m n", m=2), ACT.Copy), got, free)
            return bank_free[bk]

        def make_v(b, first_bank):
            w, at = take()
            for t in range(TT):
                bk = first_bank + t
                pairs = []
                for k in range(KT):
                    pairs += three(tuple(c[:, k, t * P:(t + 1) * P] for c in cols), tuple(c[:, k, :] for c in w))
                got = product(bank(bk)[:, 0:256], pairs, at, cols_at, bank_free[bk])
                dst = view(v_pad, (b * TT + t) * G * 192 + HALF, [[192, G], [1, HALF]])
                bank_free[bk] = v_at = act.run(lambda e, dst=dst, bk=bk, t=t, r=token_r[0]: e.activation(
                    dst, view(bank(bk), 0, [[HALF, G], [1, HALF]]), ACT.Copy, scale=r[:, t:t + 1]), got, token_r_at, z_at)
            give_back(got)
            return v_at

        kc_cols = misc[:, 0:64]
        hid = [ctx_hid[:, b * 128:(b + 1) * 128].rearrange("p (k n) -> p k n", k=2) for b in range(2)]
        natural_at, cmp_at = [], []
        for b in range(2):
            w, at = take()
            got, n_at = columns_product(w, cols, at, cols_at, b, copy_out(natural[b], free))
            give_back(got)
            natural_at.append(n_at)
        def shift_tokens(b):
            bk = 6 + b
            got = product(bank(bk), [(swap, natural[b].rearrange("p m n -> p (m n)"))], natural_at[b], at_swap, bank_free[bk])
            swapped = bank(bk).rearrange("p (m n) -> p m n", m=2)
            for m in range(2):
                for par in range(2):
                    g = 2 * m + par
                    upper, lower = (natural[b], swapped) if par == 0 else (swapped, natural[b])
                    act.run(lambda e, g=g, b=b, m=m, upper=upper: e.activation(
                        shifted[b][0:HALF, g, :], upper[0:HALF, m, :], ACT.Copy), got, natural_at[b], free)
                    a1 = act.run(lambda e, g=g, b=b, m=m, lower=lower: e.activation(
                        shifted[b][HALF:P, g, 0:SEQ - 1], lower[HALF:P, m, 1:SEQ], ACT.Copy), got, natural_at[b], free)
            bank_free[bk] = a1
            cmp_at.append(a1)

        def window_blocks(b, blk_free):
            full = blk_l
            z0 = pool.run(lambda e: e.memset(ctx_rows[:, 1, :], 0.0), blk_free)
            for g in range(G):
                f_at = dve.run(lambda e, g=g: e.tensor_tensor(view(full, g * NC, [[64, 16], [1, N_CMP]]),
                               view(shifted[b], g * SEQ, [[2, 16], [CMP_STRIDE, N_CMP]]), view(pe_cols[b], 0, [[1, 16], [0, N_CMP]]), ALU.add),
                               z0, at_pe[b], cmp_at[b])
            h_at = act.run(lambda e: e.activation(twin(blk_h), full, ACT.Copy), f_at, blk_free)
            return dve.run(lambda e: e.tensor_tensor(twin(blk_l), full, twin(blk_h).bitcast(F32), ALU.subtract), h_at)

        def hidden_product(l_at):
            for c in range(2):
                w, at = take()
                for k in range(8):
                    for m, (lhs, rhs) in enumerate(three((twin(blk_h)[:, 8 * c + k, :], twin(blk_l)[:, 8 * c + k, :]),
                                                        tuple(x[:, k, :] for x in w))):
                        last = k == 7 and m == 2
                        step = mm(bank(0)[0:HALF, 0:256], lhs, rhs, c == 0 and k == 0 and m == 0, c == 1 and last)
                        if last:
                            got = pe.run(step)
                        else:
                            pe.quiet(step, at, l_at, bank_free[0])
                give_back(got)
            return got

        def gelu(got):
            u, v = gelu_in[:, :], gelu_out[:, :]
            bank_free[0] = tok = act.run(lambda e: e.activation(u, bank(0)[0:HALF, 0:256], ACT.Copy), got, gelu_used)
            tok = dve.run(lambda e: e.tensor_tensor(v, u, u, ALU.mult), tok)
            tok = dve.run(lambda e: e.tensor_tensor(v, v, u, ALU.mult), tok)
            tok = dve.run(lambda e: e.scalar_tensor_tensor(v, v, 0.044715, u, ALU.mult, ALU.add), tok)
            tok = act.run(lambda e: e.activation(v, v, ACT.Tanh, scale=math.sqrt(2 / math.pi)), tok)
            tok = dve.run(lambda e: e.scalar_tensor_tensor(v, v, 1.0, u, ALU.add, ALU.mult), tok)
            return dve.run(lambda e: e.tensor_scalar(v, v, 0.5, None, ALU.mult), tok)

        def turn_hidden(b, rows_at):
            for k in range(2):
                got = pe.run(lambda e, k=k: e.transpose(bank(1)[:, k * HALF:(k + 1) * HALF], gelu_out[:, k * P:(k + 1) * P], ident[0:HALF, 0:HALF]),
                             rows_at, bank_free[1])
            gelu_used.append(got)
            bank_free[1] = act.run(lambda e: e.activation(hid[b], bank(1)[:, 0:P].rearrange("p (k n) -> p k n", k=2), ACT.Copy), got)
            return bank_free[1]

        gelu_used = []
        shift_tokens(0)
        blocks_at = window_blocks(0, free)
        make_q(0)
        shift_tokens(1)
        wg_h = wf_hi3[:, :].rearrange("p (k n) -> p k n", k=KT)
        tok = dve.run(lambda e: e.tensor_copy(wg_h, w_g), at_wg)
        wg_l = twin(w_g)
        wg_at = dve.run(lambda e: e.tensor_tensor(wg_l, w_g, wg_h.bitcast(F32), ALU.subtract), tok)
        make_q(1)
        gate_cols_at = gate_product()
        blk_free = hidden_product(blocks_at)
        rows_at = gelu(blk_free)
        blocks_at = window_blocks(1, blk_free)
        make_q(2)
        gate_at = turn_gates(gate_cols_at)
        q_at = make_q(3)
        hid_at = turn_hidden(0, rows_at)
        got = product(bank(0)[:, 0:64], [(w2k[:, k, :], hid[0][:, k, :]) for k in range(2)], hid_at, at_w2k, bank_free[0])
        bank_free[0] = kc_at = act.run(lambda e: e.activation(kc_cols, bank(0)[:, 0:64], ACT.Copy), got, gate_at)
        k_sel_at = make_k(0)
        blk_free = hidden_product(blocks_at)
        rows_at = gelu(blk_free)
        swap_k(0, k_sel_at)
        win_at = make_k(1)
        hid_at = turn_hidden(1, rows_at)
        spread_hid = blk_h.rearrange("p k n -> p (k n)")[:, 0:512].rearrange("p (m k n) -> p m k n", m=2, k=2)
        for m in range(2):
            for k in range(2):
                for gg in range(2):
                    sp_at = dve.run(lambda e, m=m, k=k, gg=gg: e.tensor_copy(
                        view(spread_hid, (2 * m + k) * P + gg * 64, [[NC, R], [1, NC]]),
                        view(hid[1], k * HALF + (2 * m + gg) * NC, [[0, R], [1, NC]])), hid_at, blk_free)
        make_v(0, 2)
        k_at = swap_k(1, win_at)
        for m in range(2):
            got = product(bank(0)[:, m * HALF:(m + 1) * HALF],
                          [(spread_hid[:, m, k, :], w2v[:, k, :]) for k in range(2)], sp_at, at_w2v, bank_free[0])
        for m in range(2):
            vb_at = dve.run(lambda e, m=m: e.tensor_tensor(v_block[:, m, :, :], view(bank(0), m * HALF, [[0, 8], [1, HALF]]),
                            view(head_row[:, :], 0, [[1, 8], [0, HALF]]), ALU.mult), got, at_hr, free)
        bank_free[0] = vb_at

        bc = cmp_bias[:, :]
        b0_at = pool.run(lambda e: e.memset(bc, NEG8))
        at_bc = []
        for t, first in ((1, CMP_LEN - 1), (0, P + CMP_LEN - 1)):
            n = len(range(first, SEQ, CMP_STRIDE))
            at_bc.append(dve.run(lambda e, t=t, first=first, n=n: e.tensor_copy(
                view(bc, t * 256, [[NC, 16], [1, n]]), view(bias8, first, [[SEQ, 16], [CMP_STRIDE, n]])), b0_at, bias_at))
        at_valid = load("valid", valid[:, :], A["k_valid"].rearrange("p t a -> p (t a)"))
        for t in range(TT):
            for h in range(16):
                g = h // R
                part = slice(HALF * (h % 2), HALF * (h % 2) + HALF)
                bk = 6 + h % 2
                s_at = product(bank(bk)[:, (t * 8 + h // 2) * NC:(t * 8 + h // 2 + 1) * NC],
                               [(q_cols[part, h // 2, t * P:(t + 1) * P], kc_cols[part, g * NC:(g + 1) * NC])], q_at, kc_at, bank_free[bk])
        by_head = lambda a: view(a, 0, [[NC, 32], [1, NC]])
        m32 = stats2[:, 0:32]
        s32 = stats2[:, 32:64]
        spread = lambda a: view(a, 0, [[1, 32], [0, NC]])
        for par in range(2):
            heads = lambda a, par=par: view(a, par * NC, [[256, TT], [2 * NC, 8], [1, NC]])
            tok = dve.run(lambda e, heads=heads, par=par: e.tensor_tensor(heads(s_cmp), view(bank(6 + par), 0, [[P, TT], [NC, 8], [1, NC]]),
                          heads(bc), ALU.add), s_at, at_bc)
            bank_free[6 + par] = tok
        tok = dve.run(lambda e: e.tensor_reduce(m32, by_head(s_cmp), AX.X, ALU.max), tok)
        tok = dve.run(lambda e: e.tensor_tensor(by_head(s_cmp), by_head(s_cmp), spread(m32), ALU.subtract), tok)
        tok = act.run(lambda e: e.activation(p_cmp, s_cmp, ACT.Exp, scale=0.125), tok)
        tok = dve.run(lambda e: e.tensor_reduce(s32, by_head(p_cmp), AX.X, ALU.add), tok)
        tok = dve.run(lambda e: e.reciprocal(s32, s32), tok)
        for t in range(TT):
            tok = dve.run(lambda e, t=t: e.scalar_tensor_tensor(s32[:, 16 * t:16 * t + 16], s32[:, 16 * t:16 * t + 16], valid[:, t:t + 1],
                          view(g_rows, t * 48, [[3, 16]]), ALU.mult, ALU.mult), tok, at_valid, gate_at)
        pn_at = dve.run(lambda e: e.tensor_tensor(by_head(p_cmp), by_head(p_cmp), spread(s32), ALU.mult), tok)
        v_at = make_v(1, 4)
        for m in range(2):
            for t in range(TT):
                got = pe.run(lambda e, m=m, t=t: e.transpose(bank(2)[:, m * SEQ + t * P:m * SEQ + (t + 1) * P],
                             p_cmp[:, t * 256 + m * P:t * 256 + (m + 1) * P], ident[:, :]), pn_at, bank_free[2])
        pc_at = act.run(lambda e: e.activation(pc_cols, bank(2).rearrange("p (m n) -> p m n", m=2), ACT.Copy), got, free)
        bank_free[2] = pc_at

        oh, ol = hcols_split(SEQ)
        e_free, pc_free = [[pn_at, last_square[0]]] * 4, [[pn_at, got]] * 3
        exp_at, norm_at, turned_at, o_done = {}, {}, {}, []

        def scores(h):
            part, swapped = slice(HALF * (h % 2), HALF * (h % 2) + HALF), (h + h // R) % 2
            for b in range(2):
                for t in range(TT):
                    s_at = product(blocks(bank(b), t), [(q_cols[part, h // 2, t * P:(t + 1) * P], k_cols[part, b, swapped, h // R // 2, 0:(t + 1) * P])],
                                   q_at, k_at, bank_free[b])
                exp_at[h, b] = softmax_part(h, b, e_buf[h % 4][b], 4 * (h % 4) + 2 * b, s_at, e_free[h % 4])

        def normalize(h):
            c0 = 4 * (h % 4)
            r = recips[:, c0:c0 + 4]
            tok = dve.run(lambda e: e.reciprocal(r, stats2[:, 32 + c0:36 + c0]), exp_at[h, 0], exp_at[h, 1])
            tok = dve.run(lambda e: e.tensor_tensor(view(r, 0, [[TT, 2], [1, TT]]), view(r, 0, [[TT, 2], [1, TT]]),
                                                    view(g_rows, h * 3 + 1, [[1, 2], [48, TT]]), ALU.mult), tok, gate_at)
            for b in range(2):
                norm_at[h, b] = scale_blocks(e_buf[h % 4][b], r[:, 2 * b:2 * b + 2], tok)

        def turn(h):
            for b in range(2):
                e_free[h % 4] = got = transpose_blocks(2 + b, e_buf[h % 4][b], norm_at[h, b])
                turned_at[h, b] = bank_free[2 + b] = act.run(lambda e, b=b: e.activation(p_cols[h % 3][b], bank(2 + b)[:, 0:3 * P], ACT.Copy),
                                                             got, pc_free[h % 3])

        def values(h):
            if h % 2 == 0:
                return
            j, g = h // 2, h // R
            ob = 4 + j % 2
            steps = [mm(bank(ob)[:, 0:SEQ], v_block[:, j // 4, 2 * (j % 4):2 * (j % 4) + 2, :].rearrange("p h d -> p (h d)"),
                        pc_cols[:, j // 4, :], True, False)]
            for par in range(2):
                for b in range(2):
                    pc = p_cols[(h - 1 + par) % 3][b]
                    v = lambda t: v_pad[:, b, t, g, HALF - par * HALF:HALF - par * HALF + P]
                    steps.append(mm(bank(ob)[:, 0:SEQ], v(0), pc[:, 0:SEQ], False, False))
                    steps.append(mm(bank(ob)[:, P:SEQ], v(1), pc[:, SEQ:3 * P], False, par == 1 and b == 1))
            o_done.append(pair_values(steps, ob, oh[:, j, :], ol[:, j, :], [turned_at[x, b] for x in (h - 1, h) for b in range(2)],
                                      v_at, vb_at, pc_at))
            pc_free[h % 3] = pc_free[(h - 1) % 3] = o_done[-1][0]

        pipelined(16, scores, normalize, None, turn, values)
        o_at = o_done[-1][1]
        return rows_product((oh, ol), KT, o_at)

    wf_hi = sb("wf_hi", [P, 128], F32R)
    wf_hi3 = sb("wg_hi", [P, 384], F32R)
    head_row = sb("head_row", [P, 8])
    valid = sb("valid", [P, TT])
    cmp_bias = sb("cmp_bias", [P, 512])
    gate_turn = sb("gate_turn", [48, SEQ])
    gelu_in = sb("gelu_in", [P // 2, 256])
    gelu_out = sb("gelu_out", [P // 2, 256])
    ctx_hid = sb("ctx_hid", [P, 256])

    for i in range(4):
        g0, g_2 = column(f"n0_{i}"), column(f"n2_{i}")
        ra = row_gain(f"n1_{i}", 0, A["norm_g_2"][i, 1], x_at)
        rb = row_gain(f"n3_{i}", 1, A["norm_g_2"][i, 3], x_at)
        free = [x_at[-1], x_at[0], got, stored]
        mh, ml = hcols_split(SEQ)
        cols_at = turn_cols(x_at, g0, mh, ml, free)
        r_row_at.clear()
        token_r[0], token_r_at[0] = inverse_rms(x_at)
        free = free + [cols_at]
        y_first = 0
        if i % 3 == 0:
            got, y_first = differential(i, i // 3, (mh, ml), cols_at, free)
        elif i == 1:
            got = sparse(i, (mh, ml), cols_at, free)
        else:
            got = forgetting(i, (mh, ml), cols_at, free)
        x_at = add_y(got, 0, ra, x_at, first_bank=y_first)

        p_rows = work[:, 8192:8704].rearrange("p (t n) -> p t n", t=TT)
        pl = lambda o: twin(work[:, 8704 + o:9216 + o].rearrange("p (k n) -> p k n", k=2))
        ph, plo = pl(0), pl(512)
        at_p = load(f"p{i}", p_rows, A["p_2"][i, 0].rearrange("(t p) n -> p t n", p=P), x_at, got)
        p_split = []

        def turn_p():
            for k in range(2):
                for t in range(TT):
                    tp = pe.run(lambda e, k=k, t=t: e.transpose(bank(4)[:, (2 * k + t) * P:(2 * k + t + 1) * P], p_rows[:, t, k * P:(k + 1) * P], ident[:, :]),
                                at_p, bank_free[4])
            src = bank(4).rearrange("p (k n) -> p k n", k=2)
            a = act.run(lambda e: e.activation(ph, src, ACT.Copy), tp)
            bank_free[4] = dve.run(lambda e: e.tensor_tensor(plo, src, ph.bitcast(F32), ALU.subtract), a)
            p_split.append(bank_free[4])

        def after_mlp():
            return rows_product((ph, plo), 2, p_split, first_bank=4)

        x_at, got, p_done = mlp_half(x_at, g_2, None, 1, rb, got, x_at[-1], meanwhile=turn_p, then=after_mlp, turn_in=4 - y_first)
        cols_at = turn_cols(x_at, None, mh, ml, got, first_bank=0)
        got = rows_product((mh, ml), KT, cols_at=[cols_at[2 * n:2 * n + 2] for n in range(KT // 2)])
        new = []
        for t in range(TT):
            new.append([])
            for ch in range(2):
                th, x = work[:, t * D + ch * 512:t * D + ch * 512 + 512], half(x_rows[:, t, :], ch)
                a = act.run(lambda e, t=t, ch=ch, th=th: e.activation(th, bank(2 * t + ch), ACT.Tanh, scale=0.5), got[t][ch], x_at)
                bank_free[2 * t + ch] = a
                m = dve.run(lambda e, t=t, ch=ch, th=th: e.scalar_tensor_tensor(th, th, 1.0, bank(4 + 2 * t + ch), ALU.add, ALU.mult), a, p_done)
                bank_free[4 + 2 * t + ch] = m
                new[t].append(dve.run(lambda e, th=th, x=x: e.scalar_tensor_tensor(x, th, 0.5, x, ALU.mult, ALU.add), m, x_at[t]))
        x_at = new
    assert len(used) == len(plan), (len(used), len(plan))

    out_at = sp.dma(out.rearrange("a (t p) d -> p (a t) d", p=P), x_rows[:, :, :], sem("out_stored"), 16, x_at)
    sp.wait(out_at)

    block = ctx.enter_context(nc.Block())
    for decorate, lane in ((block.sync, sp), (block.gpsimd, pool), (block.scalar, act), (block.vector, dve), (block.tensor, pe)):
        def program(e, lane=lane):
            for step in lane.steps:
                step(e)
        decorate(program)


_INPUTS = (
    "x", "c", "ctx", "c_ctx", "w_ada", "b_ada", "g_mix_pre", "g_mix_post", "g_mlp_pre", "g_mlp_post", "w_pool",
    "pool_scale", "w_qkv", "g_q", "g_k", "w_o", "w_mlp_in", "w_mlp_out", "p_2", "rel_bias_2", "norm_g_2", "mlp_w1_2",
    "mlp_w2_2", "ple_w_2", "ple_gate_w_2", "da_w_in_2", "da_lambda_2", "da_subln_2", "da_w_out_2", "nsa_w_in_2",
    "nsa_cmp_pe_2", "nsa_cmp_w1_2", "nsa_cmp_w2_2", "nsa_w_out_2", "fox_w_in_2", "fox_b_f_2", "fox_w_out_2")


def kernel(**inputs):
    import concourse.bacc as bacc
    from concourse.bass_utils import run_bass_kernel_spmd

    nc = bacc.Bacc("TRN2", target_bir_lowering=False, num_devices=1)
    arrays, aps = {}, {}
    for name, value in [(n, inputs[n]) for n in _INPUTS] + list(shape_constants().items()):
        a = np.ascontiguousarray(value)
        arrays["in_" + name] = a
        aps[name] = nc.dram_tensor("in_" + name, a.shape, F32, kind="ExternalInput").ap()
    out = nc.dram_tensor("out", (1, SEQ, D), F32, kind="ExternalOutput").ap()
    build(nc, aps, out)
    result = run_bass_kernel_spmd(nc, [arrays], core_ids=[0])
    return result.results[0]["out"]
```
